# Optimizing a Trainium2 kernel written in Bass

```python
import jax, jax.numpy as jnp
from jax import lax
import numpy as np

D_MODEL = 1024
BATCH = 1
SEQ = 512
DEPTH = 1

CHUNK = 64
MIX_WIDTH = D_MODEL
HEAD_DIM = 64
ATTN_WIDTH = MIX_WIDTH // 2
RWKV_WIDTH = MIX_WIDTH - ATTN_WIDTH
ATTN_Q_HEADS = ATTN_WIDTH // HEAD_DIM
ATTN_KV_HEADS = 2
ATTN_GROUP = ATTN_Q_HEADS // ATTN_KV_HEADS
WINDOW = 128
WINDOW_CHUNKS = WINDOW // CHUNK
ROPE_THETA = 10000.0
RWKV_HEADS = RWKV_WIDTH // HEAD_DIM
RWKV_N = HEAD_DIM
D_DECAY_LORA = 32
D_AAA_LORA = 32
D_GATE_LORA = 96
D_FF = 2816
NORM_EPS = 1e-5
RWKV_GN_EPS = 64e-5
MASK_VALUE = -1e30

Q_COLS = ATTN_Q_HEADS * HEAD_DIM
KV_COLS = ATTN_KV_HEADS * HEAD_DIM
ATTN_COLS = Q_COLS + 2 * KV_COLS
RWKV_R_END = RWKV_WIDTH
RWKV_K_END = 2 * RWKV_WIDTH
RWKV_V_END = 3 * RWKV_WIDTH
RWKV_W_END = RWKV_V_END + D_DECAY_LORA
RWKV_A_END = RWKV_W_END + D_AAA_LORA
RWKV_COLS = RWKV_A_END + D_GATE_LORA
IN_COLS = ATTN_COLS + RWKV_COLS

kernel_name = "hymba_swa_sink_rwkv7_macaron"

def _rmsnorm(x, g):
    xf = x.astype(jnp.float32)
    y = xf * lax.rsqrt(jnp.mean(xf * xf, axis=-1, keepdims=True) + NORM_EPS)
    return (y * g.astype(jnp.float32)).astype(x.dtype)

def _swiglu(h, w_gate, w_up, w_down):
    return (jax.nn.silu(h @ w_gate) * (h @ w_up)) @ w_down

def _rope_tables(seq_len):
    pos = jnp.arange(seq_len, dtype=jnp.float32)
    inv_freq = ROPE_THETA ** (-jnp.arange(0, HEAD_DIM, 2, dtype=jnp.float32) / HEAD_DIM)
    ang = pos[:, None] * inv_freq[None, :]
    return jnp.cos(ang), jnp.sin(ang)

def _apply_rope(x, cos, sin):
    x1, x2 = jnp.split(x, 2, axis=-1)
    c = cos[None, :, None, :]
    s = sin[None, :, None, :]
    return jnp.concatenate([x1 * c - x2 * s, x2 * c + x1 * s], axis=-1)

def _shift_chunks(xc, j):
    if j == 0:
        return xc
    return jnp.concatenate([jnp.zeros_like(xc[:, :j]), xc[:, :-j]], axis=1)

def _sliding_window_sink_attention(q, k, v, sinks):
    b, t = q.shape[0], q.shape[1]
    nc = t // CHUNK
    cos, sin = _rope_tables(t)
    q = _apply_rope(q.astype(jnp.float32).reshape(b, t, ATTN_Q_HEADS, HEAD_DIM), cos, sin)
    k = _apply_rope(k.astype(jnp.float32).reshape(b, t, ATTN_KV_HEADS, HEAD_DIM), cos, sin)
    v = v.astype(jnp.float32).reshape(b, t, ATTN_KV_HEADS, HEAD_DIM)
    qb = q.reshape(b, nc, CHUNK, ATTN_KV_HEADS, ATTN_GROUP, HEAD_DIM)
    kc = k.reshape(b, nc, CHUNK, ATTN_KV_HEADS, HEAD_DIM)
    vc = v.reshape(b, nc, CHUNK, ATTN_KV_HEADS, HEAD_DIM)
    offsets = list(range(WINDOW_CHUNKS - 1, -1, -1))
    kb = jnp.concatenate([_shift_chunks(kc, j) for j in offsets], axis=2)
    vb = jnp.concatenate([_shift_chunks(vc, j) for j in offsets], axis=2)
    s = jnp.einsum('bnqhgd,bnkhd->bnhgqk', qb, kb) * (HEAD_DIM ** -0.5)
    slot_off = jnp.repeat(jnp.arange(WINDOW_CHUNKS - 1, -1, -1), CHUNK)
    valid = jnp.arange(nc)[:, None] >= slot_off[None, :]
    s = jnp.where(valid[None, :, None, None, None, :], s, MASK_VALUE)
    sink = sinks.astype(jnp.float32).reshape(ATTN_KV_HEADS, ATTN_GROUP)[None, None, :, :, None, None]
    sink = jnp.broadcast_to(sink, s.shape[:-1] + (1,))
    p = jax.nn.softmax(jnp.concatenate([s, sink], axis=-1), axis=-1)[..., :-1]
    o = jnp.einsum('bnhgqk,bnkhd->bnqhgd', p, vb)
    return o.reshape(b, t, ATTN_WIDTH)

def _rwkv7_step(state, inp):
    r, w, k, v, a_vec, b_vec = inp
    sa = jnp.einsum('bhvk,bhk->bhv', state, a_vec)
    state = state * w[:, :, None, :] + sa[..., None] * b_vec[:, :, None, :] + v[..., None] * k[:, :, None, :]
    y = jnp.einsum('bhvk,bhk->bhv', state, r)
    return state, y

def _rwkv7_time_mix(p, shift_mu, w0, w2, a0, a2, g2, k_k, k_a, r_k, ln_w, ln_b):
    b, t = p.shape[0], p.shape[1]
    p = p.astype(jnp.float32)
    prev = jnp.concatenate([jnp.zeros_like(p[:, :1]), p[:, :-1]], axis=1)
    xs = p + (prev - p) * shift_mu.astype(jnp.float32)
    r = xs[..., :RWKV_R_END]
    k = xs[..., RWKV_R_END:RWKV_K_END]
    v = xs[..., RWKV_K_END:RWKV_V_END]
    wd = xs[..., RWKV_V_END:RWKV_W_END]
    ad = xs[..., RWKV_W_END:RWKV_A_END]
    gd = xs[..., RWKV_A_END:]
    w_log = -jax.nn.softplus(-(w0.astype(jnp.float32) + jnp.tanh(wd) @ w2.astype(jnp.float32))) - 0.5
    decay = jnp.exp(-jnp.exp(w_log))
    a = jax.nn.sigmoid(a0.astype(jnp.float32) + ad @ a2.astype(jnp.float32))
    g = jax.nn.sigmoid(gd) @ g2.astype(jnp.float32)
    hs = (b, t, RWKV_HEADS, RWKV_N)
    kk = (k * k_k.astype(jnp.float32)).reshape(hs)
    kk = kk * lax.rsqrt(jnp.maximum(jnp.sum(kk * kk, axis=-1, keepdims=True), 1e-24))
    k = k * (1.0 + (a - 1.0) * k_a.astype(jnp.float32))
    r_h, k_h, v_h = r.reshape(hs), k.reshape(hs), v.reshape(hs)
    a_h, w_h = a.reshape(hs), decay.reshape(hs)
    tm = lambda z: jnp.moveaxis(z, 1, 0)
    s0 = jnp.zeros((b, RWKV_HEADS, RWKV_N, RWKV_N), jnp.float32)
    _, y = lax.scan(_rwkv7_step, s0, (tm(r_h), tm(w_h), tm(k_h), tm(v_h), tm(-kk), tm(kk * a_h)))
    y = jnp.moveaxis(y, 0, 1)
    mean = jnp.mean(y, axis=-1, keepdims=True)
    var = jnp.mean(jnp.square(y - mean), axis=-1, keepdims=True)
    y = ((y - mean) * lax.rsqrt(var + RWKV_GN_EPS)).reshape(b, t, RWKV_WIDTH)
    y = y * ln_w.astype(jnp.float32) + ln_b.astype(jnp.float32)
    bonus = jnp.sum(r_h * k_h * r_k.astype(jnp.float32), axis=-1, keepdims=True) * v_h
    return (y + bonus.reshape(b, t, RWKV_WIDTH)) * g

def setup_inputs(seed: int = 0) -> dict:
    key = jax.random.key(seed)
    ks = jax.random.split(key, 28)
    f32 = jnp.float32
    nrm = lambda k, shape, scale: jax.random.normal(k, shape, f32) * scale
    gain = lambda k, n: 1.0 + 0.02 * jax.random.normal(k, (n,), f32)
    return {
        "x": jax.random.normal(ks[0], (BATCH, SEQ, D_MODEL), f32),
        "ffn1_norm": gain(ks[1], D_MODEL),
        "ffn1_w_gate": nrm(ks[2], (D_MODEL, D_FF), D_MODEL ** -0.5),
        "ffn1_w_up": nrm(ks[3], (D_MODEL, D_FF), D_MODEL ** -0.5),
        "ffn1_w_down": nrm(ks[4], (D_FF, D_MODEL), D_FF ** -0.5),
        "mix_norm": gain(ks[5], D_MODEL),
        "w_in": nrm(ks[6], (D_MODEL, IN_COLS), D_MODEL ** -0.5),
        "attn_sinks": nrm(ks[7], (ATTN_Q_HEADS,), 0.5),
        "rwkv_shift_mu": jax.random.uniform(ks[8], (RWKV_COLS,), f32),
        "rwkv_w0": jax.random.uniform(ks[9], (RWKV_WIDTH,), f32, minval=-5.0, maxval=0.0),
        "rwkv_w2": nrm(ks[10], (D_DECAY_LORA, RWKV_WIDTH), 0.5 * D_DECAY_LORA ** -0.5),
        "rwkv_a0": nrm(ks[11], (RWKV_WIDTH,), 0.1),
        "rwkv_a2": nrm(ks[12], (D_AAA_LORA, RWKV_WIDTH), 0.5 * D_AAA_LORA ** -0.5),
        "rwkv_g2": nrm(ks[13], (D_GATE_LORA, RWKV_WIDTH), D_GATE_LORA ** -0.5),
        "rwkv_k_k": 0.85 + 0.05 * jax.random.normal(ks[14], (RWKV_WIDTH,), f32),
        "rwkv_k_a": 1.0 + 0.05 * jax.random.normal(ks[15], (RWKV_WIDTH,), f32),
        "rwkv_r_k": nrm(ks[16], (RWKV_HEADS, RWKV_N), 0.1),
        "rwkv_ln_w": gain(ks[17], RWKV_WIDTH),
        "rwkv_ln_b": nrm(ks[18], (RWKV_WIDTH,), 0.02),
        "w_out": nrm(ks[19], (MIX_WIDTH, D_MODEL), MIX_WIDTH ** -0.5),
        "ffn2_norm": gain(ks[20], D_MODEL),
        "ffn2_w_gate": nrm(ks[21], (D_MODEL, D_FF), D_MODEL ** -0.5),
        "ffn2_w_up": nrm(ks[22], (D_MODEL, D_FF), D_MODEL ** -0.5),
        "ffn2_w_down": nrm(ks[23], (D_FF, D_MODEL), D_FF ** -0.5),
        "final_norm": gain(ks[24], D_MODEL),
    }

def reference(x, ffn1_norm, ffn1_w_gate, ffn1_w_up, ffn1_w_down, mix_norm, w_in, attn_sinks,
              rwkv_shift_mu, rwkv_w0, rwkv_w2, rwkv_a0, rwkv_a2, rwkv_g2, rwkv_k_k, rwkv_k_a,
              rwkv_r_k, rwkv_ln_w, rwkv_ln_b, w_out, ffn2_norm, ffn2_w_gate, ffn2_w_up,
              ffn2_w_down, final_norm):
    dt = x.dtype
    for _ in range(DEPTH):
        x = x + (0.5 * _swiglu(_rmsnorm(x, ffn1_norm), ffn1_w_gate, ffn1_w_up, ffn1_w_down)).astype(dt)
        h = _rmsnorm(x, mix_norm)
        proj = h @ w_in
        q = proj[..., :Q_COLS]
        k = proj[..., Q_COLS:Q_COLS + KV_COLS]
        v = proj[..., Q_COLS + KV_COLS:ATTN_COLS]
        attn = _sliding_window_sink_attention(q, k, v, attn_sinks)
        rwkv = _rwkv7_time_mix(proj[..., ATTN_COLS:], rwkv_shift_mu, rwkv_w0, rwkv_w2, rwkv_a0,
                               rwkv_a2, rwkv_g2, rwkv_k_k, rwkv_k_a, rwkv_r_k, rwkv_ln_w, rwkv_ln_b)
        mixed = jnp.concatenate([attn, rwkv], axis=-1).astype(dt)
        x = x + (mixed @ w_out).astype(dt)
        x = x + (0.5 * _swiglu(_rmsnorm(x, ffn2_norm), ffn2_w_gate, ffn2_w_up, ffn2_w_down)).astype(dt)
    return _rmsnorm(x, final_norm)


_drawn_inputs = setup_inputs


def setup_inputs(seed=0):
    import zlib

    import numpy as np

    out = dict(_drawn_inputs(seed))
    spreads = {}
    factors = {'ffn1_norm': 5.501,
     'mix_norm': 4.056,
     'attn_sinks': 200.0,
     'rwkv_w2': 5.182,
     'rwkv_a0': 3.811,
     'rwkv_k_k': 121.501,
     'rwkv_k_a': 3.229,
     'rwkv_ln_w': 187.899,
     'rwkv_ln_b': 186.622,
     'ffn2_norm': 29.194,
     'final_norm': 23.137}
    for name, (base, spread) in spreads.items():
        noise = np.random.default_rng([zlib.crc32(name.encode()), seed]).standard_normal(out[name].shape)
        drawn = base * np.exp(spread * noise) if base else spread * noise
        out[name] = __import__('jax').numpy.asarray(drawn.astype(out[name].dtype))
    for name, factor in factors.items():
        out[name] = (out[name] * factor).astype(out[name].dtype)
    return out
```

```python
from contextlib import ExitStack

import numpy as np
import concourse.bass as bass
from concourse import mybir

P = 128
D = 1024
T = 512
FF = 2816
HD = 64
NH = 8
KD = D // P
KF = FF // P
CH = 64
NC = T // CH
NP = 4
BLK = 16
NB = CH // BLK
IN_TILES = 20
UP_UNIT = KD * P
DOWN_UNIT = KF // 2 * P
NORM_EPS = 1e-5
GN_EPS = 64e-5
KAPPA = float(np.exp(-0.5))
SCALE = HD ** -0.5
NEG = -1e30

ALU = mybir.AluOpType
ACT = mybir.ActivationFunctionType
AX_X = mybir.AxisListType.X
F32 = mybir.dt.float32
F32R = mybir.dt.float32r

LORA, KT, RT, VT, AK, AV, QT = 0, 2, 6, 10, 14, 15, 16
G0, LW0, A0, KK0, D0, E0, BON0, X0 = 20, 24, 28, 32, 36, 40, 44, 48
ARENA = 52
M0 = LW0
BT0 = KT
TT0 = E0
DI0 = X0
DIT0 = G0
RSW = G0 + 2

PARAMS = {}
_at = 0
for _name, _n in [("g1", 8), ("gm", 8), ("g2", 8), ("gf", 8), ("mu", 14), ("w0", 4), ("a0", 4), ("k_k", 4),
                  ("k_a", 4), ("r_k", 4), ("ln_w", 4), ("ln_b", 4)]:
    PARAMS[_name] = (_at, _n)
    _at += _n
NPARAM = _at

CONST = {}
_at = 0
for _name, _n in [("cos", T), ("sin", T), ("reset", T), ("ident", P), ("ones", P), ("headones", P), ("mmask", P),
                  ("atmask", CH), ("offblock", CH), ("winmask", 192), ("eps", 4)]:
    CONST[_name] = (_at, _n)
    _at += _n
NCONST = _at

PHASES = [("up1", 2 * KF, UP_UNIT), ("down1", 2 * KD, DOWN_UNIT), ("win", IN_TILES, UP_UNIT),
          ("wout", KD, UP_UNIT), ("up2", 2 * KF, UP_UNIT), ("down2", 2 * KD, DOWN_UNIT)]
FIRST_UNIT = {}
_at = 0
for _name, _n, _ in PHASES:
    FIRST_UNIT[_name] = _at
    _at += _n
NRAW = 4
NHL = 2


def constants():
    c = np.zeros((P, NCONST), np.float32)

    def put(name, v):
        c[:, CONST[name][0]:CONST[name][0] + CONST[name][1]] = v

    half = HD // 2
    inv = np.float32(10000.0) ** (-np.arange(0, HD, 2, dtype=np.float32) / np.float32(HD))
    ang = np.arange(T, dtype=np.float32)[:, None] * inv[None, :].astype(np.float32)
    row = np.arange(P)
    put("cos", np.cos(ang).T[row % half])
    put("sin", np.sin(ang).T[row % half] * np.where(row % HD < half, -1.0, 1.0)[:, None])
    put("reset", (np.arange(T) % CH != 0)[None, :])
    put("ident", np.eye(P))
    put("ones", 1.0)
    put("headones", row[:, None] // HD == row[None, :] // HD)
    s, t = row[:, None] % CH, np.arange(CH)[None, :]
    put("mmask", np.concatenate([s < t, s <= t], 1))
    put("atmask", s < t)
    put("offblock", s // BLK != t // BLK)
    key = np.arange(192)[None, :]
    put("winmask", np.where((key >= CH * (row[:, None] // CH)) & (key < CH * (row[:, None] // CH) + 2 * CH), 0.0, NEG))
    c[:, CONST["eps"][0]] = NORM_EPS
    c[:, CONST["eps"][0] + 1] = GN_EPS
    return c


def build(nc, xT, w, params, sinks, w2, a2, g2, const, blocks_dram, inv_dram, invt_dram, out):
    ctx = ExitStack()
    with ctx:
        def keep(name, shape, dt=F32):
            return ctx.enter_context(nc.sbuf_tensor(name, shape, dt))

        def sem(name):
            return ctx.enter_context(nc.semaphore(name))

        x = keep("x", [P, KD, T])
        raw = keep("raw", [P, NRAW, DOWN_UNIT])
        par = keep("par", [P, NPARAM])
        cst = keep("cst", [P, NCONST])
        small = keep("small", [P, 112])

        def overlay(*layouts):
            made = []
            for n, layout in enumerate(layouts):
                scope = ExitStack()
                made += [(ctx if n == len(layouts) - 1 else scope).enter_context(nc.sbuf_tensor(*t)) for t in layout]
                if n < len(layouts) - 1:
                    scope.close()
            return made

        h_hi, h_lo, armain = overlay(
            [("h_hi", [P, KD, T], F32R), ("h_lo", [P, KD, T], F32R)],
            [("chunk_ops", [P, 2 * KD, T], F32)])
        w_hi, w_lo, side = overlay(
            [("w_hi", [P, NHL, DOWN_UNIT], F32R), ("w_lo", [P, NHL, DOWN_UNIT], F32R)],
            [("side", [P, 11, T], F32)])
        hid_hi, hid_lo, sil, tmp, acc, rs, nt, _, mix_hi, mix_lo, arena = overlay(
            [("hid_hi", [P, KF, T], F32R), ("hid_lo", [P, KF, T], F32R), ("sil", [P, 2, T], F32),
             ("tmp", [P, 2, T], F32), ("acc", [P, T], F32), ("rs", [P, T], F32), ("nt", [P, T], F32)],
            [("before_mix", [P, M0, T], F32), ("mix_hi", [P, KD, T], F32R), ("mix_lo", [P, KD, T], F32R)],
            [("arena", [P, ARENA, T], F32)])
        ps = [ctx.enter_context(nc.psum_tensor(f"ps{i}", [P, T], F32)) for i in range(8)]

        def C(name, rows=P):
            a, n = CONST[name]
            return cst[0:rows, a:a + n]

        def par_col(name, i, lo=0, hi=P):
            return par[lo:hi, PARAMS[name][0] + i:PARAMS[name][0] + i + 1]

        def par_at(name, i):
            a, n = PARAMS[name]
            return par[:, a:a + n][:, i:i + 1] if isinstance(i, int) else par[:, bass.ds(i + a, 1)]

        def par_all(name):
            a, n = PARAMS[name]
            return par[:, a:a + n]

        def tiles(first, n=4):
            return arena[:, first:first + n, :]

        AR = armain[:, 0:8, :].rearrange("q a b -> q (a b)").rearrange("q (p n c) -> q p n c", p=NP, n=NC)
        BK = armain[:, 8:16, :].rearrange("q a b -> q (a b)").rearrange("q (p n c) -> q p n c", p=NP, n=NC)
        OFF = armain[:, 8:12, :].rearrange("q a b -> q (a b)").rearrange("q (m c) -> q m c", c=CH)
        QQ = armain[:, 12:16, :].rearrange("q a b -> q (a b)").rearrange("q (m c) -> q m c", c=CH)
        UV = armain[:, 8:16, :].rearrange("q a b -> q (a b)").rearrange("q (n p c) -> q n p c", n=NC, p=NP)
        MM = tiles(M0, 16).rearrange("q a b -> q (a b)").rearrange("q (n e p c) -> q n e p c", n=NC, e=2, p=NP)
        BT = tiles(BT0, 8).rearrange("q a b -> q (a b)").rearrange("q (n p c) -> q n p c", n=NC, p=NP)
        def mats(first):
            return tiles(first).rearrange("q a b -> q (a b)").rearrange("q (m c) -> q m c", c=CH)

        AT = TT = mats(TT0)
        DI, DIT = mats(DI0), mats(DIT0)
        Y = tiles(DI0)
        SC = side[:, 0:3, :].rearrange("q a b -> q (a b)").rearrange("q (h k) -> q h k", h=NH)
        PT1 = side[:, 3:5, :].rearrange("q a b -> q (a b)").rearrange("q (h k) -> q h k", h=NH)
        PT0 = side[:, 5:7, :].rearrange("q a b -> q (a b)").rearrange("q (h k) -> q h k", h=NH)
        AB = side[:, 7, :].rearrange("q (e s t) -> q e s t", e=2, s=BLK)
        TB = side[:, 8, :].rearrange("q (e t j) -> q e t j", e=2, t=BLK)
        TBT = side[:, 9, :].rearrange("q (e j t) -> q e j t", e=2, j=BLK)
        PROD = side[:, 10, :]
        RS = side[:, 7, 0:256].rearrange("q (p c) -> q p c", p=NP)
        ST = side[:, 8, :].rearrange("q (b p c) -> q b p c", b=2, p=NP)
        VA = arena[:, LORA + 1, :].rearrange("q (i c) -> q i c", c=P)
        VB = arena[:, AV, :].rearrange("q (i c) -> q i c", c=P)
        HALF = small[:, 0:32].rearrange("q (p n) -> q p n", p=NP)
        FAC = small[:, 32:64].rearrange("q (p n) -> q p n", p=NP)
        MX, NMX, DEN, ESK = (small[:, 64 + 8 * i:72 + 8 * i] for i in range(4))
        OMKA = small[:, 96:100]
        SINK = small[:, 104:112]
        GN_SQ, GN_X, GN_Y, GN_T = (armain[:, 4 * i:4 * i + 4, :] for i in range(4))
        GD = arena[0:96, LORA, :]
        WD = arena[96:128, LORA, :]
        AD = arena[0:32, LORA + 1, :]
        w2_t, a2_t, g2_t = arena[96:128, G0, :], arena[0:32, G0 + 1, :], side[0:96, 9, :]

        raw_ready = [sem(f"raw_ready{j}") for j in range(NRAW)]
        hi_done = sem("hi_done")
        lo_done = sem("lo_done")
        w_used = sem("w_used")
        x_ready = [sem(f"x_ready{k}") for k in range(KD)]
        par_ready = sem("par_ready")
        const_ready = sem("const_ready")
        sq_done = sem("sq_done")
        acc_done = sem("acc_done")
        sum_done = sem("sum_done")
        ms_done = sem("ms_done")
        root_done = sem("root_done")
        y_ready = sem("y_ready")
        h_hi_done = sem("h_hi_done")
        h_lo_done = sem("h_lo_done")
        gate_done = sem("gate_done")
        silu_done = sem("silu_done")
        up_done = sem("up_done")
        hid_done = sem("hid_done")
        hid_hi_done = sem("hid_hi_done")
        hid_lo_done = sem("hid_lo_done")
        resid_done = sem("resid_done")
        dve_own = sem("dve_own")
        out_done = sem("out_done")
        proj = sem("proj")
        lora_w = sem("lora_w")
        shifted = sem("shifted")
        lora_act = sem("lora_act")
        z_done = sem("z_done")
        z_kept = sem("z_kept")
        kk_raw = sem("kk_raw")
        kk_sq = sem("kk_sq")
        kk_root = sem("kk_root")
        kk_ready = sem("kk_ready")
        rk_ready = sem("rk_ready")
        cum_ready = sem("cum_ready")
        exps = sem("exps")
        ops = sem("ops")
        swap_in = sem("swap_in")
        rope_own = sem("rope_own")
        roped = sem("roped")
        zeroed = sem("zeroed")
        at_done, at_kept = sem("at_done"), sem("at_kept")
        mm_done, mm_kept = sem("mm_done"), sem("mm_kept")
        bt_done, bt_kept = sem("bt_done"), sem("bt_kept")
        vt_done, vt_kept = sem("vt_done"), sem("vt_kept")
        blk_out, blk_in = sem("blk_out"), sem("blk_in")
        inv_ready = sem("inv_ready")
        inv_out, inv_in = sem("inv_out"), sem("inv_in")
        s_done, s_kept = sem("s_done"), sem("s_kept")
        mx_ready = sem("mx_ready")
        e_ready = sem("e_ready")
        p_ready = sem("p_ready")
        pt_done = sem("pt_done")
        pt_act, pt_dve = sem("pt_act"), sem("pt_dve")
        o_done, o_kept = sem("o_done"), sem("o_kept")
        off_ready = sem("off_ready")
        q_done, q_kept = sem("q_done"), sem("q_kept")
        tt_done, tt_kept = sem("tt_done"), sem("tt_kept")
        v_done, v_kept = sem("v_done"), sem("v_kept")
        g2_in = sem("g2_in")
        g_done, g_kept = sem("g_done"), sem("g_kept")
        r_done, r_kept = sem("r_done"), sem("r_kept")
        u_done, u_dve, u_act = sem("u_done"), sem("u_dve"), sem("u_act")
        st_done, st_kept = sem("st_done"), sem("st_kept")
        y_done, y_kept = sem("y_done"), sem("y_kept")
        gn_done = sem("gn_done")
        gn_kept = sem("gn_kept")
        gn_sq = sem("gn_sq")
        gn_root = sem("gn_root")
        mix_ready = sem("mix_ready")
        mix_hi_done = sem("mix_hi_done")
        mix_lo_done = sem("mix_lo_done")

        def ge(eng, s, v):
            if not (isinstance(v, int) and v <= 0):
                eng.wait_ge(s, v)

        def units(name):
            return FIRST_UNIT[name], dict((n, k) for n, k, _ in PHASES)[name] // NRAW

        block = ctx.enter_context(nc.Block())

        @block.sync
        def _(sp):
            sp.dma_start(par[:, :], params).then_inc(par_ready, 16)

            def load(name, i, j):
                n = dict((a, c) for a, _, c in PHASES)[name]
                ge(sp, lo_done, FIRST_UNIT[name] + NRAW * i + j + 1 - NRAW)
                sp.dma_start(raw[:, j, 0:n], w[name][NRAW * i + j]).then_inc(raw_ready[j], 16)

            def load_all(name, first=0):
                with sp.Fori(first, units(name)[1]) as i:
                    for j in range(NRAW):
                        load(name, i, j)

            for k in range(KD):
                sp.dma_start(x[:, k, :], xT[:, k, :]).then_inc(x_ready[k], 16)
                if k < NRAW:
                    load("up1", 0, k)
            sp.dma_start(cst[:, :], const).then_inc(const_ready, 16)
            sp.dma_start(SINK, sinks.partition_broadcast(P)).then_inc(const_ready, 16)
            load_all("up1", 1)
            load_all("down1")
            load("win", 0, 0)
            load("win", 0, 1)
            load("win", 0, 2)
            load("win", 0, 3)
            sp.wait_ge(w_used, FIRST_UNIT["win"])
            sp.dma_start(w2_t, w2).then_inc(lora_w, 16)
            sp.dma_start(a2_t, a2).then_inc(lora_w, 16)
            load_all("win", 1)
            sp.wait_ge(proj, IN_TILES)
            sp.wait_ge(z_done, 8)
            sp.wait_ge(kk_ready, 1)
            for a in range(4):
                b = a ^ 1
                sp.dma_start(arena[32 * a:32 * a + 32, LORA + 1, :], arena[32 * b:32 * b + 32, AK, :]).then_inc(swap_in, 16)
                sp.dma_start(arena[32 * a:32 * a + 32, X0:X0 + 4, :],
                             arena[32 * b:32 * b + 32, QT:QT + 4, :]).then_inc(swap_in, 16)
            for j in range(NRAW):
                load("wout", 0, j)
            sp.wait_ge(at_kept, 4)
            for e in range(2):
                for b in range(NB):
                    r = CH * e + BLK * b
                    sp.dma_start(blocks_dram[32 * b:32 * b + 32, e].rearrange("m s t -> s m t"),
                                 AT[r:r + BLK, :, BLK * b:BLK * b + BLK]).then_inc(blk_out, 16)
            sp.wait_ge(blk_out, 16 * 2 * NB)
            sp.dma_start(AB, blocks_dram).then_inc(blk_in, 16)
            sp.wait_ge(inv_ready, 1)
            sp.dma_start(inv_dram, TB).then_inc(inv_out, 16)
            sp.dma_start(invt_dram, TBT).then_inc(inv_out, 16)
            sp.wait_ge(inv_out, 32)
            sp.wait_ge(zeroed, 2)
            for e in range(2):
                for b in range(NB):
                    r = CH * e + BLK * b
                    for dst, src in ((DI, inv_dram), (DIT, invt_dram)):
                        sp.dma_start(dst[r:r + BLK, :, BLK * b:BLK * b + BLK],
                                     src[32 * b:32 * b + 32, e].rearrange("m t j -> t m j")).then_inc(inv_in, 16)
            sp.dma_start(g2_t, g2).then_inc(g2_in, 16)
            load_all("wout", 1)
            load_all("up2")
            load_all("down2")
            for k in range(KD):
                sp.wait_ge(y_ready, k + 1)
                sp.dma_start(out[:, k, :], x[:, k, :]).then_inc(out_done, 16)
            sp.wait_ge(out_done, 16 * KD)

        @block.gpsimd
        def _(pool):
            own = [0]

            def link(ins):
                own[0] += 1
                ins.then_inc(rope_own, 1)
                pool.wait_ge(rope_own, own[0])

            pool.wait_ge(const_ready, 32)
            pool.wait_ge(swap_in, 16 * 8)
            for x_t, s_t in [(AK, LORA + 1)] + [(QT + i, X0 + i) for i in range(4)]:
                link(nc.gpsimd.tensor_tensor(arena[:, x_t, :], arena[:, x_t, :], C("cos"), ALU.mult))
                link(nc.gpsimd.tensor_tensor(arena[:, s_t, :], arena[:, s_t, :], C("sin"), ALU.mult))
                nc.gpsimd.tensor_tensor(arena[:, x_t, :], arena[:, x_t, :], arena[:, s_t, :], ALU.add).then_inc(roped, 1)
            pool.wait_ge(roped, 5)
            nc.gpsimd.memset(tiles(DI0), 0.0).then_inc(zeroed, 1)
            pool.wait_ge(z_done, 8)
            nc.gpsimd.memset(tiles(DIT0), 0.0).then_inc(zeroed, 1)
            pool.wait_ge(tt_done, 12)
            nc.gpsimd.memset(UV[0:CH, :, :, :], 0.0).then_inc(zeroed, 1)

        @block.scalar
        def _(act):
            A = nc.scalar

            def split(name, i, j):
                n = dict((a, c) for a, _, c in PHASES)[name]
                u = FIRST_UNIT[name] + NRAW * i + j
                act.wait_ge(raw_ready[j], 16 * (FIRST_UNIT[name] // NRAW + i + 1))
                ge(act, w_used, u + 1 - NHL)
                A.activation(w_hi[:, j % NHL, 0:n], raw[:, j, 0:n], ACT.Copy).then_inc(hi_done, 1)

            def silu(fbase, f, slot):
                act.wait_ge(gate_done, fbase + f + 1)
                A.activation(sil[:, slot, :], sil[:, slot, :], ACT.Silu).then_inc(silu_done, 1)

            def hid_high(fbase, f, slot):
                act.wait_ge(hid_done, fbase + f + 1)
                A.activation(hid_hi[:, f, :], tmp[:, slot, :], ACT.Copy).then_inc(hid_hi_done, 1)

            def square(base, d, slot, high=True):
                n = base + KD + d
                if base < 0:
                    act.wait_ge(x_ready[d], 16)
                else:
                    act.wait_ge(resid_done, base + d + 1)
                ge(act, acc_done, n - 1)
                if high:
                    A.activation(h_hi[:, d, :], x[:, d, :], ACT.Copy,
                                 scale=par_at(("g1", "gm", "g2")[base // KD + 1], d)).then_inc(h_hi_done, 1)
                first = isinstance(d, int) and d == 0
                A.activation(acc[:, :] if first else sil[:, slot, :], x[:, d, :], ACT.Square).then_inc(sq_done, 1)

            def root(n):
                act.wait_ge(ms_done, n + 1)
                A.activation(rs[:, :], nt[:, :], ACT.Sqrt).then_inc(root_done, 1)

            def ffn(n, up, down, fbase):
                def up_body(i):
                    first = isinstance(i, int) and i == 0
                    split(up, i, 0)
                    if first:
                        if n == 2:
                            square(KD, KD - 1, 1)
                    else:
                        silu(fbase, 2 * i - 1, 1)
                    split(up, i, 1)
                    if first:
                        root(n)
                    else:
                        hid_high(fbase, 2 * i - 1, 1)
                    split(up, i, 2)
                    silu(fbase, 2 * i, 0)
                    split(up, i, 3)
                    hid_high(fbase, 2 * i, 0)

                def down_body(i):
                    first = isinstance(i, int) and i == 0
                    split(down, i, 0)
                    if first:
                        silu(fbase, KF - 1, 1)
                    split(down, i, 1)
                    if first:
                        hid_high(fbase, KF - 1, 1)
                    else:
                        square(KD * n, 2 * i - 1, 1, n == 0)
                    split(down, i, 2)
                    split(down, i, 3)
                    square(KD * n, 2 * i, 0, n == 0)

                up_body(0)
                with act.Fori(1, units(up)[1]) as i:
                    up_body(i)
                down_body(0)
                with act.Fori(1, units(down)[1]) as i:
                    down_body(i)

            act.wait_ge(par_ready, 16)
            for d in range(KD):
                square(-KD, d, d % 2)
            ffn(0, "up1", "down1", 0)

            for t in range(IN_TILES):
                split("win", t // NRAW, t % NRAW)
                if t == 0:
                    square(0, KD - 1, 1)
                if t == 1:
                    root(1)
                if t == 9:
                    for c in range(4):
                        act.wait_ge(z_done, c + 1)
                        A.activation(arena[:, LW0 + c, :], ps[4 + c][:, :], ACT.Sigmoid,
                                     bias=par_col("w0", c)).then_inc(z_kept, 1)
                    for c in range(4):
                        act.wait_ge(z_done, 4 + c + 1)
                        A.activation(arena[:, A0 + c, :], ps[4 + c][:, :], ACT.Sigmoid,
                                     bias=par_col("a0", c)).then_inc(z_kept, 1)
                if t == 6:
                    act.wait_ge(shifted, 2)
                    A.activation(WD, WD, ACT.Tanh).then_inc(lora_act, 1)
                    A.activation(GD, GD, ACT.Sigmoid).then_inc(lora_act, 1)
                if t == 12:
                    act.wait_ge(kk_raw, 4)
                    A.activation(tiles(D0), tiles(KK0), ACT.Square).then_inc(kk_sq, 1)
                if t == 18:
                    act.wait_ge(z_kept, 12)
                    act.wait_ge(shifted, 14)
                    A.activation(tiles(E0), tiles(D0), ACT.Sqrt).then_inc(kk_root, 1)

            act.wait_ge(cum_ready, 2)
            A.activation(tiles(E0), tiles(D0), ACT.Exp, scale=KAPPA).then_inc(exps, 1)
            act.wait_ge(ops, 1)
            A.activation(tiles(A0), tiles(D0), ACT.Exp, scale=-KAPPA).then_inc(exps, 1)
            A.activation(tiles(LW0), tiles(LW0), ACT.Exp, scale=-KAPPA).then_inc(exps, 1)
            A.activation(FAC[:, :, 0:NC - 1], FAC[:, :, 0:NC - 1], ACT.Exp, scale=-KAPPA).then_inc(exps, 1)

            act.wait_ge(vt_done, 2)
            A.activation(VA[:, :, :], ps[0][:, :].rearrange("q (i c) -> q i c", c=P), ACT.Copy).then_inc(vt_kept, 1)
            A.activation(VB[0:CH, 0:3, :], ps[1][0:CH, 0:3 * P].rearrange("q (i c) -> q i c", c=P),
                         ACT.Copy).then_inc(vt_kept, 1)
            for n in range(NC):
                act.wait_ge(bt_done, n + 1)
                A.activation(BT[:, n, :, :], ps[n % 4][:, :].rearrange("q (p c) -> q p c", p=NP), ACT.Copy).then_inc(bt_kept, 1)

            for i in range(T // P):
                k0 = CH if i == 0 else 0
                act.wait_ge(mx_ready, 2 * i + 2)
                for h in range(NH):
                    A.activation(SC[:, h, k0:192], SC[:, h, k0:192], ACT.Exp, bias=NMX[:, h:h + 1],
                                 accum_out=DEN[:, h:h + 1])
                A.activation(ESK, ESK, ACT.Exp).then_inc(e_ready, 1)
                act.wait_ge(pt_done, max(1, 2 * i))
                A.activation(PT1[:, 0:4, :], ps[0][:, :].rearrange("q (h c) -> q h c", h=4), ACT.Copy).then_inc(pt_act, 1)
                if i:
                    act.wait_ge(pt_done, 2 * i + 1)
                    A.activation(PT0[0:CH, 0:4, :], ps[2][0:CH, :].rearrange("q (h c) -> q h c", h=4),
                                 ACT.Copy).then_inc(pt_act, 1)
                act.wait_ge(o_done, i + 1)
                A.activation(arena[:, QT:QT + 4, P * i:P * i + P], ps[4][:, :].rearrange("q (p c) -> q p c", p=NP),
                             ACT.Copy).then_inc(o_kept, 1)

            for n in range(NC):
                act.wait_ge(v_done, n + 1)
                A.activation(UV[CH:P, n, :, :], ps[n % 4][0:CH, :].rearrange("q (p c) -> q p c", p=NP),
                             ACT.Copy).then_inc(v_kept, 1)
            for c in range(4):
                act.wait_ge(g_done, c + 1)
                A.activation(arena[:, G0 + c, :], ps[4 + c][:, :], ACT.Copy).then_inc(g_kept, 1)
            for n in range(NC):
                act.wait_ge(u_done, n + 1)
                A.activation(UV[0:CH, n, :, CH:P], ps[3][0:CH, 0:NP * CH].rearrange("q (p c) -> q p c", p=NP),
                             ACT.Copy).then_inc(u_act, 1)
                act.wait_ge(y_done, n + 1)
                A.activation(Y[:, :, CH * n:CH * n + CH], ps[5 + n % 2][:, 0:NP * CH].rearrange("q (p c) -> q p c", p=NP),
                             ACT.Copy).then_inc(y_kept, 1)
            act.wait_ge(gn_kept, 4)
            A.activation(GN_SQ, Y, ACT.Square).then_inc(gn_sq, 1)
            act.wait_ge(gn_kept, 8)
            A.activation(GN_Y, GN_X, ACT.Sqrt).then_inc(gn_root, 1)
            act.wait_ge(y_done, NC)
            act.wait_ge(o_kept, T // P)
            for k in range(KD):
                if k >= 4:
                    act.wait_ge(mix_ready, k - 3)
                src = arena[:, QT + k, :] if k < 4 else arena[:, DI0 + k - 4, :]
                A.activation(mix_hi[:, k, :], src, ACT.Copy).then_inc(mix_hi_done, 1)

            def wout_body(i):
                for j in range(NRAW):
                    split("wout", i, j)
                    if not (isinstance(i, int) and i == 0 and j == 0):
                        square(KD, NRAW * i + j - 1, (j + 1) % 2)

            wout_body(0)
            with act.Fori(1, units("wout")[1]) as i:
                wout_body(i)
            ffn(2, "up2", "down2", KF)
            square(2 * KD, KD - 1, 1, False)
            root(3)

        @block.vector
        def _(dve):
            V = nc.vector
            own = [0]

            def link(ins):
                own[0] += 1
                ins.then_inc(dve_own, 1)
                dve.wait_ge(dve_own, own[0])

            def low(name, i, j):
                n = dict((a, c) for a, _, c in PHASES)[name]
                dve.wait_ge(hi_done, FIRST_UNIT[name] + NRAW * i + j + 1)
                V.tensor_tensor(w_lo[:, j % NHL, 0:n], raw[:, j, 0:n], w_hi[:, j % NHL, 0:n].bitcast(F32),
                                ALU.subtract).then_inc(lo_done, 1)

            def hidden(fbase, f, slot):
                dve.wait_ge(w_used, FIRST_UNIT["up1" if fbase == 0 else "up2"] + 2 * f + 2)
                ge(dve, hid_lo_done, fbase + f - 1)
                V.tensor_tensor(tmp[:, slot, :], ps[2 * slot + 1][:, :], rs[:, :], ALU.mult).then_inc(up_done, 1)
                dve.wait_ge(up_done, fbase + f + 1)
                dve.wait_ge(silu_done, fbase + f + 1)
                V.tensor_tensor(tmp[:, slot, :], tmp[:, slot, :], sil[:, slot, :], ALU.mult).then_inc(hid_done, 1)

            def gate(fbase, f, slot):
                dve.wait_ge(w_used, FIRST_UNIT["up1" if fbase == 0 else "up2"] + 2 * f + 1)
                ge(dve, hid_done, fbase + f - 1)
                V.tensor_tensor(sil[:, slot, :], ps[2 * slot][:, :], rs[:, :], ALU.mult).then_inc(gate_done, 1)

            def hid_low(fbase, f, slot):
                dve.wait_ge(hid_hi_done, fbase + f + 1)
                V.tensor_tensor(hid_lo[:, f, :], tmp[:, slot, :], hid_hi[:, f, :].bitcast(F32),
                                ALU.subtract).then_inc(hid_lo_done, 1)

            def residual(base, name, d, per, bank, scale):
                dve.wait_ge(w_used, FIRST_UNIT[name] + per * (d + 1))
                V.scalar_tensor_tensor(x[:, d, :], ps[bank][:, :], scale, x[:, d, :], ALU.mult, ALU.add).then_inc(resid_done, 1)

            def add_square(base, d, slot):
                n = base + KD + d
                dve.wait_ge(sq_done, n + 1)
                if isinstance(d, int) and d == 0:
                    V.tensor_copy(small[:, 100:101], acc[:, 0:1]).then_inc(acc_done, 1)
                else:
                    dve.wait_ge(acc_done, n)
                    V.tensor_tensor(acc[:, :], acc[:, :], sil[:, slot, :], ALU.add).then_inc(acc_done, 1)

            def inverse_root(y, xx, t):
                link(V.reciprocal(y, y))
                link(V.tensor_tensor(t, xx, y, ALU.mult))
                link(V.scalar_tensor_tensor(t, t, -0.5, y, ALU.mult, ALU.mult))
                link(V.scalar_tensor_tensor(y, t, 1.5, y, ALU.add, ALU.mult))

            def norm(n, y=None):
                dve.wait_ge(sum_done, n + 1)
                V.tensor_scalar(nt[:, :], ps[7][:, :], 1.0 / D, NORM_EPS, ALU.mult, ALU.add).then_inc(ms_done, 1)
                dve.wait_ge(root_done, n + 1)
                inverse_root(rs[:, :], nt[:, :], tmp[:, 0, :])
                if y is not None:
                    link(V.tensor_copy(y, rs[:, :]))

            def h_low(base, d):
                dve.wait_ge(h_hi_done, base + KD + d + 1)
                V.scalar_tensor_tensor(h_lo[:, d, :], x[:, d, :], par_at(("g1", "gm", "g2")[base // KD + 1], d),
                                       h_hi[:, d, :].bitcast(F32), ALU.mult, ALU.subtract).then_inc(h_lo_done, 1)

            def ffn(n, up, down, fbase):
                def up_body(i):
                    first = isinstance(i, int) and i == 0
                    low(up, i, 0)
                    if first:
                        if n == 2:
                            residual(KD, "wout", KD - 1, 1, 5 + (KD - 1) % 2, 1.0)
                            h_low(KD, KD - 1)
                            add_square(KD, KD - 1, 1)
                    else:
                        hidden(fbase, 2 * i - 1, 1)
                    low(up, i, 1)
                    if first:
                        norm(n)
                    else:
                        hid_low(fbase, 2 * i - 1, 1)
                    low(up, i, 2)
                    gate(fbase, 2 * i, 0)
                    hidden(fbase, 2 * i, 0)
                    low(up, i, 3)
                    gate(fbase, 2 * i + 1, 1)
                    hid_low(fbase, 2 * i, 0)

                def down_body(i):
                    first = isinstance(i, int) and i == 0
                    low(down, i, 0)
                    if first:
                        hidden(fbase, KF - 1, 1)
                    else:
                        residual(KD * n, down, 2 * i - 1, 2, 5, 0.5)
                        if n == 0:
                            h_low(0, 2 * i - 1)
                    low(down, i, 1)
                    if first:
                        hid_low(fbase, KF - 1, 1)
                    else:
                        add_square(KD * n, 2 * i - 1, 1)
                    low(down, i, 2)
                    residual(KD * n, down, 2 * i, 2, 4, 0.5)
                    low(down, i, 3)
                    if n == 0:
                        h_low(0, 2 * i)
                    add_square(KD * n, 2 * i, 0)

                up_body(0)
                with dve.Fori(1, units(up)[1]) as i:
                    up_body(i)
                down_body(0)
                with dve.Fori(1, units(down)[1]) as i:
                    down_body(i)

            dve.wait_ge(par_ready, 16)
            for d in range(KD):
                h_low(-KD, d)
                add_square(-KD, d, d % 2)
            ffn(0, "up1", "down1", 0)

            def shift(t):
                dve.wait_ge(proj, t + 1)
                d, p = arena[:, E0 + t % 4, :], arena[:, t, :]
                V.tensor_tensor(d[:, 1:T], p[:, 0:T - 1], p[:, 1:T], ALU.subtract)
                link(V.tensor_scalar(d[:, 0:1], p[:, 0:1], -1.0, None, ALU.mult))
                V.scalar_tensor_tensor(p, d, par_col("mu", t), p, ALU.mult, ALU.add).then_inc(shifted, 1)

            def keep_proj(t):
                dve.wait_ge(w_used, FIRST_UNIT["win"] + t + 1)
                V.tensor_tensor(arena[:, t, :], ps[t % 4][:, :], arena[:, RSW, :], ALU.mult).then_inc(proj, 1)

            for t in range(IN_TILES):
                low("win", t // NRAW, t % NRAW)
                if t == 0:
                    residual(0, "down1", KD - 1, 2, 5, 0.5)
                    h_low(0, KD - 1)
                    add_square(0, KD - 1, 1)
                if t == 1:
                    norm(1, arena[:, RSW, :])
                if t:
                    keep_proj(t - 1)
                if 2 <= t < 16:
                    shift(t - 2)
                if t == 8:
                    dve.wait_ge(shifted, 6)
                    for c in range(4):
                        V.tensor_scalar(arena[:, KK0 + c, :], arena[:, KT + c, :], par_col("k_k", c), None,
                                        ALU.mult).then_inc(kk_raw, 1)
                    V.tensor_scalar(OMKA, par_all("k_a"), -1.0, 1.0, ALU.mult, ALU.add).then_inc(kk_raw, 1)
                if t == 11:
                    dve.wait_ge(z_kept, 8)
                    dve.wait_ge(kk_raw, 5)
                    for c in range(3):
                        V.tensor_scalar(arena[:, X0 + c, :], arena[:, A0 + c, :], par_col("k_a", c), OMKA[:, c:c + 1],
                                        ALU.mult, ALU.add)
                    link(V.tensor_scalar(arena[:, X0 + 3, :], arena[:, A0 + 3, :], par_col("k_a", 3), OMKA[:, 3:4],
                                         ALU.mult, ALU.add))
                    link(V.tensor_tensor(tiles(KT), tiles(KT), tiles(X0), ALU.mult))
                if t == 13:
                    dve.wait_ge(shifted, 10)
                    for c in range(4):
                        V.scalar_tensor_tensor(arena[:, BON0 + c, :], arena[:, RT + c, :], par_col("r_k", c),
                                               arena[:, KT + c, :], ALU.mult, ALU.mult).then_inc(rk_ready, 1)
                if t == 17:
                    for c in range(4):
                        dve.wait_ge(z_done, 8 + c + 1)
                        V.tensor_scalar(arena[:, D0 + c, :], ps[4 + c][:, :], 1e-24, None, ALU.max).then_inc(z_kept, 1)
                if t == 19:
                    dve.wait_ge(kk_root, 1)
                    inverse_root(tiles(E0), tiles(D0), tiles(X0))
                    V.tensor_tensor(tiles(KK0), tiles(KK0), tiles(E0), ALU.mult).then_inc(kk_ready, 1)
            keep_proj(IN_TILES - 1)
            dve.wait_ge(kk_ready, 1)
            V.tensor_tensor(tiles(A0), tiles(KK0), tiles(A0), ALU.mult).then_inc(cum_ready, 1)
            for c in range(3):
                V.tensor_tensor_scan(arena[:, D0 + c, :], C("reset"), arena[:, LW0 + c, :], 0.0, ALU.mult, ALU.add)
            link(V.tensor_tensor_scan(arena[:, D0 + 3, :], C("reset"), arena[:, LW0 + 3, :], 0.0, ALU.mult, ALU.add))
            cum = tiles(D0).rearrange("q p (n c) -> q p n c", c=CH)
            link(V.tensor_scalar(HALF, cum[:, :, :, CH - 1], 0.5, None, ALU.mult))
            link(V.tensor_tensor(cum, cum, HALF.unsqueeze(3).to_broadcast([P, NP, NC, CH]), ALU.subtract))
            V.tensor_tensor(FAC[:, :, 0:NC - 1], HALF[:, :, 0:NC - 1], HALF[:, :, 1:NC], ALU.add)
            V.tensor_tensor(tiles(LW0), tiles(D0), tiles(LW0), ALU.subtract).then_inc(cum_ready, 1)
            for c in range(4):
                dve.wait_ge(z_done, 12 + c + 1)
                V.tensor_tensor(arena[:, BON0 + c, :], ps[4 + c][:, :], arena[:, VT + c, :], ALU.mult).then_inc(z_kept, 1)

            def by_chunk(first):
                return tiles(first).rearrange("q p (n c) -> q p n c", c=CH)

            dve.wait_ge(w_used, FIRST_UNIT["wout"])
            dve.wait_ge(exps, 1)
            dve.wait_ge(cum_ready, 1)
            V.tensor_tensor(BK[:, :, :, 0:CH], by_chunk(A0), by_chunk(E0), ALU.mult)
            V.tensor_tensor(BK[:, :, :, CH:P], by_chunk(KT), by_chunk(E0), ALU.mult).then_inc(ops, 1)
            dve.wait_ge(exps, 2)
            V.tensor_tensor(AR[:, :, :, CH:P], by_chunk(RT), by_chunk(A0), ALU.mult).then_inc(ops, 1)
            dve.wait_ge(exps, 3)
            for c in range(NP):
                V.scalar_tensor_tensor(AR[:, c, :, 0:CH], by_chunk(KK0)[:, c], -1.0, by_chunk(LW0)[:, c],
                                       ALU.mult, ALU.mult).then_inc(ops, 1)
            for g in range(4):
                dve.wait_ge(at_done, g + 1)
                V.tensor_tensor(AT[:, 8 * g:8 * g + 8, :], ps[g][:, :].rearrange("q (m c) -> q m c", c=CH),
                                C("atmask").unsqueeze(1).to_broadcast([P, 8, CH]), ALU.mult).then_inc(at_kept, 1)
            for n in range(NC):
                dve.wait_ge(mm_done, n + 1)
                for e in range(2):
                    V.tensor_tensor(MM[:, n, e, :, :], ps[4 + 2 * (n % 2) + e][:, :].rearrange("q (p c) -> q p c", p=NP),
                                    C("mmask").unsqueeze(1).to_broadcast([P, NP, P]), ALU.mult).then_inc(mm_kept, 1)
            dve.wait_ge(bt_done, NC)
            dve.wait_ge(at_kept, 4)
            V.tensor_tensor(OFF, AT, C("offblock").unsqueeze(1).to_broadcast([P, 32, CH]), ALU.mult).then_inc(off_ready, 1)
            dve.wait_ge(blk_in, 16)
            link(V.memset(TB, 0.0))
            for e in range(2):
                diag = side[:, 8, BLK * BLK * e:BLK * BLK * (e + 1)]
                ins = V.memset(diag[:, 0:BLK * BLK:BLK + 1], 1.0)
            link(ins)
            for t in range(1, BLK):
                prod = PROD[:, 0:2 * t * t].rearrange("q (e j s) -> q e j s", e=2, j=t)
                link(V.tensor_tensor(prod, TB[:, :, 0:t, 0:t].rearrange("q e s j -> q e j s"),
                                     AB[:, :, 0:t, t].unsqueeze(2).to_broadcast([P, 2, t, t]), ALU.mult))
                link(V.tensor_reduce(TB[:, :, t, 0:t], prod, AX_X, ALU.add))
            V.tensor_copy(TBT, TB.rearrange("q e t j -> q e j t")).then_inc(inv_ready, 1)

            for i in range(T // P):
                k0 = CH if i == 0 else 0
                w_ = 192 - k0
                for b in range(4):
                    dve.wait_ge(s_done, 4 * i + b + 1)
                    if i:
                        dve.wait_ge(pt_done, 2 * i - 1)
                    V.scalar_tensor_tensor(SC[:, 2 * b:2 * b + 2, k0:192],
                                           ps[4 + b][:, 0:384].rearrange("q (h k) -> q h k", h=2)[:, :, k0:192], SCALE,
                                           C("winmask")[:, k0:192].unsqueeze(1).to_broadcast([P, 2, w_]),
                                           ALU.mult, ALU.add).then_inc(s_kept, 1)
                dve.wait_ge(s_kept, 4 * i + 4)
                link(V.tensor_reduce(MX, SC[:, :, k0:192], AX_X, ALU.max))
                link(V.tensor_tensor(MX, MX, SINK, ALU.max))
                V.tensor_scalar(NMX, MX, -1.0, None, ALU.mult).then_inc(mx_ready, 1)
                V.tensor_tensor(ESK, SINK, MX, ALU.subtract).then_inc(mx_ready, 1)
                dve.wait_ge(e_ready, i + 1)
                link(V.tensor_tensor(DEN, DEN, ESK, ALU.add))
                link(V.reciprocal(DEN, DEN))
                V.tensor_tensor(SC[:, :, k0:192], SC[:, :, k0:192], DEN.unsqueeze(2).to_broadcast([P, NH, w_]),
                                ALU.mult).then_inc(p_ready, 1)
                dve.wait_ge(pt_done, max(1, 2 * i))
                V.tensor_copy(PT1[:, 4:8, :], ps[1][:, :].rearrange("q (h c) -> q h c", h=4)).then_inc(pt_dve, 1)
                if i:
                    dve.wait_ge(pt_done, 2 * i + 1)
                    V.tensor_copy(PT0[0:CH, 4:8, :], ps[3][0:CH, :].rearrange("q (h c) -> q h c", h=4)).then_inc(pt_dve, 1)

            for g in range(4):
                dve.wait_ge(q_done, g + 1)
                V.tensor_copy(QQ[:, 8 * g:8 * g + 8, :], ps[g][:, :].rearrange("q (m c) -> q m c", c=CH)).then_inc(q_kept, 1)
            for it in range(NB - 1):
                for g in range(4):
                    dve.wait_ge(tt_done, 4 * it + g + 1)
                    V.tensor_tensor(TT[:, 8 * g:8 * g + 8, :], ps[4 * ((it + 1) % 2) + g][:, :].rearrange("q (m c) -> q m c", c=CH),
                                    DIT[:, 8 * g:8 * g + 8, :], ALU.add).then_inc(tt_kept, 1)

            for n in range(NC):
                dve.wait_ge(r_done, n + 1)
                V.tensor_copy(RS, ps[0][:, 0:NP * CH].rearrange("q (p c) -> q p c", p=NP)).then_inc(r_kept, 1)
                dve.wait_ge(u_done, n + 1)
                V.tensor_copy(UV[0:CH, n, :, 0:CH], ps[2][0:CH, 0:NP * CH].rearrange("q (p c) -> q p c", p=NP)).then_inc(u_dve, 1)
                if n < NC - 1:
                    dve.wait_ge(st_done, n + 1)
                    delta = ps[4][:, 0:NP * CH].rearrange("q (p c) -> q p c", p=NP)
                    new = ST[:, (n + 1) % 2]
                    if n:
                        link(V.tensor_tensor(new, delta, ST[:, n % 2], ALU.add))
                        delta = new
                    else:
                        dve.wait_ge(exps, 4)
                    V.tensor_tensor(new, delta, FAC[:, :, n:n + 1].to_broadcast([P, NP, CH]), ALU.mult).then_inc(st_kept, 1)

            for c in range(4):
                dve.wait_ge(gn_done, c + 1)
                V.scalar_tensor_tensor(arena[:, DI0 + c, :], ps[c][:, :], -1.0 / HD, arena[:, DI0 + c, :],
                                       ALU.mult, ALU.add).then_inc(gn_kept, 1)
            for c in range(4):
                dve.wait_ge(gn_done, 4 + c + 1)
                V.tensor_scalar(GN_X[:, c, :], ps[4 + c][:, :], 1.0 / HD, GN_EPS, ALU.mult, ALU.add).then_inc(gn_kept, 1)
            dve.wait_ge(gn_root, 1)
            inverse_root(GN_Y, GN_X, GN_T)
            link(V.tensor_tensor(Y, Y, GN_Y, ALU.mult))
            for c in range(3):
                V.tensor_scalar(arena[:, DI0 + c, :], arena[:, DI0 + c, :], par_col("ln_w", c), par_col("ln_b", c),
                                ALU.mult, ALU.add)
            link(V.tensor_scalar(arena[:, DI0 + 3, :], arena[:, DI0 + 3, :], par_col("ln_w", 3), par_col("ln_b", 3),
                                 ALU.mult, ALU.add))
            link(V.tensor_tensor(Y, Y, tiles(BON0), ALU.add))
            dve.wait_ge(g_kept, 4)
            V.tensor_tensor(Y, Y, tiles(G0), ALU.mult).then_inc(mix_ready, 4)
            for k in range(KD):
                dve.wait_ge(mix_hi_done, k + 1)
                src = arena[:, QT + k, :] if k < 4 else arena[:, DI0 + k - 4, :]
                V.tensor_tensor(mix_lo[:, k, :], src, mix_hi[:, k, :].bitcast(F32), ALU.subtract).then_inc(mix_lo_done, 1)

            def wout_body(i):
                first = isinstance(i, int) and i == 0
                for j in range(NRAW):
                    low("wout", i, j)
                    if not (first and j == 0):
                        residual(KD, "wout", NRAW * i + j - 1, 1, 5 + (j + 1) % 2, 1.0)
                        h_low(KD, NRAW * i + j - 1)
                        add_square(KD, NRAW * i + j - 1, (j + 1) % 2)

            wout_body(0)
            with dve.Fori(1, units("wout")[1]) as i:
                wout_body(i)
            ffn(2, "up2", "down2", KF)
            residual(2 * KD, "down2", KD - 1, 2, 5, 0.5)
            add_square(2 * KD, KD - 1, 1)
            norm(3)
            for k in range(KD):
                V.scalar_tensor_tensor(x[:, k, :], x[:, k, :], par_col("gf", k), rs[:, :], ALU.mult, ALU.mult).then_inc(y_ready, 1)

        @block.tensor
        def _(pe):
            M = nc.tensor

            def product(bank, j, cols, hi, lo, start, stop):
                whi, wlo = w_hi[:, j % NHL, cols:cols + P], w_lo[:, j % NHL, cols:cols + P]
                M.matmul(ps[bank][:, :], whi, hi, start=start, stop=False)
                M.matmul(ps[bank][:, :], whi, lo, start=False, stop=False)
                return M.matmul(ps[bank][:, :], wlo, hi, start=False, stop=stop)

            def unit(name, i, j, bank, hi, lo, k0, nk, last_k, h_base=None):
                pe.wait_ge(lo_done, FIRST_UNIT[name] + NRAW * i + j + 1)
                for k in range(nk):
                    if h_base is not None:
                        pe.wait_ge(h_lo_done, h_base + k + 1)
                    ins = product(bank, j, k * P, hi[:, k0 + k, :], lo[:, k0 + k, :], k0 + k == 0, k0 + k == last_k)
                ins.then_inc(w_used, 1)

            def norm_sum(n):
                pe.wait_ge(acc_done, KD * (n + 1))
                if n == 0:
                    pe.wait_ge(const_ready, 32)
                M.matmul(ps[7][:, :], C("ones"), acc[:, :], start=True, stop=True).then_inc(sum_done, 1)

            def ffn(n, up, down, fbase):
                def up_body(i):
                    for j in range(NRAW):
                        if j % 2 == 0:
                            ge(pe, up_done, fbase + 2 * i + j // 2 - 1)
                        first = isinstance(i, int) and i == 0 and j == 0
                        unit(up, i, j, j, h_hi, h_lo, 0, KD, KD - 1, KD * n if first else None)
                        if first:
                            norm_sum(n)

                def down_body(i):
                    for j in range(NRAW):
                        if j % 2 == 0:
                            ge(pe, resid_done, KD * n + 2 * i + j // 2 - 1)
                        unit(down, i, j, 4 + j // 2, hid_hi, hid_lo, KF // 2 * (j % 2), KF // 2, KF - 1)

                up_body(0)
                with pe.Fori(1, units(up)[1]) as i:
                    up_body(i)
                pe.wait_ge(hid_lo_done, fbase + KF)
                down_body(0)
                with pe.Fori(1, units(down)[1]) as i:
                    down_body(i)

            ffn(0, "up1", "down1", 0)

            def win_body(i):
                for j in range(NRAW):
                    ge(pe, proj, NRAW * i + j - 3)
                    first = isinstance(i, int) and i == 0 and j == 0
                    unit("win", i, j, j, h_hi, h_lo, 0, KD, KD - 1, KD if first else None)
                    if first:
                        norm_sum(1)

            win_body(0)
            win_body(1)
            pe.wait_ge(lora_w, 32)
            pe.wait_ge(lora_act, 1)
            for c in range(4):
                M.matmul(ps[4 + c][:, :], w2_t[:, c * P:c * P + P], WD, start=True, stop=True).then_inc(z_done, 1)
            for c in range(4):
                pe.wait_ge(z_kept, c + 1)
                M.matmul(ps[4 + c][:, :], a2_t[:, c * P:c * P + P], AD, start=True, stop=True).then_inc(z_done, 1)
            with pe.Fori(2, 4) as i:
                win_body(i)
            pe.wait_ge(kk_sq, 1)
            for c in range(4):
                pe.wait_ge(z_kept, 4 + c + 1)
                M.matmul(ps[4 + c][:, :], C("headones"), arena[:, D0 + c, :], start=True, stop=True).then_inc(z_done, 1)
            win_body(4)
            for c in range(4):
                pe.wait_ge(rk_ready, c + 1)
                pe.wait_ge(z_kept, 8 + c + 1)
                M.matmul(ps[4 + c][:, :], C("headones"), arena[:, BON0 + c, :], start=True, stop=True).then_inc(z_done, 1)

            pe.wait_ge(proj, IN_TILES)
            pe.wait_ge(roped, 1)
            for i in range(T // P):
                ins = M.transpose(ps[0][:, P * i:P * i + P], arena[:, AV, P * i:P * i + P], C("ident"))
            ins.then_inc(vt_done, 1)
            for i in range(1, T // P):
                ins = M.transpose(ps[1][0:CH, P * (i - 1):P * i], arena[:, AV, P * i - CH:P * i], C("ident"))
            ins.then_inc(vt_done, 1)

            pe.wait_ge(ops, 6)
            pe.wait_ge(vt_kept, 2)
            for g in range(4):
                for n in (2 * g, 2 * g + 1):
                    for p in range(NP):
                        for e in range(2):
                            r, m = CH * e, (n % 2 * NP + p) * CH
                            ins = M.matmul(ps[g][r:r + CH, m:m + CH], BK[r:r + CH, p, n, 0:CH], AR[r:r + CH, p, n, 0:CH],
                                           start=True, stop=True)
                ins.then_inc(at_done, 1)
            pe.wait_ge(z_kept, 16)
            for n in range(NC):
                ge(pe, mm_kept, 2 * (n - 1))
                for p in range(NP):
                    for e in range(2):
                        r = CH * e
                        ins = M.matmul(ps[4 + 2 * (n % 2) + e][:, p * P:p * P + P], BK[r:r + CH, p, n, :],
                                       AR[r:r + CH, p, n, :], start=True, stop=True)
                ins.then_inc(mm_done, 1)
                if n < 4:
                    pe.wait_ge(at_kept, n + 1)
                else:
                    pe.wait_ge(bt_kept, n - 3)
                for p in range(NP):
                    ins = M.transpose(ps[n % 4][:, p * P:p * P + P], BK[:, p, n, :], C("ident"))
                ins.then_inc(bt_done, 1)

            pe.wait_ge(roped, 5)
            pe.wait_ge(bt_kept, NC)
            pe.wait_ge(mm_kept, 2 * NC)
            for i in range(T // P):
                k0 = CH if i == 0 else 0
                ge(pe, o_kept, i)
                ge(pe, s_kept, 4 * i)
                for b in range(4):
                    e = b // 2
                    r = CH * e
                    for p in (2 * (b % 2), 2 * (b % 2) + 1):
                        c = p % 2 * 192
                        ins = M.matmul(ps[4 + b][:, c + k0:c + 192], arena[r:r + CH, QT + p, P * i:P * i + P],
                                       arena[r:r + CH, AK, P * i - CH + k0:P * i + P], start=True, stop=True)
                    ins.then_inc(s_done, 1)
                pe.wait_ge(p_ready, i + 1)
                if i:
                    pe.wait_ge(pt_act, 2 * i - 1)
                    pe.wait_ge(pt_dve, 2 * i - 1)
                for h in range(NH):
                    ins = M.transpose(ps[h // 4][:, h % 4 * P:h % 4 * P + P], SC[:, h, CH:192], C("ident"))
                ins.then_inc(pt_done, 1)
                if i:
                    for h in range(NH):
                        ins = M.transpose(ps[2 + h // 4][0:CH, h % 4 * P:h % 4 * P + P], SC[:, h, 0:CH], C("ident"))
                    ins.then_inc(pt_done, 1)
                pe.wait_ge(pt_act, max(1, 2 * i + 1))
                pe.wait_ge(pt_dve, max(1, 2 * i + 1))
                for p in range(NP):
                    for e in range(2):
                        o = ps[4][CH * e:CH * e + CH, p * P:p * P + P]
                        ins = M.matmul(o, VA[:, i, CH * e:CH * e + CH], PT1[:, NP * e + p, :], start=True, stop=i == 0)
                        if i:
                            ins = M.matmul(o, VB[0:CH, i - 1, CH * e:CH * e + CH], PT0[0:CH, NP * e + p, :],
                                           start=False, stop=True)
                ins.then_inc(o_done, 1)

            pe.wait_ge(off_ready, 1)
            pe.wait_ge(inv_in, 16 * 4 * NB)
            pe.wait_ge(pt_act, 7)
            pe.wait_ge(pt_dve, 7)
            pe.wait_ge(o_kept, T // P)

            def by_matrix(bank, g, lhs, rhs, done):
                for m in range(8 * g, 8 * g + 8):
                    for e in range(2):
                        r = CH * e
                        ins = M.matmul(ps[bank][r:r + CH, m % 8 * CH:m % 8 * CH + CH], lhs[r:r + CH, m, :], rhs[r:r + CH, m, :],
                                       start=True, stop=True)
                ins.then_inc(done, 1)

            for g in range(4):
                by_matrix(g, g, OFF, DI, q_done)
            for it in range(NB - 1):
                for g in range(4):
                    pe.wait_ge(q_kept, g + 1)
                    if it:
                        pe.wait_ge(tt_kept, 4 * (it - 1) + g + 1)
                    by_matrix(4 * ((it + 1) % 2) + g, g, QQ, TT if it else DIT, tt_done)

            for n in range(NC):
                pe.wait_ge(v_kept, n - 3) if n >= 4 else pe.wait_ge(tt_kept, 4 + n + 1)
                for p in range(NP):
                    ins = M.transpose(ps[n % 4][0:CH, p * P:p * P + P], arena[:, VT + p, CH * n:CH * n + CH], C("ident"))
                ins.then_inc(v_done, 1)
            pe.wait_ge(g2_in, 16)
            pe.wait_ge(tt_kept, 12)
            for c in range(4):
                M.matmul(ps[4 + c][:, :], g2_t[:, c * P:c * P + P], GD, start=True, stop=True).then_inc(g_done, 1)

            pe.wait_ge(v_kept, NC)
            pe.wait_ge(zeroed, 3)
            pe.wait_ge(g_kept, 4)
            for n in range(NC):
                ge(pe, r_kept, n)
                for p in range(NP):
                    for e in range(2):
                        r = CH * e
                        o = ps[0][r:r + CH, p * CH:p * CH + CH]
                        ins = M.matmul(o, MM[:, n, e, p, 0:CH], UV[:, n, p, r:r + CH], start=True, stop=n == 0)
                        if n:
                            if p == 0 and e == 0:
                                pe.wait_ge(st_kept, n)
                            ins = M.matmul(o, AR[r:r + CH, p, n, 0:CH], ST[r:r + CH, n % 2, p, :], start=False, stop=True)
                ins.then_inc(r_done, 1)
                pe.wait_ge(r_kept, n + 1)
                for p in range(NP):
                    for e in range(2):
                        r = CH * e
                        ins = M.matmul(ps[2 + e][0:CH, p * CH:p * CH + CH], TT[r:r + CH, n * NP + p, :], RS[r:r + CH, p, :],
                                       start=True, stop=True)
                ins.then_inc(u_done, 1)
                pe.wait_ge(u_dve, n + 1)
                pe.wait_ge(u_act, n + 1)
                if n < NC - 1:
                    for p in range(NP):
                        for e in range(2):
                            r = CH * e
                            ins = M.matmul(ps[4][r:r + CH, p * CH:p * CH + CH], BT[:, n, p, r:r + CH], UV[:, n, p, r:r + CH],
                                           start=True, stop=True)
                    ins.then_inc(st_done, 1)
                ge(pe, y_kept, n - 1)
                for p in range(NP):
                    for e in range(2):
                        r = CH * e
                        o = ps[5 + n % 2][r:r + CH, p * CH:p * CH + CH]
                        ins = M.matmul(o, UV[:, n, p, r:r + CH], MM[:, n, e, p, CH:P], start=True, stop=n == 0)
                        if n:
                            ins = M.matmul(o, ST[r:r + CH, n % 2, p, :], AR[r:r + CH, p, n, CH:P], start=False, stop=True)
                ins.then_inc(y_done, 1)

            pe.wait_ge(y_kept, NC)
            for c in range(4):
                M.matmul(ps[c][:, :], C("headones"), arena[:, DI0 + c, :], start=True, stop=True).then_inc(gn_done, 1)
            pe.wait_ge(gn_sq, 1)
            for c in range(4):
                M.matmul(ps[4 + c][:, :], C("headones"), GN_SQ[:, c, :], start=True, stop=True).then_inc(gn_done, 1)

            def wout_body(i):
                for j in range(NRAW):
                    ge(pe, resid_done, KD + NRAW * i + j - 1)
                    unit("wout", i, j, 5 + j % 2, mix_hi, mix_lo, 0, KD, KD - 1)

            pe.wait_ge(mix_lo_done, KD)
            pe.wait_ge(gn_kept, 8)
            with pe.Fori(0, units("wout")[1]) as i:
                wout_body(i)
            ffn(2, "up2", "down2", KF)
            norm_sum(3)


def unit_layout(wt, nk):
    k, n = wt.shape
    return np.ascontiguousarray(
        wt.reshape(k // (nk * P), nk, P, n // P, P).transpose(3, 0, 2, 1, 4).reshape(-1, P, nk * P))


def columns(v):
    return v.reshape(-1, P).T


def kernel(**inputs):
    import concourse.bacc as _bacc
    from concourse.bass_utils import run_bass_kernel_spmd as _run

    g = {k: np.asarray(v) for k, v in inputs.items()}
    nq, nkv = NH * HD, 2 * HD
    r0 = nq + 2 * nkv
    w_in, w_out = g["w_in"], g["w_out"]
    heads = np.arange(NH).reshape(2, NP).T.ravel()
    q_cols = (heads[:, None] * HD + np.arange(HD)[None, :]).ravel()
    lo = r0 + 3 * nq
    rw = np.concatenate([np.arange(lo + 64, lo + 160), np.arange(lo, lo + 32), np.arange(lo + 32, lo + 64),
                         np.arange(lo + 64, lo + 160), np.arange(r0 + nq, r0 + 2 * nq), np.arange(r0, r0 + nq),
                         np.arange(r0 + 2 * nq, r0 + 3 * nq)])
    cols = np.concatenate([rw, np.arange(nq, nq + nkv), np.arange(nq + nkv, r0), q_cols])
    rows = np.concatenate([q_cols, np.arange(nq, 2 * nq)])

    def up_units(a, b):
        return np.ascontiguousarray(np.stack([unit_layout(a, KD), unit_layout(b, KD)], 1).reshape(2 * KF, P, UP_UNIT))

    parts = {"g1": g["ffn1_norm"], "gm": g["mix_norm"], "g2": g["ffn2_norm"], "gf": g["final_norm"],
             "mu": g["rwkv_shift_mu"][rw - r0], "w0": g["rwkv_w0"], "a0": g["rwkv_a0"], "k_k": g["rwkv_k_k"],
             "k_a": g["rwkv_k_a"], "r_k": g["rwkv_r_k"].reshape(-1), "ln_w": g["rwkv_ln_w"], "ln_b": g["rwkv_ln_b"]}
    arrays = {
        "xT": np.ascontiguousarray(g["x"].reshape(T, KD, P).transpose(2, 1, 0)),
        "up1": up_units(g["ffn1_w_gate"], g["ffn1_w_up"]), "down1": unit_layout(g["ffn1_w_down"], KF // 2),
        "win": unit_layout(w_in[:, cols], KD), "wout": unit_layout(w_out[rows], KD),
        "up2": up_units(g["ffn2_w_gate"], g["ffn2_w_up"]), "down2": unit_layout(g["ffn2_w_down"], KF // 2),
        "params": np.ascontiguousarray(np.concatenate([columns(parts[n]) for n in PARAMS], 1)),
        "sinks": g["attn_sinks"], "w2": g["rwkv_w2"], "a2": g["rwkv_a2"], "g2": g["rwkv_g2"], "const": constants(),
    }
    nc = _bacc.Bacc("TRN2", target_bir_lowering=False, num_devices=1)
    d = {n: nc.dram_tensor(n, a.shape, F32, kind="ExternalInput").ap() for n, a in arrays.items()}
    out = nc.dram_tensor("out", (P, KD, T), F32, kind="ExternalOutput").ap()
    scratch = [nc.dram_tensor(n, (P, 2, BLK, BLK), F32, kind="Internal").ap() for n in ("blocks", "inverses", "inverses_t")]
    build(nc, d["xT"], {n: d[n] for n, _, _ in PHASES}, d["params"], d["sinks"], d["w2"], d["a2"], d["g2"], d["const"],
          *scratch, out)
    r = _run(nc, [arrays], core_ids=[0])
    return r.results[0]["out"].transpose(2, 1, 0).reshape(1, T, D)
```

```python
from contextlib import ExitStack

import numpy as np
import concourse.bass as bass
from concourse import mybir

P = 128
D = 1024
T = 512
FF = 2816
HD = 64
NH = 8
KD = D // P
KF = FF // P
CH = 64
NC = T // CH
NP = 4
BLK = 16
NB = CH // BLK
IN_TILES = 20
UP_UNIT = KD * P
DOWN_UNIT = KF // 2 * P
NORM_EPS = 1e-5
GN_EPS = 64e-5
KAPPA = float(np.exp(-0.5))
SCALE = HD ** -0.5
NEG = -1e30

ALU = mybir.AluOpType
ACT = mybir.ActivationFunctionType
AX_X = mybir.AxisListType.X
F32 = mybir.dt.float32
F32R = mybir.dt.float32r

LORA, KT, RT, VT, AK, AV, QT = 0, 2, 6, 10, 14, 15, 16
G0, LW0, A0, KK0, D0, E0, BON0, X0 = 20, 24, 28, 32, 36, 40, 44, 48
ARENA = 52
M0 = LW0
BT0 = KT
TT0 = E0
DI0 = X0
DIT0 = G0
RSW = G0 + 2
DIFF0 = QT + 2
SELECT0, KRT0 = QT + 1, QT
SELECT1, KRT1 = LORA, KT
SWAP_Q = [G0, G0 + 1, G0 + 3, G0]

PARAMS = {}
_at = 0
for _name, _n in [("g1", 8), ("gm", 8), ("g2", 8), ("gf", 8), ("mu", 14), ("w0", 4), ("a0", 4), ("k_k", 4),
                  ("k_a", 4), ("r_k", 4), ("ln_w", 4), ("ln_b", 4)]:
    PARAMS[_name] = (_at, _n)
    _at += _n
NPARAM = _at

CONST = {}
_at = 0
for _name, _n in [("cos", T), ("sin", T), ("reset", T), ("ident", P), ("ones", P), ("headones", P), ("mmask", P),
                  ("atmask", CH), ("offblock", CH), ("winmask", 192), ("eps", 4)]:
    CONST[_name] = (_at, _n)
    _at += _n
NCONST = _at

PHASES = [("up1", 2 * KF, UP_UNIT), ("down1", 2 * KD, DOWN_UNIT), ("win", IN_TILES, UP_UNIT),
          ("wout", KD, UP_UNIT), ("up2", 2 * KF, UP_UNIT), ("down2", 2 * KD, DOWN_UNIT)]
FIRST_UNIT = {}
_at = 0
for _name, _n, _ in PHASES:
    FIRST_UNIT[_name] = _at
    _at += _n
NRAW = 4
NHL = 2
RESID = {1: 0, 2: 2 * KD, 3: 3 * KD}
GAIN = ("g1", "gm", "g2")


def constants():
    c = np.zeros((P, NCONST), np.float32)

    def put(name, v):
        c[:, CONST[name][0]:CONST[name][0] + CONST[name][1]] = v

    half = HD // 2
    inv = np.float32(10000.0) ** (-np.arange(0, HD, 2, dtype=np.float32) / np.float32(HD))
    ang = np.arange(T, dtype=np.float32)[:, None] * inv[None, :].astype(np.float32)
    row = np.arange(P)
    put("cos", np.cos(ang).T[row % half])
    put("sin", np.sin(ang).T[row % half] * np.where(row % HD < half, -1.0, 1.0)[:, None])
    put("reset", (np.arange(T) % CH != 0)[None, :])
    put("ident", np.eye(P))
    put("ones", 1.0)
    put("headones", row[:, None] // HD == row[None, :] // HD)
    s, t = row[:, None] % CH, np.arange(CH)[None, :]
    put("mmask", np.concatenate([s < t, s <= t], 1))
    put("atmask", s < t)
    put("offblock", s // BLK != t // BLK)
    key = np.arange(192)[None, :]
    put("winmask", np.where((key >= CH * (row[:, None] // CH)) & (key < CH * (row[:, None] // CH) + 2 * CH), 0.0, NEG))
    c[:, CONST["eps"][0]] = NORM_EPS
    c[:, CONST["eps"][0] + 1] = GN_EPS
    return c


def head_selection():
    return (np.arange(NH)[:, None] == np.arange(NH * HD)[None, :] // HD).astype(np.float32)


def build(nc, xT, w, params, sinks, w2, a2, g2, const, selection, blocks_dram, inv_dram, invt_dram, out):
    ctx = ExitStack()
    with ctx:
        def keep(name, shape, dt=F32):
            return ctx.enter_context(nc.sbuf_tensor(name, shape, dt))

        def sem(name):
            return ctx.enter_context(nc.semaphore(name))

        x = keep("x", [P, KD, T])
        raw = keep("raw", [P, NRAW, DOWN_UNIT])
        par = keep("par", [P, NPARAM])
        cst = keep("cst", [P, NCONST])
        small = keep("small", [P, 220])

        def overlay(*layouts):
            made = []
            for n, layout in enumerate(layouts):
                scope = ExitStack()
                made += [(ctx if n == len(layouts) - 1 else scope).enter_context(nc.sbuf_tensor(*t)) for t in layout]
                if n < len(layouts) - 1:
                    scope.close()
            return made

        h_hi, h_lo, armain = overlay(
            [("h_hi", [P, KD, T], F32R), ("h_lo", [P, KD, T], F32R)],
            [("chunk_ops", [P, 2 * KD, T], F32)])
        w_hi, w_lo, side = overlay(
            [("w_hi", [P, NHL, DOWN_UNIT], F32R), ("w_lo", [P, NHL, DOWN_UNIT], F32R)],
            [("side", [P, 11, T], F32)])
        hid_hi, hid_lo, sil, tmp, acc, rs, nt, _, mix_hi, mix_lo, arena = overlay(
            [("hid_hi", [P, KF, T], F32R), ("hid_lo", [P, KF, T], F32R), ("sil", [P, 2, T], F32),
             ("tmp", [P, 2, T], F32), ("acc", [P, T], F32), ("rs", [P, T], F32), ("nt", [P, T], F32)],
            [("before_mix", [P, M0, T], F32), ("mix_hi", [P, KD, T], F32R), ("mix_lo", [P, KD, T], F32R)],
            [("arena", [P, ARENA, T], F32)])
        ps = [ctx.enter_context(nc.psum_tensor(f"ps{i}", [P, T], F32)) for i in range(8)]

        def C(name, rows=P):
            a, n = CONST[name]
            return cst[0:rows, a:a + n]

        def par_col(name, i, lo=0, hi=P):
            return par[lo:hi, PARAMS[name][0] + i:PARAMS[name][0] + i + 1]

        def par_at(name, i):
            a, n = PARAMS[name]
            return par[:, a:a + n][:, i:i + 1] if isinstance(i, int) else par[:, bass.ds(i + a, 1)]

        def par_all(name):
            a, n = PARAMS[name]
            return par[:, a:a + n]

        def tiles(first, n=4):
            return arena[:, first:first + n, :]

        def by_chunk(first):
            return tiles(first).rearrange("q p (n c) -> q p n c", c=CH)

        AR = armain[:, 0:8, :].rearrange("q a b -> q (a b)").rearrange("q (p n c) -> q p n c", p=NP, n=NC)
        BK = armain[:, 8:16, :].rearrange("q a b -> q (a b)").rearrange("q (p n c) -> q p n c", p=NP, n=NC)
        OFF = side[:, 7:11, :].rearrange("q a b -> q (a b)").rearrange("q (m c) -> q m c", c=CH)
        QQ = side[:, 3:7, :].rearrange("q a b -> q (a b)").rearrange("q (m c) -> q m c", c=CH)
        UV = armain[:, 8:16, :].rearrange("q a b -> q (a b)").rearrange("q (n p c) -> q n p c", n=NC, p=NP)
        MM = tiles(M0, 16).rearrange("q a b -> q (a b)").rearrange("q (n e p c) -> q n e p c", n=NC, e=2, p=NP)
        BT = tiles(BT0, 8).rearrange("q a b -> q (a b)").rearrange("q (n p c) -> q n p c", n=NC, p=NP)
        def mats(first):
            return tiles(first).rearrange("q a b -> q (a b)").rearrange("q (m c) -> q m c", c=CH)

        AT = mats(LW0)
        TT = mats(TT0)
        DI, DIT = mats(DI0), mats(DIT0)
        Y = tiles(DI0)
        SC = side[:, 0:3, :].rearrange("q a b -> q (a b)").rearrange("q (h k) -> q h k", h=NH)
        PT1 = side[:, 3:5, :].rearrange("q a b -> q (a b)").rearrange("q (h k) -> q h k", h=NH)
        PT0 = side[:, 5:7, :].rearrange("q a b -> q (a b)").rearrange("q (h k) -> q h k", h=NH)
        AB = arena[:, X0, :].rearrange("q (e s t) -> q e s t", e=2, s=BLK)
        TB = arena[:, X0 + 1, :].rearrange("q (e t j) -> q e t j", e=2, t=BLK)
        TBT = arena[:, X0 + 2, :].rearrange("q (e j t) -> q e j t", e=2, j=BLK)
        PROD = arena[:, X0 + 3, :]
        RS = side[:, 7, 0:256].rearrange("q (p c) -> q p c", p=NP)
        ST = side[:, 8, :].rearrange("q (b p c) -> q b p c", b=2, p=NP)
        VA = arena[:, LORA + 1, :].rearrange("q (i c) -> q i c", c=P)
        VB = arena[:, AV, :].rearrange("q (i c) -> q i c", c=P)
        HALF = small[:, 0:32].rearrange("q (p n) -> q p n", p=NP)
        FAC = small[:, 32:64].rearrange("q (p n) -> q p n", p=NP)
        MX, NMX, DEN, ESK = (small[:, 64 + 8 * i:72 + 8 * i] for i in range(4))
        OMKA = small[:, 96:100]
        SINK = small[:, 104:112]
        KS, KR, KX = (small[:, 112 + 32 * i:144 + 32 * i] for i in range(3))
        MS, NR, NX = (small[:, 208 + 4 * i:212 + 4 * i] for i in range(3))
        GN_SQ = armain[:, 0:4, :]
        GD = arena[0:96, LORA, :]
        WD = arena[96:128, LORA, :]
        AD = arena[0:32, LORA + 1, :]
        w2_t, a2_t, g2_t = arena[96:128, G0, :], arena[0:32, G0 + 1, :], side[0:96, 9, :]

        raw_ready = [sem(f"raw_ready{j}") for j in range(NRAW)]
        hi_done = sem("hi_done")
        lo_done = sem("lo_done")
        w_used = sem("w_used")
        x_ready = [sem(f"x_ready{k}") for k in range(KD)]
        par_ready = sem("par_ready")
        const_ready = sem("const_ready")
        sq_done = sem("sq_done")
        acc_done = sem("acc_done")
        sum_done = sem("sum_done")
        ms_done = sem("ms_done")
        ms_root = sem("ms_root")
        root_done = sem("root_done")
        factor_done = sem("factor_done")
        y_ready = sem("y_ready")
        h_hi_done = sem("h_hi_done")
        h_lo_done = sem("h_lo_done")
        gate_done = sem("gate_done")
        silu_done = sem("silu_done")
        up_done = sem("up_done")
        hid_done = sem("hid_done")
        hid_hi_done = sem("hid_hi_done")
        hid_lo_done = sem("hid_lo_done")
        resid_done = sem("resid_done")
        dve_own = sem("dve_own")
        out_done = sem("out_done")
        proj = sem("proj")
        lora_w = sem("lora_w")
        diffed = sem("diffed")
        shifted = sem("shifted")
        lora_act = sem("lora_act")
        z_done = sem("z_done")
        z_kept = sem("z_kept")
        omka_ready = sem("omka_ready")
        kk_raw = sem("kk_raw")
        kk_sq = sem("kk_sq")
        ks_done = sem("ks_done")
        ks_ready = sem("ks_ready")
        ks_root = sem("ks_root")
        kr_ready = sem("kr_ready")
        krt_done, krt_kept = sem("krt_done"), sem("krt_kept")
        select_in = sem("select_in")
        kk_ready = sem("kk_ready")
        k_ready = sem("k_ready")
        rk_ready = sem("rk_ready")
        scanned = sem("scanned")
        cum_ready = sem("cum_ready")
        exps = sem("exps")
        ka_ready = sem("ka_ready")
        early_b, early_a = sem("early_b"), sem("early_a")
        ops_act = sem("ops_act")
        ops_dve = sem("ops_dve")
        swap_in = [sem(f"swap_in{n}") for n in range(5)]
        rope_own = sem("rope_own")
        roped = sem("roped")
        zeroed = sem("zeroed")
        at_done, at_kept = sem("at_done"), sem("at_kept")
        mm_done, mm_kept = sem("mm_done"), sem("mm_kept")
        bt_done, bt_kept = sem("bt_done"), sem("bt_kept")
        vt_done, vt_kept = sem("vt_done"), sem("vt_kept")
        blk_out, blk_in = sem("blk_out"), sem("blk_in")
        inv_ready = sem("inv_ready")
        inv_out, inv_in = sem("inv_out"), sem("inv_in")
        s_done, s_kept = sem("s_done"), sem("s_kept")
        mx_ready = sem("mx_ready")
        e_ready = sem("e_ready")
        p_ready = sem("p_ready")
        pt_done = sem("pt_done")
        pt0_done = sem("pt0_done")
        pt_act, pt_dve = sem("pt_act"), sem("pt_dve")
        o_done, o_kept = sem("o_done"), sem("o_kept")
        off_ready = sem("off_ready")
        q_done, q_kept = sem("q_done"), sem("q_kept")
        tt_done, tt_kept = sem("tt_done"), sem("tt_kept")
        v_done, v_kept = sem("v_done"), sem("v_kept")
        g2_in = sem("g2_in")
        g_done, g_kept = sem("g_done"), sem("g_kept")
        r_done, r_kept = sem("r_done"), sem("r_kept")
        u_done, u_dve, u_act = sem("u_done"), sem("u_dve"), sem("u_act")
        st_done, st_kept = sem("st_done"), sem("st_kept")
        y_done, y_kept = sem("y_done"), sem("y_kept")
        gn_done = sem("gn_done")
        gn_kept = sem("gn_kept")
        gn_sq = sem("gn_sq")
        tail_ready = sem("tail_ready")
        mix_ready = sem("mix_ready")
        mix_hi_done = sem("mix_hi_done")
        mix_lo_done = sem("mix_lo_done")

        def ge(eng, s, v):
            if not (isinstance(v, int) and v <= 0):
                eng.wait_ge(s, v)

        def units(name):
            return FIRST_UNIT[name], dict((n, k) for n, k, _ in PHASES)[name] // NRAW

        block = ctx.enter_context(nc.Block())

        @block.sync
        def _(sp):
            sp.dma_start(par[:, :], params).then_inc(par_ready, 16)

            def load(name, i, j):
                n = dict((a, c) for a, _, c in PHASES)[name]
                ge(sp, lo_done, FIRST_UNIT[name] + NRAW * i + j + 1 - NRAW)
                sp.dma_start(raw[:, j, 0:n], w[name][NRAW * i + j]).then_inc(raw_ready[j], 16)

            def load_all(name, first=0):
                with sp.Fori(first, units(name)[1]) as i:
                    for j in range(NRAW):
                        load(name, i, j)

            for k in range(KD):
                sp.dma_start(x[:, k, :], xT[:, k, :]).then_inc(x_ready[k], 16)
                if k < NRAW:
                    load("up1", 0, k)
            sp.dma_start(cst[:, :], const).then_inc(const_ready, 16)
            sp.dma_start(SINK, sinks.partition_broadcast(P)).then_inc(const_ready, 16)
            load_all("up1", 1)
            load_all("down1")
            load("win", 0, 0)
            load("win", 0, 1)
            load("win", 0, 2)
            load("win", 0, 3)
            sp.wait_ge(w_used, FIRST_UNIT["win"])
            sp.dma_start(w2_t, w2).then_inc(lora_w, 16)
            sp.dma_start(a2_t, a2).then_inc(lora_w, 16)
            sp.dma_start(arena[0:NH, SELECT0, :], selection).then_inc(select_in, 16)
            with sp.Fori(1, 4) as i:
                for j in range(NRAW):
                    load("win", i, j)
            load("win", 4, 0)
            load("win", 4, 1)
            sp.wait_ge(at_kept, 4)
            for e in range(2):
                for b in range(NB):
                    r = CH * e + BLK * b
                    sp.dma_start(blocks_dram[32 * b:32 * b + 32, e].rearrange("m s t -> s m t"),
                                 AT[r:r + BLK, :, BLK * b:BLK * b + BLK]).then_inc(blk_out, 16)
            load("win", 4, 2)
            load("win", 4, 3)
            sp.wait_ge(blk_out, 16 * 2 * NB)
            sp.wait_ge(k_ready, 1)
            sp.dma_start(AB, blocks_dram).then_inc(blk_in, 16)

            def swap(n, src, dst):
                for a in range(4):
                    b = a ^ 1
                    sp.dma_start(arena[32 * a:32 * a + 32, dst, :],
                                 arena[32 * b:32 * b + 32, src, :]).then_inc(swap_in[n], 16)

            sp.wait_ge(z_done, 8)
            sp.wait_ge(proj, AK + 1)
            swap(0, AK, LORA + 1)
            for i in range(3):
                sp.wait_ge(proj, QT + i + 1)
                swap(i + 1, QT + i, SWAP_Q[i])
            sp.wait_ge(inv_ready, 1)
            sp.dma_start(inv_dram, TB).then_inc(inv_out, 16)
            sp.dma_start(invt_dram, TBT).then_inc(inv_out, 16)
            sp.wait_ge(proj, QT + 4)
            sp.wait_ge(roped, 2)
            swap(4, QT + 3, SWAP_Q[3])
            sp.wait_ge(inv_out, 32)
            sp.wait_ge(zeroed, 2)
            for e in range(2):
                for b in range(NB):
                    r = CH * e + BLK * b
                    for dst, src in ((DI, inv_dram), (DIT, invt_dram)):
                        sp.dma_start(dst[r:r + BLK, :, BLK * b:BLK * b + BLK],
                                     src[32 * b:32 * b + 32, e].rearrange("m t j -> t m j")).then_inc(inv_in, 16)
            for j in range(NRAW):
                load("wout", 0, j)
            sp.wait_ge(q_done, 4)
            sp.dma_start(g2_t, g2).then_inc(g2_in, 16)
            sp.wait_ge(g_done, 4)
            sp.dma_start(arena[0:NH, SELECT1, :], selection).then_inc(select_in, 16)
            load_all("wout", 1)
            load_all("up2")
            load_all("down2")
            for k in range(KD):
                sp.wait_ge(y_ready, k + 1)
                sp.dma_start(out[:, k, :], x[:, k, :]).then_inc(out_done, 16)
            sp.wait_ge(out_done, 16 * KD)

        @block.gpsimd
        def _(pool):
            own = [0]

            def link(ins):
                own[0] += 1
                ins.then_inc(rope_own, 1)
                pool.wait_ge(rope_own, own[0])

            def diff(t):
                pool.wait_ge(proj, t + 1)
                ge(pool, shifted, t - 1)
                d, p = arena[:, DIFF0 + t % 2, :], arena[:, t, :]
                link(nc.gpsimd.tensor_tensor(d[:, 1:T], p[:, 0:T - 1], p[:, 1:T], ALU.subtract))
                nc.gpsimd.tensor_scalar(d[:, 0:1], p[:, 0:1], -1.0, None, ALU.mult).then_inc(diffed, 1)

            for t in range(8):
                diff(t)
            pool.wait_ge(z_kept, 8)
            pool.wait_ge(omka_ready, 1)
            for c in range(4):
                ins = nc.gpsimd.tensor_scalar(arena[:, X0 + c, :], arena[:, A0 + c, :], par_col("k_a", c),
                                              OMKA[:, c:c + 1], ALU.mult, ALU.add)
            link(ins)
            diff(8)
            pool.wait_ge(kk_raw, 4)
            nc.gpsimd.tensor_tensor(tiles(KT), tiles(KT), tiles(X0), ALU.mult).then_inc(k_ready, 1)
            diff(9)
            pool.wait_ge(kk_ready, 4)
            nc.gpsimd.tensor_tensor(tiles(A0), tiles(KK0), tiles(A0), ALU.mult).then_inc(ka_ready, 1)
            diff(10)
            pool.wait_ge(exps, 1)
            pool.wait_ge(ka_ready, 1)
            nc.gpsimd.tensor_tensor(tiles(A0), tiles(A0), tiles(E0), ALU.mult).then_inc(early_b, 1)
            for t in range(11, 14):
                diff(t)
            pool.wait_ge(const_ready, 32)
            for n, (x_t, s_t) in enumerate([(AK, LORA + 1)] + [(QT + i, SWAP_Q[i]) for i in range(4)]):
                pool.wait_ge(swap_in[n], 64)
                link(nc.gpsimd.tensor_tensor(arena[:, x_t, :], arena[:, x_t, :], C("cos"), ALU.mult))
                link(nc.gpsimd.tensor_tensor(arena[:, s_t, :], arena[:, s_t, :], C("sin"), ALU.mult))
                nc.gpsimd.tensor_tensor(arena[:, x_t, :], arena[:, x_t, :], arena[:, s_t, :], ALU.add).then_inc(roped, 1)
            pool.wait_ge(inv_out, 32)
            nc.gpsimd.memset(tiles(DI0), 0.0).then_inc(zeroed, 1)
            pool.wait_ge(roped, 5)
            nc.gpsimd.memset(tiles(DIT0), 0.0).then_inc(zeroed, 1)
            pool.wait_ge(bt_done, NC)
            pool.wait_ge(mm_done, NC)
            nc.gpsimd.memset(UV[0:CH, :, :, :], 0.0).then_inc(zeroed, 1)
            pool.wait_ge(z_kept, 12)
            pool.wait_ge(g_kept, 4)
            for c in range(4):
                ins = nc.gpsimd.tensor_scalar(arena[:, BON0 + c, :], arena[:, BON0 + c, :], par_col("ln_b", c), None, ALU.add)
            link(ins)
            link(nc.gpsimd.tensor_tensor(tiles(BON0), tiles(BON0), tiles(G0), ALU.mult))
            for c in range(4):
                nc.gpsimd.tensor_scalar(arena[:, G0 + c, :], arena[:, G0 + c, :], par_col("ln_w", c), None,
                                        ALU.mult).then_inc(tail_ready, 1)

        @block.scalar
        def _(act):
            A = nc.scalar

            def split(name, i, j):
                n = dict((a, c) for a, _, c in PHASES)[name]
                u = FIRST_UNIT[name] + NRAW * i + j
                act.wait_ge(raw_ready[j], 16 * (FIRST_UNIT[name] // NRAW + i + 1))
                ge(act, w_used, u + 1 - NHL)
                A.activation(w_hi[:, j % NHL, 0:n], raw[:, j, 0:n], ACT.Copy).then_inc(hi_done, 1)

            def silu(fbase, f, slot):
                act.wait_ge(gate_done, fbase + f + 1)
                A.activation(sil[:, slot, :], sil[:, slot, :], ACT.Silu).then_inc(silu_done, 1)

            def hid_high(fbase, f, slot):
                act.wait_ge(hid_done, fbase + f + 1)
                A.activation(hid_hi[:, f, :], tmp[:, slot, :], ACT.Copy).then_inc(hid_hi_done, 1)

            def square(n, d, slot):
                if n == 0:
                    act.wait_ge(x_ready[d], 16)
                else:
                    act.wait_ge(resid_done, RESID[n] + d + 1)
                ge(act, acc_done, KD * n + d - 1)
                if n < 3:
                    A.activation(h_hi[:, d, :], x[:, d, :], ACT.Copy, scale=par_at(GAIN[n], d)).then_inc(h_hi_done, 1)
                first = isinstance(d, int) and d == 0
                A.activation(acc[:, :] if first else sil[:, slot, :], x[:, d, :], ACT.Square).then_inc(sq_done, 1)

            def root(n):
                act.wait_ge(ms_done, n + 1)
                A.activation(NR, MS, ACT.Sqrt).then_inc(ms_root, 1)

            def krt_copy(n, bank, dst):
                act.wait_ge(krt_done, n + 1)
                A.activation(arena[0:NH, dst, :], bank[0:NH, :], ACT.Copy).then_inc(krt_kept, 1)

            def ffn(n, up, down, fbase):
                def up_body(i):
                    first = isinstance(i, int) and i == 0
                    split(up, i, 0)
                    if first:
                        if n == 2:
                            square(2, KD - 2, 0)
                            square(2, KD - 1, 1)
                    else:
                        silu(fbase, 2 * i - 1, 1)
                    split(up, i, 1)
                    if first:
                        root(n)
                    else:
                        hid_high(fbase, 2 * i - 1, 1)
                    split(up, i, 2)
                    silu(fbase, 2 * i, 0)
                    split(up, i, 3)
                    hid_high(fbase, 2 * i, 0)

                def down_body(i):
                    first = isinstance(i, int) and i == 0
                    split(down, i, 0)
                    if first:
                        silu(fbase, KF - 1, 1)
                    split(down, i, 1)
                    if first:
                        hid_high(fbase, KF - 1, 1)
                    else:
                        square(n + 1, 2 * i - 1, 1)
                    split(down, i, 2)
                    split(down, i, 3)
                    square(n + 1, 2 * i, 0)

                up_body(0)
                with act.Fori(1, units(up)[1]) as i:
                    up_body(i)
                down_body(0)
                with act.Fori(1, units(down)[1]) as i:
                    down_body(i)

            act.wait_ge(par_ready, 16)
            for d in range(KD):
                square(0, d, d % 2)
            ffn(0, "up1", "down1", 0)

            for t in range(IN_TILES):
                split("win", t // NRAW, t % NRAW)
                if t == 0:
                    square(1, KD - 1, 1)
                if t == 1:
                    root(1)
                if t == 6:
                    act.wait_ge(shifted, 2)
                    A.activation(WD, WD, ACT.Tanh).then_inc(lora_act, 1)
                    A.activation(GD, GD, ACT.Sigmoid).then_inc(lora_act, 1)
                if t == 9:
                    for c in range(4):
                        act.wait_ge(z_done, c + 1)
                        A.activation(arena[:, LW0 + c, :], ps[4 + c][:, :], ACT.Sigmoid,
                                     bias=par_col("w0", c)).then_inc(z_kept, 1)
                    act.wait_ge(kk_raw, 4)
                    A.activation(tiles(E0), tiles(KK0), ACT.Square).then_inc(kk_sq, 1)
                    for c in range(4):
                        act.wait_ge(z_done, 4 + c + 1)
                        A.activation(arena[:, A0 + c, :], ps[4 + c][:, :], ACT.Sigmoid,
                                     bias=par_col("a0", c)).then_inc(z_kept, 1)
                if t == 10:
                    act.wait_ge(ks_ready, 1)
                    A.activation(KR, KS, ACT.Sqrt).then_inc(ks_root, 1)
                if t == 11:
                    krt_copy(0, ps[7], KRT0)
                    act.wait_ge(cum_ready, 1)
                    A.activation(tiles(E0), tiles(D0), ACT.Exp, scale=KAPPA).then_inc(exps, 1)
                    A.activation(tiles(LW0), tiles(LW0), ACT.Exp, scale=-KAPPA).then_inc(exps, 1)
                if t == 12:
                    A.activation(tiles(D0), tiles(D0), ACT.Exp, scale=-KAPPA).then_inc(exps, 1)
                    A.activation(FAC[:, :, 0:NC - 1], FAC[:, :, 0:NC - 1], ACT.Exp, scale=-KAPPA).then_inc(exps, 1)

            act.wait_ge(w_used, FIRST_UNIT["wout"])
            act.wait_ge(early_b, 1)
            act.wait_ge(early_a, 1)
            for half in range(2):
                ns = slice(NC // 2 * half, NC // 2 * (half + 1))
                A.activation(BK[:, :, ns, 0:CH], by_chunk(A0)[:, :, ns], ACT.Copy).then_inc(ops_act, 1)
                A.activation(AR[:, :, ns, 0:CH], by_chunk(KK0)[:, :, ns], ACT.Copy).then_inc(ops_act, 1)

            act.wait_ge(vt_done, 2)
            act.wait_ge(roped, 1)
            A.activation(VA[:, :, :], ps[0][:, :].rearrange("q (i c) -> q i c", c=P), ACT.Copy).then_inc(vt_kept, 1)
            A.activation(VB[0:CH, 0:3, :], ps[1][0:CH, 0:3 * P].rearrange("q (i c) -> q i c", c=P),
                         ACT.Copy).then_inc(vt_kept, 1)
            act.wait_ge(ops_dve, 4)
            act.wait_ge(rk_ready, 4)
            for n in range(NC):
                act.wait_ge(bt_done, n + 1)
                A.activation(BT[:, n, :, :], ps[n % 4][:, :].rearrange("q (p c) -> q p c", p=NP), ACT.Copy).then_inc(bt_kept, 1)
            act.wait_ge(mm_done, NC)
            for n in range(NC):
                act.wait_ge(v_done, n + 1)
                A.activation(UV[CH:P, n, :, :], ps[n % 4][0:CH, :].rearrange("q (p c) -> q p c", p=NP),
                             ACT.Copy).then_inc(v_kept, 1)
            for c in range(4):
                act.wait_ge(g_done, c + 1)
                A.activation(arena[:, G0 + c, :], ps[4 + c][:, :], ACT.Copy).then_inc(g_kept, 1)

            def pt_copy(m):
                i, e = m // 2, m % 2
                act.wait_ge(pt_done, m + 1)
                A.activation(PT1[:, 4 * e:4 * e + 4, :], ps[5][:, :].rearrange("q (h c) -> q h c", h=4),
                             ACT.Copy).then_inc(pt_act, 1)

            def o_copy(m):
                i, e = m // 2, m % 2
                act.wait_ge(o_done, m + 1)
                r = CH * e
                A.activation(arena[r:r + CH, QT:QT + 4, P * i:P * i + P],
                             ps[7][r:r + CH, :].rearrange("q (p c) -> q p c", p=NP), ACT.Copy).then_inc(o_kept, 1)

            for n in range(NC):
                i, e = n // 2, n % 2
                k0 = CH if i == 0 else 0
                act.wait_ge(u_done, n + 1)
                A.activation(UV[0:CH, n, :, CH:P], ps[2][0:CH, 0:NP * CH].rearrange("q (p c) -> q p c", p=NP),
                             ACT.Copy).then_inc(u_act, 1)
                if n:
                    pt_copy(n - 1)
                    o_copy(n - 1)
                act.wait_ge(mx_ready, 2 * n + 2)
                for h in range(4 * e, 4 * e + 4):
                    A.activation(SC[:, h, k0:192], SC[:, h, k0:192], ACT.Exp, bias=NMX[:, h:h + 1],
                                 accum_out=DEN[:, h:h + 1])
                A.activation(ESK[:, 4 * e:4 * e + 4], ESK[:, 4 * e:4 * e + 4], ACT.Exp).then_inc(e_ready, 1)
                act.wait_ge(y_done, n + 1)
                A.activation(Y[:, :, CH * n:CH * n + CH], ps[4][:, 0:NP * CH].rearrange("q (p c) -> q p c", p=NP),
                             ACT.Copy).then_inc(y_kept, 1)
            pt_copy(NC - 1)
            act.wait_ge(pt0_done, NC - 2)
            split("wout", 0, 0)
            o_copy(NC - 1)

            def mix_high(k):
                src = arena[:, QT + k, :] if k < 4 else arena[:, DI0 + k - 4, :]
                A.activation(mix_hi[:, k, :], src, ACT.Copy).then_inc(mix_hi_done, 1)

            act.wait_ge(y_done, NC)
            act.wait_ge(o_kept, NC)
            for k in range(4):
                mix_high(k)
            split("wout", 0, 1)
            act.wait_ge(gn_kept, 4)
            A.activation(GN_SQ, Y, ACT.Square).then_inc(gn_sq, 1)
            act.wait_ge(ks_ready, 2)
            A.activation(KR, KS, ACT.Sqrt).then_inc(ks_root, 1)
            split("wout", 0, 2)
            krt_copy(1, ps[3], KRT1)
            split("wout", 0, 3)
            for k in range(4, KD):
                act.wait_ge(mix_ready, k - 3)
                mix_high(k)

            split("wout", 1, 0)
            for j in range(1, NRAW):
                split("wout", 1, j)
                square(2, 2 * j - 2, 0)
                square(2, 2 * j - 1, 1)
            ffn(2, "up2", "down2", KF)
            square(3, KD - 1, 1)
            root(3)

        @block.vector
        def _(dve):
            V = nc.vector
            own = [0]

            def link(ins):
                own[0] += 1
                ins.then_inc(dve_own, 1)
                dve.wait_ge(dve_own, own[0])

            def low(name, i, j):
                n = dict((a, c) for a, _, c in PHASES)[name]
                dve.wait_ge(hi_done, FIRST_UNIT[name] + NRAW * i + j + 1)
                V.tensor_tensor(w_lo[:, j % NHL, 0:n], raw[:, j, 0:n], w_hi[:, j % NHL, 0:n].bitcast(F32),
                                ALU.subtract).then_inc(lo_done, 1)

            def hidden(fbase, f, slot):
                dve.wait_ge(w_used, FIRST_UNIT["up1" if fbase == 0 else "up2"] + 2 * f + 2)
                ge(dve, hid_lo_done, fbase + f - 1)
                V.tensor_tensor(tmp[:, slot, :], ps[2 * slot + 1][:, :], rs[:, :], ALU.mult).then_inc(up_done, 1)
                dve.wait_ge(up_done, fbase + f + 1)
                dve.wait_ge(silu_done, fbase + f + 1)
                V.tensor_tensor(tmp[:, slot, :], tmp[:, slot, :], sil[:, slot, :], ALU.mult).then_inc(hid_done, 1)

            def gate(fbase, f, slot):
                dve.wait_ge(w_used, FIRST_UNIT["up1" if fbase == 0 else "up2"] + 2 * f + 1)
                ge(dve, hid_done, fbase + f - 1)
                V.tensor_tensor(sil[:, slot, :], ps[2 * slot][:, :], rs[:, :], ALU.mult).then_inc(gate_done, 1)

            def hid_low(fbase, f, slot):
                dve.wait_ge(hid_hi_done, fbase + f + 1)
                V.tensor_tensor(hid_lo[:, f, :], tmp[:, slot, :], hid_hi[:, f, :].bitcast(F32),
                                ALU.subtract).then_inc(hid_lo_done, 1)

            def residual(name, used, d, bank, scale):
                dve.wait_ge(w_used, FIRST_UNIT[name] + used)
                V.scalar_tensor_tensor(x[:, d, :], ps[bank][:, :], scale, x[:, d, :], ALU.mult, ALU.add).then_inc(resid_done, 1)

            def add_square(n, d, slot):
                dve.wait_ge(sq_done, KD * n + d + 1)
                if isinstance(d, int) and d == 0:
                    V.tensor_copy(small[:, 100:101], acc[:, 0:1]).then_inc(acc_done, 1)
                else:
                    dve.wait_ge(acc_done, KD * n + d)
                    V.tensor_tensor(acc[:, :], acc[:, :], sil[:, slot, :], ALU.add).then_inc(acc_done, 1)

            def inverse_root(y, xx, t, done):
                link(V.reciprocal(y, y))
                link(V.tensor_tensor(t, xx, y, ALU.mult))
                link(V.scalar_tensor_tensor(t, t, -0.5, y, ALU.mult, ALU.mult))
                V.scalar_tensor_tensor(y, t, 1.5, y, ALU.add, ALU.mult).then_inc(done, 1)

            def norm(n):
                dve.wait_ge(sum_done, n + 1)
                V.tensor_scalar(MS, ps[7][:, 0:T // P], 1.0 / D, NORM_EPS, ALU.mult, ALU.add).then_inc(ms_done, 1)
                dve.wait_ge(ms_done, n + 1)
                dve.wait_ge(ms_root, n + 1)
                inverse_root(NR, MS, NX, root_done)

            def factor(n, dst):
                dve.wait_ge(factor_done, n + 1)
                link(V.tensor_copy(dst, ps[7][:, :]))

            def h_low(n, d):
                dve.wait_ge(h_hi_done, KD * n + d + 1)
                V.scalar_tensor_tensor(h_lo[:, d, :], x[:, d, :], par_at(GAIN[n], d), h_hi[:, d, :].bitcast(F32),
                                       ALU.mult, ALU.subtract).then_inc(h_lo_done, 1)

            def wout_residual(u):
                for e in range(2):
                    residual("wout", u + 1, 2 * (u % NRAW) + e, 4 + 2 * (u % 2) + e, 1.0)
                if u >= NRAW:
                    for e in range(2):
                        h_low(2, 2 * (u - NRAW) + e)
                        add_square(2, 2 * (u - NRAW) + e, e)

            def ffn(n, up, down, fbase):
                def up_body(i):
                    first = isinstance(i, int) and i == 0
                    low(up, i, 0)
                    if first:
                        if n == 2:
                            wout_residual(KD - 1)
                    else:
                        hidden(fbase, 2 * i - 1, 1)
                    low(up, i, 1)
                    if first:
                        norm(n)
                    else:
                        hid_low(fbase, 2 * i - 1, 1)
                    low(up, i, 2)
                    if first:
                        factor(n, rs[:, :])
                    gate(fbase, 2 * i, 0)
                    hidden(fbase, 2 * i, 0)
                    low(up, i, 3)
                    gate(fbase, 2 * i + 1, 1)
                    hid_low(fbase, 2 * i, 0)

                def down_body(i):
                    first = isinstance(i, int) and i == 0
                    low(down, i, 0)
                    if first:
                        hidden(fbase, KF - 1, 1)
                    else:
                        residual(down, 4 * i, 2 * i - 1, 5, 0.5)
                        if n == 0:
                            h_low(1, 2 * i - 1)
                    low(down, i, 1)
                    if first:
                        hid_low(fbase, KF - 1, 1)
                    else:
                        add_square(n + 1, 2 * i - 1, 1)
                    low(down, i, 2)
                    residual(down, 4 * i + 2, 2 * i, 4, 0.5)
                    low(down, i, 3)
                    if n == 0:
                        h_low(1, 2 * i)
                    add_square(n + 1, 2 * i, 0)

                up_body(0)
                with dve.Fori(1, units(up)[1]) as i:
                    up_body(i)
                down_body(0)
                with dve.Fori(1, units(down)[1]) as i:
                    down_body(i)

            dve.wait_ge(par_ready, 16)
            for d in range(KD):
                h_low(0, d)
                add_square(0, d, d % 2)
            ffn(0, "up1", "down1", 0)

            def shift(t):
                dve.wait_ge(diffed, t + 1)
                p = arena[:, t, :]
                V.scalar_tensor_tensor(p, arena[:, DIFF0 + t % 2, :], par_col("mu", t), p, ALU.mult,
                                       ALU.add).then_inc(shifted, 1)

            def keep_proj(t):
                dve.wait_ge(w_used, FIRST_UNIT["win"] + t + 1)
                V.tensor_tensor(arena[:, t, :], ps[t % 4][:, :], arena[:, RSW, :], ALU.mult).then_inc(proj, 1)

            def substitute(first, last):
                for t in range(first, last):
                    prod = PROD[:, 0:2 * t * t].rearrange("q (e j s) -> q e j s", e=2, j=t)
                    link(V.tensor_tensor(prod, TB[:, :, 0:t, 0:t].rearrange("q e s j -> q e j s"),
                                         AB[:, :, 0:t, t].unsqueeze(2).to_broadcast([P, 2, t, t]), ALU.mult))
                    link(V.tensor_reduce(TB[:, :, t, 0:t], prod, AX_X, ALU.add))

            for t in range(IN_TILES):
                low("win", t // NRAW, t % NRAW)
                if t == 0:
                    residual("down1", 2 * KD, KD - 1, 5, 0.5)
                    h_low(1, KD - 1)
                    add_square(1, KD - 1, 1)
                if t == 1:
                    norm(1)
                    V.tensor_scalar(OMKA, par_all("k_a"), -1.0, 1.0, ALU.mult, ALU.add).then_inc(omka_ready, 1)
                if t == 11:
                    V.tensor_tensor(FAC[:, :, 0:NC - 1], HALF[:, :, 0:NC - 1], HALF[:, :, 1:NC], ALU.add)
                    V.tensor_tensor(tiles(LW0), tiles(D0), tiles(LW0), ALU.subtract).then_inc(cum_ready, 1)
                if t == 2:
                    factor(1, arena[:, RSW, :])
                    keep_proj(0)
                if t > 1:
                    keep_proj(t - 1)
                if 3 <= t < 17:
                    shift(t - 3)
                if t == 8:
                    dve.wait_ge(shifted, 6)
                    for c in range(4):
                        V.tensor_scalar(arena[:, KK0 + c, :], arena[:, KT + c, :], par_col("k_k", c), None,
                                        ALU.mult).then_inc(kk_raw, 1)
                if t == 9:
                    dve.wait_ge(z_kept, 4)
                    for c in range(4):
                        V.tensor_tensor_scan(arena[:, D0 + c, :], C("reset"), arena[:, LW0 + c, :], 0.0,
                                             ALU.mult, ALU.add).then_inc(scanned, 1)
                if t == 10:
                    cum = by_chunk(D0)
                    dve.wait_ge(scanned, 4)
                    link(V.tensor_scalar(HALF, cum[:, :, :, CH - 1], 0.5, None, ALU.mult))
                    link(V.tensor_tensor(cum, cum, HALF.unsqueeze(3).to_broadcast([P, NP, NC, CH]), ALU.subtract))
                    dve.wait_ge(ks_done, 1)
                    V.tensor_scalar(KS, ps[4][:, 0:32], 1e-24, None, ALU.max).then_inc(ks_ready, 1)
                    dve.wait_ge(ks_ready, 1)
                    dve.wait_ge(ks_root, 1)
                    inverse_root(KR, KS, KX, kr_ready)
                if t == 12:
                    for c in range(4):
                        dve.wait_ge(z_done, 8 + c + 1)
                        V.tensor_tensor(arena[:, KK0 + c, :], arena[:, KK0 + c, :], ps[4 + c][:, :],
                                        ALU.mult).then_inc(kk_ready, 1)
                if t == 14:
                    dve.wait_ge(ka_ready, 1)
                    dve.wait_ge(exps, 2)
                    V.scalar_tensor_tensor(tiles(KK0), tiles(KK0), -1.0, tiles(LW0), ALU.mult, ALU.mult).then_inc(early_a, 1)
                if t == 15:
                    dve.wait_ge(k_ready, 1)
                    dve.wait_ge(shifted, 10)
                    for c in range(4):
                        V.scalar_tensor_tensor(arena[:, BON0 + c, :], arena[:, RT + c, :], par_col("r_k", c),
                                               arena[:, KT + c, :], ALU.mult, ALU.mult).then_inc(rk_ready, 1)
                if t == 16:
                    for g in range(4):
                        dve.wait_ge(at_done, g + 1)
                        V.tensor_tensor(AT[:, 8 * g:8 * g + 8, :], ps[4 + g][:, :].rearrange("q (m c) -> q m c", c=CH),
                                        C("atmask").unsqueeze(1).to_broadcast([P, 8, CH]), ALU.mult).then_inc(at_kept, 1)
                if t == 18:
                    dve.wait_ge(blk_in, 16)
                    link(V.memset(TB, 0.0))
                    for e in range(2):
                        ins = V.memset(arena[:, X0 + 1, BLK * BLK * e:BLK * BLK * (e + 1):BLK + 1], 1.0)
                    link(ins)
                    substitute(1, 6)
                if t == 19:
                    substitute(6, 11)
            keep_proj(IN_TILES - 1)

            dve.wait_ge(w_used, FIRST_UNIT["wout"])
            dve.wait_ge(exps, 3)
            dve.wait_ge(shifted, 14)
            for half in range(2):
                ns = slice(NC // 2 * half, NC // 2 * (half + 1))
                V.tensor_tensor(BK[:, :, ns, CH:P], by_chunk(KT)[:, :, ns], by_chunk(E0)[:, :, ns], ALU.mult).then_inc(ops_dve, 1)
                V.tensor_tensor(AR[:, :, ns, CH:P], by_chunk(RT)[:, :, ns], by_chunk(D0)[:, :, ns], ALU.mult).then_inc(ops_dve, 1)
                for c in (2 * half, 2 * half + 1):
                    dve.wait_ge(z_done, 12 + c + 1)
                    V.tensor_tensor(arena[:, BON0 + c, :], ps[4 + c][:, :], arena[:, VT + c, :], ALU.mult).then_inc(z_kept, 1)
            dve.wait_ge(at_kept, 4)
            V.tensor_tensor(OFF, AT, C("offblock").unsqueeze(1).to_broadcast([P, 32, CH]), ALU.mult).then_inc(off_ready, 1)
            substitute(11, BLK)
            V.tensor_copy(TBT, TB.rearrange("q e t j -> q e j t")).then_inc(inv_ready, 1)
            for n in range(NC):
                dve.wait_ge(mm_done, n + 1)
                for e in range(2):
                    V.tensor_tensor(MM[:, n, e, :, :], ps[4 + 2 * (n % 2) + e][:, :].rearrange("q (p c) -> q p c", p=NP),
                                    C("mmask").unsqueeze(1).to_broadcast([P, NP, P]), ALU.mult).then_inc(mm_kept, 1)

            for g in range(4):
                dve.wait_ge(q_done, g + 1)
                V.tensor_copy(QQ[:, 8 * g:8 * g + 8, :], ps[g][:, :].rearrange("q (m c) -> q m c", c=CH)).then_inc(q_kept, 1)
            for it in range(NB - 1):
                for g in range(4):
                    dve.wait_ge(tt_done, 4 * it + g + 1)
                    V.tensor_tensor(TT[:, 8 * g:8 * g + 8, :], ps[4 * ((it + 1) % 2) + g][:, :].rearrange("q (m c) -> q m c", c=CH),
                                    DIT[:, 8 * g:8 * g + 8, :], ALU.add).then_inc(tt_kept, 1)

            def normalize(m):
                hs = slice(NP * (m % 2), NP * (m % 2) + NP)
                k0 = CH if m < 2 else 0
                dve.wait_ge(e_ready, m + 1)
                link(V.tensor_tensor(DEN[:, hs], DEN[:, hs], ESK[:, hs], ALU.add))
                link(V.reciprocal(DEN[:, hs], DEN[:, hs]))
                V.tensor_tensor(SC[:, hs, k0:192], SC[:, hs, k0:192],
                                DEN[:, hs].unsqueeze(2).to_broadcast([P, NP, 192 - k0]), ALU.mult).then_inc(p_ready, 1)

            def pt0_copy(m):
                if m >= 2:
                    dve.wait_ge(pt0_done, m - 1)
                    V.tensor_copy(PT0[0:CH, NP * (m % 2):NP * (m % 2) + NP, :],
                                  ps[6][0:CH, :].rearrange("q (h c) -> q h c", h=NP)).then_inc(pt_dve, 1)

            for n in range(NC):
                e = n % 2
                if n:
                    normalize(n - 1)
                dve.wait_ge(r_done, n + 1)
                V.tensor_copy(RS, ps[0][:, 0:NP * CH].rearrange("q (p c) -> q p c", p=NP)).then_inc(r_kept, 1)
                dve.wait_ge(u_done, n + 1)
                V.tensor_copy(UV[0:CH, n, :, 0:CH], ps[1][0:CH, 0:NP * CH].rearrange("q (p c) -> q p c", p=NP)).then_inc(u_dve, 1)
                if n:
                    pt0_copy(n - 1)
                if n < NC - 1:
                    dve.wait_ge(st_done, n + 1)
                    delta = ps[3][:, 0:NP * CH].rearrange("q (p c) -> q p c", p=NP)
                    new = ST[:, (n + 1) % 2]
                    if n:
                        link(V.tensor_tensor(new, delta, ST[:, n % 2], ALU.add))
                        delta = new
                    else:
                        dve.wait_ge(exps, 4)
                    V.tensor_tensor(new, delta, FAC[:, :, n:n + 1].to_broadcast([P, NP, CH]), ALU.mult).then_inc(st_kept, 1)
                hs = slice(NP * e, NP * e + NP)
                k0 = CH if n < 2 else 0
                for b in range(2):
                    dve.wait_ge(s_done, 2 * n + b + 1)
                    V.scalar_tensor_tensor(SC[:, NP * e + 2 * b:NP * e + 2 * b + 2, k0:192],
                                           ps[5 + b][:, 0:384].rearrange("q (h k) -> q h k", h=2)[:, :, k0:192], SCALE,
                                           C("winmask")[:, k0:192].unsqueeze(1).to_broadcast([P, 2, 192 - k0]),
                                           ALU.mult, ALU.add).then_inc(s_kept, 1)
                dve.wait_ge(s_kept, 2 * n + 2)
                link(V.tensor_reduce(MX[:, hs], SC[:, hs, k0:192], AX_X, ALU.max))
                link(V.tensor_tensor(MX[:, hs], MX[:, hs], SINK[:, hs], ALU.max))
                V.tensor_scalar(NMX[:, hs], MX[:, hs], -1.0, None, ALU.mult).then_inc(mx_ready, 1)
                V.tensor_tensor(ESK[:, hs], SINK[:, hs], MX[:, hs], ALU.subtract).then_inc(mx_ready, 1)
            normalize(NC - 1)
            pt0_copy(NC - 1)

            def mix_low(k):
                dve.wait_ge(mix_hi_done, k + 1)
                src = arena[:, QT + k, :] if k < 4 else arena[:, DI0 + k - 4, :]
                V.tensor_tensor(mix_lo[:, k, :], src, mix_hi[:, k, :].bitcast(F32), ALU.subtract).then_inc(mix_lo_done, 1)

            dve.wait_ge(o_done, NC)
            low("wout", 0, 0)
            for c in range(4):
                dve.wait_ge(gn_done, c + 1)
                V.scalar_tensor_tensor(arena[:, DI0 + c, :], ps[c][:, :], -1.0 / HD, arena[:, DI0 + c, :],
                                       ALU.mult, ALU.add).then_inc(gn_kept, 1)
            for k in range(4):
                mix_low(k)
            dve.wait_ge(ks_done, 2)
            V.tensor_scalar(KS, ps[0][:, 0:32], 1.0 / HD, GN_EPS, ALU.mult, ALU.add).then_inc(ks_ready, 1)
            low("wout", 0, 1)
            dve.wait_ge(ks_ready, 2)
            dve.wait_ge(ks_root, 2)
            inverse_root(KR, KS, KX, kr_ready)
            low("wout", 0, 2)
            wout_residual(0)
            low("wout", 0, 3)
            wout_residual(1)
            for c in range(4):
                y = arena[:, DI0 + c, :]
                dve.wait_ge(gn_done, 4 + c + 1)
                link(V.tensor_tensor(y, y, ps[c][:, :], ALU.mult))
                dve.wait_ge(tail_ready, 4)
                link(V.tensor_tensor(y, y, arena[:, G0 + c, :], ALU.mult))
                V.tensor_tensor(y, y, arena[:, BON0 + c, :], ALU.add).then_inc(mix_ready, 1)
            for k in range(4, KD):
                mix_low(k)
            low("wout", 1, 0)
            wout_residual(2)
            wout_residual(3)
            for j in range(1, NRAW):
                low("wout", 1, j)
                wout_residual(NRAW + j - 1)
            ffn(2, "up2", "down2", KF)
            residual("down2", 2 * KD, KD - 1, 5, 0.5)
            add_square(3, KD - 1, 1)
            norm(3)
            dve.wait_ge(factor_done, 4)
            for k in range(KD):
                V.scalar_tensor_tensor(x[:, k, :], x[:, k, :], par_col("gf", k), ps[7][:, :], ALU.mult, ALU.mult).then_inc(y_ready, 1)

        @block.tensor
        def _(pe):
            M = nc.tensor

            def product(bank, j, cols, hi, lo, start, stop):
                whi, wlo = w_hi[:, j % NHL, cols:cols + P], w_lo[:, j % NHL, cols:cols + P]
                M.matmul(ps[bank][:, :], whi, hi, start=start, stop=False)
                M.matmul(ps[bank][:, :], whi, lo, start=False, stop=False)
                return M.matmul(ps[bank][:, :], wlo, hi, start=False, stop=stop)

            def unit(name, i, j, bank, hi, lo, k0, nk, last_k, h_base=None):
                pe.wait_ge(lo_done, FIRST_UNIT[name] + NRAW * i + j + 1)
                for k in range(nk):
                    if h_base is not None:
                        pe.wait_ge(h_lo_done, h_base + k + 1)
                    ins = product(bank, j, k * P, hi[:, k0 + k, :], lo[:, k0 + k, :], k0 + k == 0, k0 + k == last_k)
                ins.then_inc(w_used, 1)

            def norm_sum(n):
                pe.wait_ge(acc_done, KD * (n + 1))
                if n == 0:
                    pe.wait_ge(const_ready, 32)
                for i in range(T // P):
                    ins = M.matmul(ps[7][:, i:i + 1], acc[:, P * i:P * i + P], C("ones")[:, 0:1], start=True, stop=True)
                ins.then_inc(sum_done, 1)

            def norm_factor(n):
                pe.wait_ge(root_done, n + 1)
                for i in range(T // P):
                    ins = M.matmul(ps[7][:, P * i:P * i + P], NR[:, i:i + 1].to_broadcast([P, P]), C("ident"),
                                   start=True, stop=True)
                ins.then_inc(factor_done, 1)

            def ffn(n, up, down, fbase):
                def up_body(i):
                    for j in range(NRAW):
                        if j % 2 == 0:
                            ge(pe, up_done, fbase + 2 * i + j // 2 - 1)
                        first = isinstance(i, int) and i == 0 and j == 0
                        unit(up, i, j, j, h_hi, h_lo, 0, KD, KD - 1, KD * n if first else None)
                        if first:
                            norm_sum(n)
                        if isinstance(i, int) and j == 1:
                            norm_factor(n)

                def down_body(i):
                    for j in range(NRAW):
                        if isinstance(i, int) and j < 2:
                            pe.wait_ge(hid_lo_done, fbase + KF // 2 * (j + 1))
                        if j % 2 == 0:
                            ge(pe, resid_done, RESID[n + 1] + 2 * i + j // 2 - 1)
                        unit(down, i, j, 4 + j // 2, hid_hi, hid_lo, KF // 2 * (j % 2), KF // 2, KF - 1)

                up_body(0)
                with pe.Fori(1, units(up)[1]) as i:
                    up_body(i)
                down_body(0)
                with pe.Fori(1, units(down)[1]) as i:
                    down_body(i)

            ffn(0, "up1", "down1", 0)

            def win_unit(i, j):
                ge(pe, proj, NRAW * i + j - 3)
                first = isinstance(i, int) and i == 0 and j == 0
                unit("win", i, j, j, h_hi, h_lo, 0, KD, KD - 1, KD if first else None)
                if first:
                    norm_sum(1)
                if isinstance(i, int) and (i, j) == (0, 1):
                    norm_factor(1)

            def win_body(i):
                for j in range(NRAW):
                    win_unit(i, j)

            def head_sums(src, bank):
                for i in range(T // P):
                    for p in range(NP):
                        c = NH * i + 2 * p
                        ins = M.matmul(ps[bank][:, c:c + 2], src[:, p, P * i:P * i + P], C("headones")[:, 0:P:CH],
                                       start=True, stop=True)
                ins.then_inc(ks_done, 1)

            def heads_first(bank):
                for i in range(T // P):
                    ins = M.transpose(ps[bank][0:NH, P * i:P * i + P], KR[:, NH * i:NH * i + NH], C("ident"))
                ins.then_inc(krt_done, 1)

            def spread_heads(bank, select, values, done):
                for p in range(NP):
                    M.matmul(ps[bank + p][:, :], arena[0:NH, select, P * p:P * p + P], arena[0:NH, values, :],
                             start=True, stop=True).then_inc(done, 1)

            win_body(0)
            win_body(1)
            pe.wait_ge(lora_w, 32)
            pe.wait_ge(lora_act, 1)
            for c in range(4):
                M.matmul(ps[4 + c][:, :], w2_t[:, c * P:c * P + P], WD, start=True, stop=True).then_inc(z_done, 1)
            win_unit(2, 0)
            for c in range(4):
                pe.wait_ge(z_kept, c + 1)
                M.matmul(ps[4 + c][:, :], a2_t[:, c * P:c * P + P], AD, start=True, stop=True).then_inc(z_done, 1)
            win_unit(2, 1)
            pe.wait_ge(kk_sq, 1)
            pe.wait_ge(z_kept, 5)
            head_sums(tiles(E0), 4)
            win_unit(2, 2)
            pe.wait_ge(kr_ready, 1)
            pe.wait_ge(z_kept, 8)
            heads_first(7)
            win_unit(2, 3)
            pe.wait_ge(krt_kept, 1)
            pe.wait_ge(select_in, 16)
            spread_heads(4, SELECT0, KRT0, z_done)
            win_unit(3, 0)
            win_unit(3, 1)
            win_unit(3, 2)
            win_unit(3, 3)
            pe.wait_ge(early_b, 1)
            pe.wait_ge(early_a, 1)
            for g in range(4):
                for n in (2 * g, 2 * g + 1):
                    for p in range(NP):
                        for e in range(2):
                            r, m = CH * e, (n % 2 * NP + p) * CH
                            ins = M.matmul(ps[4 + g][r:r + CH, m:m + CH], arena[r:r + CH, A0 + p, CH * n:CH * n + CH],
                                           arena[r:r + CH, KK0 + p, CH * n:CH * n + CH], start=True, stop=True)
                ins.then_inc(at_done, 1)
            win_body(4)
            pe.wait_ge(at_kept, 4)
            for c in range(4):
                pe.wait_ge(rk_ready, c + 1)
                M.matmul(ps[4 + c][:, :], C("headones"), arena[:, BON0 + c, :], start=True, stop=True).then_inc(z_done, 1)

            pe.wait_ge(proj, IN_TILES)
            for i in range(T // P):
                ins = M.transpose(ps[0][:, P * i:P * i + P], arena[:, AV, P * i:P * i + P], C("ident"))
            ins.then_inc(vt_done, 1)
            for i in range(1, T // P):
                ins = M.transpose(ps[1][0:CH, P * (i - 1):P * i], arena[:, AV, P * i - CH:P * i], C("ident"))
            ins.then_inc(vt_done, 1)

            for n in range(NC):
                if n % (NC // 2) == 0:
                    pe.wait_ge(ops_act, 2 if n == 0 else 4)
                    pe.wait_ge(ops_dve, 2 if n == 0 else 4)
                if n < 2:
                    pe.wait_ge(z_kept, 10 + 2 * n)
                    pe.wait_ge(vt_kept, n + 1)
                ge(pe, mm_kept, 2 * (n - 1))
                for p in range(NP):
                    for e in range(2):
                        r = CH * e
                        ins = M.matmul(ps[4 + 2 * (n % 2) + e][:, p * P:p * P + P], BK[r:r + CH, p, n, :],
                                       AR[r:r + CH, p, n, :], start=True, stop=True)
                ins.then_inc(mm_done, 1)
                ge(pe, bt_kept, n - 3)
                for p in range(NP):
                    ins = M.transpose(ps[n % 4][:, p * P:p * P + P], BK[:, p, n, :], C("ident"))
                ins.then_inc(bt_done, 1)

            pe.wait_ge(off_ready, 1)
            pe.wait_ge(inv_in, 16 * 4 * NB)
            pe.wait_ge(bt_kept, NC)

            def by_matrix(bank, g, lhs, rhs, done):
                for m in range(8 * g, 8 * g + 8):
                    for e in range(2):
                        r = CH * e
                        ins = M.matmul(ps[bank][r:r + CH, m % 8 * CH:m % 8 * CH + CH], lhs[r:r + CH, m, :], rhs[r:r + CH, m, :],
                                       start=True, stop=True)
                ins.then_inc(done, 1)

            for g in range(4):
                by_matrix(g, g, OFF, DI, q_done)
            for it in range(NB - 1):
                for g in range(4):
                    if it == 0:
                        pe.wait_ge(mm_kept, min(2 * NC, 2 * NC - 2 + g // 2 * 2))
                    pe.wait_ge(q_kept, g + 1)
                    if it:
                        pe.wait_ge(tt_kept, 4 * (it - 1) + g + 1)
                    by_matrix(4 * ((it + 1) % 2) + g, g, QQ, TT if it else DIT, tt_done)

            for n in range(NC):
                pe.wait_ge(v_kept, n - 3) if n >= 4 else pe.wait_ge(tt_kept, 4 + n + 1)
                for p in range(NP):
                    ins = M.transpose(ps[n % 4][0:CH, p * P:p * P + P], arena[:, VT + p, CH * n:CH * n + CH], C("ident"))
                ins.then_inc(v_done, 1)
            pe.wait_ge(g2_in, 16)
            pe.wait_ge(tt_kept, 12)
            for c in range(4):
                M.matmul(ps[4 + c][:, :], g2_t[:, c * P:c * P + P], GD, start=True, stop=True).then_inc(g_done, 1)

            def scores(m):
                i, r = m // 2, CH * (m % 2)
                k0 = CH if i == 0 else 0
                ge(pe, pt_act, m)
                ge(pe, pt_dve, m - 2)
                for b in range(2):
                    for p in (2 * b, 2 * b + 1):
                        c = p % 2 * 192
                        ins = M.matmul(ps[5 + b][:, c + k0:c + 192], arena[r:r + CH, QT + p, P * i:P * i + P],
                                       arena[r:r + CH, AK, P * i - CH + k0:P * i + P], start=True, stop=True)
                    ins.then_inc(s_done, 1)

            def transpose_own(m):
                pe.wait_ge(p_ready, m + 1)
                for p in range(NP):
                    ins = M.transpose(ps[5][:, p * P:p * P + P], SC[:, NP * (m % 2) + p, CH:192], C("ident"))
                ins.then_inc(pt_done, 1)

            def transpose_before(m):
                if m >= 2:
                    for p in range(NP):
                        ins = M.transpose(ps[6][0:CH, p * P:p * P + P], SC[:, NP * (m % 2) + p, 0:CH], C("ident"))
                    ins.then_inc(pt0_done, 1)

            def attend(m):
                i, e = m // 2, m % 2
                pe.wait_ge(pt_act, m + 1)
                ge(pe, pt_dve, m - 1)
                ge(pe, o_kept, m)
                for p in range(NP):
                    o = ps[7][CH * e:CH * e + CH, p * P:p * P + P]
                    ins = M.matmul(o, VA[:, i, CH * e:CH * e + CH], PT1[:, NP * e + p, :], start=True, stop=i == 0)
                    if i:
                        ins = M.matmul(o, VB[0:CH, i - 1, CH * e:CH * e + CH], PT0[0:CH, NP * e + p, :],
                                       start=False, stop=True)
                ins.then_inc(o_done, 1)

            def quadrants():
                return [(p, e, CH * e) for p in range(NP) for e in range(2)]

            pe.wait_ge(v_kept, NC)
            pe.wait_ge(zeroed, 3)
            pe.wait_ge(g_kept, 4)
            pe.wait_ge(roped, 5)
            for n in range(NC):
                ge(pe, r_kept, n)
                for p, e, r in quadrants():
                    ins = M.matmul(ps[0][r:r + CH, p * CH:p * CH + CH], MM[:, n, e, p, 0:CH], UV[:, n, p, r:r + CH],
                                   start=p == 0, stop=n == 0 and p == NP - 1)
                if n:
                    pe.wait_ge(st_kept, n)
                    for p, e, r in quadrants():
                        ins = M.matmul(ps[0][r:r + CH, p * CH:p * CH + CH], AR[r:r + CH, p, n, 0:CH], ST[r:r + CH, n % 2, p, :],
                                       start=False, stop=p == NP - 1)
                ins.then_inc(r_done, 1)
                if n:
                    transpose_own(n - 1)
                pe.wait_ge(r_kept, n + 1)
                for p, e, r in quadrants():
                    ins = M.matmul(ps[1 + e][0:CH, p * CH:p * CH + CH], TT[r:r + CH, n * NP + p, :], RS[r:r + CH, p, :],
                                   start=True, stop=True)
                ins.then_inc(u_done, 1)
                if n:
                    transpose_before(n - 1)
                pe.wait_ge(u_dve, n + 1)
                pe.wait_ge(u_act, n + 1)
                if n < NC - 1:
                    for p, e, r in quadrants():
                        ins = M.matmul(ps[3][r:r + CH, p * CH:p * CH + CH], BT[:, n, p, r:r + CH], UV[:, n, p, r:r + CH],
                                       start=True, stop=True)
                    ins.then_inc(st_done, 1)
                scores(n)
                if n:
                    attend(n - 1)
                ge(pe, y_kept, n)
                for p, e, r in quadrants():
                    o = ps[4][r:r + CH, p * CH:p * CH + CH]
                    ins = M.matmul(o, UV[:, n, p, r:r + CH], MM[:, n, e, p, CH:P], start=True, stop=n == 0)
                    if n:
                        ins = M.matmul(o, ST[r:r + CH, n % 2, p, :], AR[r:r + CH, p, n, CH:P], start=False, stop=True)
                ins.then_inc(y_done, 1)
            transpose_own(NC - 1)
            transpose_before(NC - 1)
            attend(NC - 1)

            def wout_unit(u):
                half = u // NRAW
                pe.wait_ge(lo_done, FIRST_UNIT["wout"] + u + 1)
                if u >= 2:
                    pe.wait_ge(resid_done, KD + 2 * (u - 1))
                for e in range(2):
                    for k in range(4):
                        ins = product(4 + 2 * (u % 2) + e, u, (4 * e + k) * P, mix_hi[:, 4 * half + k, :],
                                      mix_lo[:, 4 * half + k, :], k == 0, k == 3)
                ins.then_inc(w_used, 1)

            pe.wait_ge(y_kept, NC)
            for c in range(4):
                M.matmul(ps[c][:, :], C("headones"), arena[:, DI0 + c, :], start=True, stop=True).then_inc(gn_done, 1)
            pe.wait_ge(gn_sq, 1)
            head_sums(GN_SQ, 0)
            pe.wait_ge(mix_lo_done, 4)
            wout_unit(0)
            pe.wait_ge(kr_ready, 2)
            heads_first(3)
            wout_unit(1)
            pe.wait_ge(krt_kept, 2)
            pe.wait_ge(select_in, 32)
            spread_heads(0, SELECT1, KRT1, gn_done)
            for u in range(2, NRAW):
                wout_unit(u)
            pe.wait_ge(mix_lo_done, KD)
            for u in range(NRAW, 2 * NRAW):
                wout_unit(u)
            ffn(2, "up2", "down2", KF)
            norm_sum(3)
            norm_factor(3)


def unit_layout(wt, nk):
    k, n = wt.shape
    return np.ascontiguousarray(
        wt.reshape(k // (nk * P), nk, P, n // P, P).transpose(3, 0, 2, 1, 4).reshape(-1, P, nk * P))


def columns(v):
    return v.reshape(-1, P).T


def kernel(**inputs):
    import concourse.bacc as _bacc
    from concourse.bass_utils import run_bass_kernel_spmd as _run

    g = {k: np.asarray(v) for k, v in inputs.items()}
    nq, nkv = NH * HD, 2 * HD
    r0 = nq + 2 * nkv
    w_in, w_out = g["w_in"], g["w_out"]
    heads = np.arange(NH).reshape(2, NP).T.ravel()
    q_cols = (heads[:, None] * HD + np.arange(HD)[None, :]).ravel()
    lo = r0 + 3 * nq
    rw = np.concatenate([np.arange(lo + 64, lo + 160), np.arange(lo, lo + 32), np.arange(lo + 32, lo + 64),
                         np.arange(lo + 64, lo + 160), np.arange(r0 + nq, r0 + 2 * nq), np.arange(r0, r0 + nq),
                         np.arange(r0 + 2 * nq, r0 + 3 * nq)])
    cols = np.concatenate([rw, np.arange(nq, nq + nkv), np.arange(nq + nkv, r0), q_cols])
    rows = np.concatenate([q_cols, np.arange(nq, 2 * nq)])

    def up_units(a, b):
        return np.ascontiguousarray(np.stack([unit_layout(a, KD), unit_layout(b, KD)], 1).reshape(2 * KF, P, UP_UNIT))

    parts = {"g1": g["ffn1_norm"], "gm": g["mix_norm"], "g2": g["ffn2_norm"], "gf": g["final_norm"],
             "mu": g["rwkv_shift_mu"][rw - r0], "w0": g["rwkv_w0"], "a0": g["rwkv_a0"], "k_k": g["rwkv_k_k"],
             "k_a": g["rwkv_k_a"], "r_k": g["rwkv_r_k"].reshape(-1), "ln_w": g["rwkv_ln_w"], "ln_b": g["rwkv_ln_b"]}
    arrays = {
        "xT": np.ascontiguousarray(g["x"].reshape(T, KD, P).transpose(2, 1, 0)),
        "up1": up_units(g["ffn1_w_gate"], g["ffn1_w_up"]), "down1": unit_layout(g["ffn1_w_down"], KF // 2),
        "win": unit_layout(w_in[:, cols], KD), "wout": np.concatenate([unit_layout(w_out[rows[h:h + nq]], KD // 2).reshape(KD // 2, 2, P, UP_UNIT // 2)
                                .transpose(0, 2, 1, 3).reshape(KD // 2, P, UP_UNIT) for h in (0, nq)]),
        "up2": up_units(g["ffn2_w_gate"], g["ffn2_w_up"]), "down2": unit_layout(g["ffn2_w_down"], KF // 2),
        "params": np.ascontiguousarray(np.concatenate([columns(parts[n]) for n in PARAMS], 1)),
        "sinks": g["attn_sinks"], "w2": g["rwkv_w2"], "a2": g["rwkv_a2"], "g2": g["rwkv_g2"], "const": constants(),
        "selection": head_selection(),
    }
    nc = _bacc.Bacc("TRN2", target_bir_lowering=False, num_devices=1)
    d = {n: nc.dram_tensor(n, a.shape, F32, kind="ExternalInput").ap() for n, a in arrays.items()}
    out = nc.dram_tensor("out", (P, KD, T), F32, kind="ExternalOutput").ap()
    scratch = [nc.dram_tensor(n, (P, 2, BLK, BLK), F32, kind="Internal").ap() for n in ("blocks", "inverses", "inverses_t")]
    build(nc, d["xT"], {n: d[n] for n, _, _ in PHASES}, d["params"], d["sinks"], d["w2"], d["a2"], d["g2"], d["const"],
          d["selection"], *scratch, out)
    r = _run(nc, [arrays], core_ids=[0])
    return r.results[0]["out"].transpose(2, 1, 0).reshape(1, T, D)
```

```python
from contextlib import ExitStack

import numpy as np
import concourse.bass as bass
from concourse import mybir

P = 128
D = 1024
T = 512
FF = 2816
HD = 64
NH = 8
KD = D // P
KF = FF // P
CH = 64
NC = T // CH
NP = 4
BLK = 16
NB = CH // BLK
IN_TILES = 20
UP_UNIT = KD * P
DOWN_UNIT = KF // 2 * P
NORM_EPS = 1e-5
GN_EPS = 64e-5
KAPPA = float(np.exp(-0.5))
SCALE = HD ** -0.5
NEG = -1e30

ALU = mybir.AluOpType
ACT = mybir.ActivationFunctionType
AX_X = mybir.AxisListType.X
F32 = mybir.dt.float32
F32R = mybir.dt.float32r

LORA, KT, RT, VT, AK, AV, QT = 0, 2, 6, 10, 14, 15, 16
G0, LW0, A0, KK0, D0, E0, BON0, X0 = 20, 24, 28, 32, 36, 40, 44, 48
ARENA = 52
M0 = LW0
BT0 = KT
TT0 = E0
DI0 = X0
DIT0 = G0
RSW = G0 + 2
DIFF0 = QT + 2
SELECT0, KRT0 = QT + 1, QT
SELECT1, KRT1 = LORA, KT
GATE_BANK = [4, 5, 6, 7]
PT_BANKS = [(5, 6)] * (NC - 1) + [(4, 0)]
O_BANKS = [7] * (NC - 1) + [6]
CHUNKS = [2, 3, 4, 5, 6, 7, 0, 1]
SWAP_Q = [G0, G0 + 1, G0 + 3, G0]

PARAMS = {}
_at = 0
for _name, _n in [("g1", 8), ("gm", 8), ("g2", 8), ("gf", 8), ("mu", 14), ("w0", 4), ("a0", 4), ("k_k", 4),
                  ("k_a", 4), ("r_k", 4), ("ln_w", 4), ("ln_b", 4)]:
    PARAMS[_name] = (_at, _n)
    _at += _n
NPARAM = _at

CONST = {}
_at = 0
for _name, _n in [("cos", T), ("sin", T), ("reset", T), ("ident", P), ("ones", P), ("headones", P), ("mmask", P),
                  ("atmask", CH), ("offblock", CH), ("winmask", 192), ("eps", 4)]:
    CONST[_name] = (_at, _n)
    _at += _n
NCONST = _at

PHASES = [("up1", 2 * KF, UP_UNIT), ("down1", 2 * KD, DOWN_UNIT), ("win", IN_TILES, UP_UNIT),
          ("wout", KD, UP_UNIT), ("up2", 2 * KF, UP_UNIT), ("down2", 2 * KD, DOWN_UNIT)]
FIRST_UNIT = {}
_at = 0
for _name, _n, _ in PHASES:
    FIRST_UNIT[_name] = _at
    _at += _n
NRAW = 4
NHL = 2
RESID = {1: 0, 2: 2 * KD, 3: 3 * KD}
GAIN = ("g1", "gm", "g2")


def constants():
    c = np.zeros((P, NCONST), np.float32)

    def put(name, v):
        c[:, CONST[name][0]:CONST[name][0] + CONST[name][1]] = v

    half = HD // 2
    inv = np.float32(10000.0) ** (-np.arange(0, HD, 2, dtype=np.float32) / np.float32(HD))
    ang = np.arange(T, dtype=np.float32)[:, None] * inv[None, :].astype(np.float32)
    row = np.arange(P)
    put("cos", np.cos(ang).T[row % half])
    put("sin", np.sin(ang).T[row % half] * np.where(row % HD < half, -1.0, 1.0)[:, None])
    put("reset", (np.arange(T) % CH != 0)[None, :])
    put("ident", np.eye(P))
    put("ones", 1.0)
    put("headones", row[:, None] // HD == row[None, :] // HD)
    s, t = row[:, None] % CH, np.arange(CH)[None, :]
    put("mmask", np.concatenate([s < t, s <= t], 1))
    put("atmask", s < t)
    put("offblock", s // BLK != t // BLK)
    key = np.arange(192)[None, :]
    put("winmask", np.where((key >= CH * (row[:, None] // CH)) & (key < CH * (row[:, None] // CH) + 2 * CH), 0.0, NEG))
    c[:, CONST["eps"][0]] = NORM_EPS
    c[:, CONST["eps"][0] + 1] = GN_EPS
    return c


def head_selection():
    return (np.arange(NH)[:, None] == np.arange(NH * HD)[None, :] // HD).astype(np.float32)


def build(nc, xT, w, params, sinks, w2, a2, g2, const, selection, blocks_dram, inv_dram, invt_dram, out):
    ctx = ExitStack()
    with ctx:
        def keep(name, shape, dt=F32):
            return ctx.enter_context(nc.sbuf_tensor(name, shape, dt))

        def sem(name):
            return ctx.enter_context(nc.semaphore(name))

        x = keep("x", [P, KD, T])
        raw = keep("raw", [P, NRAW, DOWN_UNIT])
        par = keep("par", [P, NPARAM])
        cst = keep("cst", [P, NCONST])
        small = keep("small", [P, 220])

        def overlay(*layouts):
            made = []
            for n, layout in enumerate(layouts):
                scope = ExitStack()
                made += [(ctx if n == len(layouts) - 1 else scope).enter_context(nc.sbuf_tensor(*t)) for t in layout]
                if n < len(layouts) - 1:
                    scope.close()
            return made

        h_hi, h_lo, armain = overlay(
            [("h_hi", [P, KD, T], F32R), ("h_lo", [P, KD, T], F32R)],
            [("chunk_ops", [P, 2 * KD, T], F32)])
        w_hi, w_lo, side = overlay(
            [("w_hi", [P, NHL, DOWN_UNIT], F32R), ("w_lo", [P, NHL, DOWN_UNIT], F32R)],
            [("side", [P, 11, T], F32)])
        hid_hi, hid_lo, sil, tmp, acc, rs, nt, _, mix_hi, mix_lo, arena = overlay(
            [("hid_hi", [P, KF, T], F32R), ("hid_lo", [P, KF, T], F32R), ("sil", [P, 2, T], F32),
             ("tmp", [P, 2, T], F32), ("acc", [P, T], F32), ("rs", [P, T], F32), ("nt", [P, T], F32)],
            [("before_mix", [P, M0, T], F32), ("mix_hi", [P, KD, T], F32R), ("mix_lo", [P, KD, T], F32R)],
            [("arena", [P, ARENA, T], F32)])
        ps = [ctx.enter_context(nc.psum_tensor(f"ps{i}", [P, T], F32)) for i in range(8)]

        def C(name, rows=P):
            a, n = CONST[name]
            return cst[0:rows, a:a + n]

        def par_col(name, i, lo=0, hi=P):
            return par[lo:hi, PARAMS[name][0] + i:PARAMS[name][0] + i + 1]

        def par_at(name, i):
            a, n = PARAMS[name]
            return par[:, a:a + n][:, i:i + 1] if isinstance(i, int) else par[:, bass.ds(i + a, 1)]

        def par_all(name):
            a, n = PARAMS[name]
            return par[:, a:a + n]

        def tiles(first, n=4):
            return arena[:, first:first + n, :]

        def by_chunk(first):
            return tiles(first).rearrange("q p (n c) -> q p n c", c=CH)

        AR = armain[:, 0:8, :].rearrange("q a b -> q (a b)").rearrange("q (p n c) -> q p n c", p=NP, n=NC)
        BK = armain[:, 8:16, :].rearrange("q a b -> q (a b)").rearrange("q (p n c) -> q p n c", p=NP, n=NC)
        OFF = side[:, 7:11, :].rearrange("q a b -> q (a b)").rearrange("q (m c) -> q m c", c=CH)
        QQ = side[:, 3:7, :].rearrange("q a b -> q (a b)").rearrange("q (m c) -> q m c", c=CH)
        UV = armain[:, 8:16, :].rearrange("q a b -> q (a b)").rearrange("q (n p c) -> q n p c", n=NC, p=NP)
        MM = tiles(M0, 16).rearrange("q a b -> q (a b)").rearrange("q (n e p c) -> q n e p c", n=NC, e=2, p=NP)
        BT = tiles(BT0, 8).rearrange("q a b -> q (a b)").rearrange("q (n p c) -> q n p c", n=NC, p=NP)
        def mats(first):
            return tiles(first).rearrange("q a b -> q (a b)").rearrange("q (m c) -> q m c", c=CH)

        AT = mats(LW0)
        TT = mats(TT0)
        DI, DIT = mats(DI0), mats(DIT0)
        Y = tiles(DI0)
        SC = side[:, 0:3, :].rearrange("q a b -> q (a b)").rearrange("q (h k) -> q h k", h=NH)
        PT1 = side[:, 3:5, :].rearrange("q a b -> q (a b)").rearrange("q (h k) -> q h k", h=NH)
        PT0 = side[:, 5:7, :].rearrange("q a b -> q (a b)").rearrange("q (h k) -> q h k", h=NH)
        AB = arena[:, X0, :].rearrange("q (e s t) -> q e s t", e=2, s=BLK)
        TB = arena[:, X0 + 1, :].rearrange("q (e t j) -> q e t j", e=2, t=BLK)
        TBT = arena[:, X0 + 2, :].rearrange("q (e j t) -> q e j t", e=2, j=BLK)
        PROD = arena[:, X0 + 3, :]
        RS = side[:, 7, 0:256].rearrange("q (p c) -> q p c", p=NP)
        ST = side[:, 8, :].rearrange("q (b p c) -> q b p c", b=2, p=NP)
        VA = arena[:, LORA + 1, :].rearrange("q (i c) -> q i c", c=P)
        VB = arena[:, AV, :].rearrange("q (i c) -> q i c", c=P)
        HALF = small[:, 0:32].rearrange("q (p n) -> q p n", p=NP)
        FAC = small[:, 32:64].rearrange("q (p n) -> q p n", p=NP)
        MX, NMX, DEN, ESK = (small[:, 64 + 8 * i:72 + 8 * i] for i in range(4))
        OMKA = small[:, 96:100]
        SINK = small[:, 104:112]
        KS, KR, KX = (small[:, 112 + 32 * i:144 + 32 * i] for i in range(3))
        MS, NR, NX = (small[:, 208 + 4 * i:212 + 4 * i] for i in range(3))
        GN_SQ = armain[:, 0:4, :]
        GD = arena[0:96, LORA, :]
        WD = arena[96:128, LORA, :]
        AD = arena[0:32, LORA + 1, :]
        w2_t, a2_t, g2_t = arena[96:128, G0, :], arena[0:32, G0 + 1, :], side[0:96, 9, :]

        raw_ready = [sem(f"raw_ready{j}") for j in range(NRAW)]
        hi_done = sem("hi_done")
        lo_done = sem("lo_done")
        w_used = sem("w_used")
        x_ready = [sem(f"x_ready{k}") for k in range(KD)]
        par_ready = sem("par_ready")
        const_ready = sem("const_ready")
        sq_done = sem("sq_done")
        acc_done = sem("acc_done")
        sum_done = sem("sum_done")
        ms_done = sem("ms_done")
        ms_root = sem("ms_root")
        root_done = sem("root_done")
        factor_done = sem("factor_done")
        y_ready = sem("y_ready")
        h_hi_done = sem("h_hi_done")
        h_lo_done = sem("h_lo_done")
        gate_done = sem("gate_done")
        silu_done = sem("silu_done")
        up_done = sem("up_done")
        hid_done = sem("hid_done")
        hid_hi_done = sem("hid_hi_done")
        hid_lo_done = sem("hid_lo_done")
        resid_done = sem("resid_done")
        dve_own = sem("dve_own")
        out_done = sem("out_done")
        proj = sem("proj")
        lora_w = sem("lora_w")
        diffed = sem("diffed")
        shifted = sem("shifted")
        lora_act = sem("lora_act")
        z_done = sem("z_done")
        z_kept = sem("z_kept")
        omka_ready = sem("omka_ready")
        kk_raw = sem("kk_raw")
        kk_sq = sem("kk_sq")
        ks_done = sem("ks_done")
        ks_ready = sem("ks_ready")
        ks_root = sem("ks_root")
        kr_ready = sem("kr_ready")
        krt_done, krt_kept = sem("krt_done"), sem("krt_kept")
        select_in = sem("select_in")
        kk_ready = sem("kk_ready")
        k_ready = sem("k_ready")
        rk_ready = sem("rk_ready")
        scanned = sem("scanned")
        cum_ready = sem("cum_ready")
        exps = sem("exps")
        ka_ready = sem("ka_ready")
        early_b, early_a = sem("early_b"), sem("early_a")
        ops_act = sem("ops_act")
        ops_dve = sem("ops_dve")
        swap_in = [sem(f"swap_in{n}") for n in range(5)]
        rope_own = sem("rope_own")
        roped = sem("roped")
        zeroed = sem("zeroed")
        at_done, at_kept = sem("at_done"), sem("at_kept")
        mm_done, mm_kept = sem("mm_done"), sem("mm_kept")
        bt_done, bt_kept = sem("bt_done"), sem("bt_kept")
        vt_done, vt_kept = sem("vt_done"), sem("vt_kept")
        blk_out, blk_in = sem("blk_out"), sem("blk_in")
        inv_ready = sem("inv_ready")
        inv_out, inv_in = sem("inv_out"), sem("inv_in")
        s_done, s_kept = sem("s_done"), sem("s_kept")
        mx_ready = sem("mx_ready")
        e_ready = sem("e_ready")
        p_ready = sem("p_ready")
        pt_done = sem("pt_done")
        pt0_done = sem("pt0_done")
        pt_act, pt_dve = sem("pt_act"), sem("pt_dve")
        o_done, o_kept = sem("o_done"), sem("o_kept")
        off_ready = sem("off_ready")
        q_done, q_kept = sem("q_done"), sem("q_kept")
        tt_done, tt_kept = sem("tt_done"), sem("tt_kept")
        v_done, v_kept = sem("v_done"), sem("v_kept")
        g2_in = sem("g2_in")
        g_done, g_kept = sem("g_done"), sem("g_kept")
        r_done, r_kept = sem("r_done"), sem("r_kept")
        u_done, u_dve, u_act = sem("u_done"), sem("u_dve"), sem("u_act")
        st_done, st_kept = sem("st_done"), sem("st_kept")
        y_done, y_kept = sem("y_done"), sem("y_kept")
        gn_done = sem("gn_done")
        gn_kept = sem("gn_kept")
        gn_sq = sem("gn_sq")
        tail_ready = sem("tail_ready")
        gated = sem("gated")
        mix_ready = sem("mix_ready")
        mix_hi_done = sem("mix_hi_done")
        mix_lo_done = sem("mix_lo_done")

        def ge(eng, s, v):
            if not (isinstance(v, int) and v <= 0):
                eng.wait_ge(s, v)

        def units(name):
            return FIRST_UNIT[name], dict((n, k) for n, k, _ in PHASES)[name] // NRAW

        block = ctx.enter_context(nc.Block())

        @block.sync
        def _(sp):
            sp.dma_start(par[:, :], params).then_inc(par_ready, 16)

            def load(name, i, j):
                n = dict((a, c) for a, _, c in PHASES)[name]
                ge(sp, lo_done, FIRST_UNIT[name] + NRAW * i + j + 1 - NRAW)
                sp.dma_start(raw[:, j, 0:n], w[name][NRAW * i + j]).then_inc(raw_ready[j], 16)

            def load_all(name, first=0):
                with sp.Fori(first, units(name)[1]) as i:
                    for j in range(NRAW):
                        load(name, i, j)

            for k in range(KD):
                sp.dma_start(x[:, k, :], xT[:, k, :]).then_inc(x_ready[k], 16)
                if k < NRAW:
                    load("up1", 0, k)
            sp.dma_start(cst[:, :], const).then_inc(const_ready, 16)
            sp.dma_start(SINK, sinks.partition_broadcast(P)).then_inc(const_ready, 16)
            load_all("up1", 1)
            load_all("down1")
            load("win", 0, 0)
            load("win", 0, 1)
            load("win", 0, 2)
            load("win", 0, 3)
            sp.wait_ge(w_used, FIRST_UNIT["win"])
            sp.dma_start(w2_t, w2).then_inc(lora_w, 16)
            sp.dma_start(a2_t, a2).then_inc(lora_w, 16)
            sp.dma_start(arena[0:NH, SELECT0, :], selection).then_inc(select_in, 16)
            with sp.Fori(1, 4) as i:
                for j in range(NRAW):
                    load("win", i, j)
            load("win", 4, 0)
            load("win", 4, 1)
            load("win", 4, 2)
            load("win", 4, 3)
            sp.wait_ge(at_kept, 4)
            for e in range(2):
                for b in range(NB):
                    r = CH * e + BLK * b
                    sp.dma_start(blocks_dram[32 * b:32 * b + 32, e].rearrange("m s t -> s m t"),
                                 AT[r:r + BLK, :, BLK * b:BLK * b + BLK]).then_inc(blk_out, 16)
            sp.wait_ge(blk_out, 16 * 2 * NB)
            sp.wait_ge(k_ready, 1)
            sp.dma_start(AB, blocks_dram).then_inc(blk_in, 16)

            def swap(n, src, dst):
                for a in range(4):
                    b = a ^ 1
                    sp.dma_start(arena[32 * a:32 * a + 32, dst, :],
                                 arena[32 * b:32 * b + 32, src, :]).then_inc(swap_in[n], 16)

            sp.wait_ge(z_done, 8)
            sp.wait_ge(proj, AK + 1)
            swap(0, AK, LORA + 1)
            for i in range(3):
                sp.wait_ge(proj, QT + i + 1)
                swap(i + 1, QT + i, SWAP_Q[i])
            sp.wait_ge(proj, QT + 4)
            sp.wait_ge(roped, 2)
            swap(4, QT + 3, SWAP_Q[3])
            sp.wait_ge(inv_ready, 1)
            sp.dma_start(inv_dram, TB).then_inc(inv_out, 16)
            sp.dma_start(invt_dram, TBT).then_inc(inv_out, 16)
            sp.wait_ge(inv_out, 32)
            sp.wait_ge(zeroed, 2)
            for e in range(2):
                for b in range(NB):
                    r = CH * e + BLK * b
                    for dst, src in ((DI, inv_dram), (DIT, invt_dram)):
                        sp.dma_start(dst[r:r + BLK, :, BLK * b:BLK * b + BLK],
                                     src[32 * b:32 * b + 32, e].rearrange("m t j -> t m j")).then_inc(inv_in, 16)
            for j in range(NRAW):
                load("wout", 0, j)
            sp.wait_ge(q_done, 4)
            sp.dma_start(g2_t, g2).then_inc(g2_in, 16)
            sp.wait_ge(g_done, 4)
            sp.dma_start(arena[0:NH, SELECT1, :], selection).then_inc(select_in, 16)
            load_all("wout", 1)
            load_all("up2")
            load_all("down2")
            for k in range(KD):
                sp.wait_ge(y_ready, k + 1)
                sp.dma_start(out[:, k, :], x[:, k, :]).then_inc(out_done, 16)
            sp.wait_ge(out_done, 16 * KD)

        @block.gpsimd
        def _(pool):
            own = [0]

            def link(ins):
                own[0] += 1
                ins.then_inc(rope_own, 1)
                pool.wait_ge(rope_own, own[0])

            def diff(t):
                pool.wait_ge(proj, t + 1)
                ge(pool, shifted, t - 1)
                d, p = arena[:, DIFF0 + t % 2, :], arena[:, t, :]
                link(nc.gpsimd.tensor_tensor(d[:, 1:T], p[:, 0:T - 1], p[:, 1:T], ALU.subtract))
                nc.gpsimd.tensor_scalar(d[:, 0:1], p[:, 0:1], -1.0, None, ALU.mult).then_inc(diffed, 1)

            for t in range(8):
                diff(t)
            pool.wait_ge(z_kept, 8)
            pool.wait_ge(omka_ready, 1)
            for c in range(4):
                ins = nc.gpsimd.tensor_scalar(arena[:, X0 + c, :], arena[:, A0 + c, :], par_col("k_a", c),
                                              OMKA[:, c:c + 1], ALU.mult, ALU.add)
            link(ins)
            diff(8)
            pool.wait_ge(kk_raw, 4)
            nc.gpsimd.tensor_tensor(tiles(KT), tiles(KT), tiles(X0), ALU.mult).then_inc(k_ready, 1)
            diff(9)
            diff(10)
            diff(11)
            pool.wait_ge(exps, 1)
            pool.wait_ge(ka_ready, 1)
            nc.gpsimd.tensor_tensor(tiles(A0), tiles(A0), tiles(E0), ALU.mult).then_inc(early_b, 1)
            for t in range(12, 14):
                diff(t)
            pool.wait_ge(const_ready, 32)
            for n, (x_t, s_t) in enumerate([(AK, LORA + 1)] + [(QT + i, SWAP_Q[i]) for i in range(4)]):
                pool.wait_ge(swap_in[n], 64)
                link(nc.gpsimd.tensor_tensor(arena[:, x_t, :], arena[:, x_t, :], C("cos"), ALU.mult))
                link(nc.gpsimd.tensor_tensor(arena[:, s_t, :], arena[:, s_t, :], C("sin"), ALU.mult))
                nc.gpsimd.tensor_tensor(arena[:, x_t, :], arena[:, x_t, :], arena[:, s_t, :], ALU.add).then_inc(roped, 1)
            pool.wait_ge(inv_out, 32)
            nc.gpsimd.memset(tiles(DI0), 0.0).then_inc(zeroed, 1)
            pool.wait_ge(roped, 5)
            nc.gpsimd.memset(tiles(DIT0), 0.0).then_inc(zeroed, 1)
            pool.wait_ge(bt_done, NC)
            pool.wait_ge(mm_done, NC)
            nc.gpsimd.memset(UV[0:CH, :, :, :], 0.0).then_inc(zeroed, 1)
            pool.wait_ge(z_kept, 12)
            pool.wait_ge(g_kept, 4)
            for c in range(4):
                ins = nc.gpsimd.tensor_scalar(arena[:, BON0 + c, :], arena[:, BON0 + c, :], par_col("ln_b", c), None, ALU.add)
            link(ins)
            link(nc.gpsimd.tensor_tensor(tiles(BON0), tiles(BON0), tiles(G0), ALU.mult))
            for c in range(4):
                nc.gpsimd.tensor_scalar(arena[:, G0 + c, :], arena[:, G0 + c, :], par_col("ln_w", c), None,
                                        ALU.mult).then_inc(tail_ready, 1)
            pool.wait_ge(gn_sq, 4)
            pool.wait_ge(tail_ready, 4)
            nc.gpsimd.tensor_tensor(Y, Y, tiles(G0), ALU.mult).then_inc(gated, 1)

        @block.scalar
        def _(act):
            A = nc.scalar

            def split(name, i, j):
                n = dict((a, c) for a, _, c in PHASES)[name]
                u = FIRST_UNIT[name] + NRAW * i + j
                act.wait_ge(raw_ready[j], 16 * (FIRST_UNIT[name] // NRAW + i + 1))
                ge(act, w_used, u + 1 - NHL)
                A.activation(w_hi[:, j % NHL, 0:n], raw[:, j, 0:n], ACT.Copy).then_inc(hi_done, 1)

            def silu(fbase, f, slot):
                act.wait_ge(gate_done, fbase + f + 1)
                A.activation(sil[:, slot, :], sil[:, slot, :], ACT.Silu).then_inc(silu_done, 1)

            def hid_high(fbase, f, slot):
                act.wait_ge(hid_done, fbase + f + 1)
                A.activation(hid_hi[:, f, :], tmp[:, slot, :], ACT.Copy).then_inc(hid_hi_done, 1)

            def square(n, d, slot):
                if n == 0:
                    act.wait_ge(x_ready[d], 16)
                else:
                    act.wait_ge(resid_done, RESID[n] + d + 1)
                ge(act, acc_done, KD * n + d - 1)
                if n < 3:
                    A.activation(h_hi[:, d, :], x[:, d, :], ACT.Copy, scale=par_at(GAIN[n], d)).then_inc(h_hi_done, 1)
                first = isinstance(d, int) and d == 0
                A.activation(acc[:, :] if first else sil[:, slot, :], x[:, d, :], ACT.Square).then_inc(sq_done, 1)

            def root(n):
                act.wait_ge(ms_done, n + 1)
                A.activation(NR, MS, ACT.Sqrt).then_inc(ms_root, 1)

            def krt_copy(n, bank, dst):
                act.wait_ge(krt_done, n + 1)
                A.activation(arena[0:NH, dst, :], bank[0:NH, :], ACT.Copy).then_inc(krt_kept, 1)

            def ffn(n, up, down, fbase):
                def up_body(i):
                    first = isinstance(i, int) and i == 0
                    if not (first and n == 0):
                        split(up, i, 0)
                    if first:
                        if n == 2:
                            square(2, KD - 2, 0)
                            square(2, KD - 1, 1)
                    else:
                        silu(fbase, 2 * i - 1, 1)
                    if not (first and n == 0):
                        split(up, i, 1)
                    if first:
                        root(n)
                    else:
                        hid_high(fbase, 2 * i - 1, 1)
                    split(up, i, 2)
                    silu(fbase, 2 * i, 0)
                    split(up, i, 3)
                    hid_high(fbase, 2 * i, 0)

                def down_body(i):
                    first = isinstance(i, int) and i == 0
                    split(down, i, 0)
                    if first:
                        silu(fbase, KF - 1, 1)
                    split(down, i, 1)
                    if first:
                        hid_high(fbase, KF - 1, 1)
                    else:
                        square(n + 1, 2 * i - 1, 1)
                    split(down, i, 2)
                    split(down, i, 3)
                    square(n + 1, 2 * i, 0)

                up_body(0)
                with act.Fori(1, units(up)[1]) as i:
                    up_body(i)
                down_body(0)
                with act.Fori(1, units(down)[1]) as i:
                    down_body(i)

            act.wait_ge(par_ready, 16)
            for d in range(KD):
                square(0, d, d % 2)
                if d in (0, 3):
                    split("up1", 0, d // 3)
            ffn(0, "up1", "down1", 0)

            for t in range(IN_TILES):
                split("win", t // NRAW, t % NRAW)
                if t == 0:
                    square(1, KD - 1, 1)
                if t == 1:
                    root(1)
                if t == 6:
                    act.wait_ge(shifted, 2)
                    A.activation(WD, WD, ACT.Tanh).then_inc(lora_act, 1)
                    A.activation(GD, GD, ACT.Sigmoid).then_inc(lora_act, 1)
                if t == 9:
                    for c in range(4):
                        act.wait_ge(z_done, c + 1)
                        A.activation(arena[:, LW0 + c, :], ps[4 + c][:, :], ACT.Sigmoid,
                                     bias=par_col("w0", c)).then_inc(z_kept, 1)
                    act.wait_ge(kk_raw, 4)
                    A.activation(tiles(E0), tiles(KK0), ACT.Square).then_inc(kk_sq, 1)
                    for c in range(4):
                        act.wait_ge(z_done, 4 + c + 1)
                        A.activation(arena[:, A0 + c, :], ps[4 + c][:, :], ACT.Sigmoid,
                                     bias=par_col("a0", c)).then_inc(z_kept, 1)
                if t == 10:
                    act.wait_ge(ks_ready, 1)
                    A.activation(KR, KS, ACT.Sqrt).then_inc(ks_root, 1)
                if t == 11:
                    krt_copy(0, ps[7], KRT0)
                    act.wait_ge(cum_ready, 1)
                    A.activation(tiles(E0), tiles(D0), ACT.Exp, scale=KAPPA).then_inc(exps, 1)
                    A.activation(tiles(LW0), tiles(LW0), ACT.Exp, scale=-KAPPA).then_inc(exps, 1)
                if t == 12:
                    A.activation(tiles(D0), tiles(D0), ACT.Exp, scale=-KAPPA).then_inc(exps, 1)
                    A.activation(FAC[:, :, 0:NC - 1], FAC[:, :, 0:NC - 1], ACT.Exp, scale=-KAPPA).then_inc(exps, 1)

            act.wait_ge(w_used, FIRST_UNIT["wout"])
            act.wait_ge(early_b, 1)
            act.wait_ge(early_a, 1)
            for half in range(2):
                ns = slice(NC // 2 * half, NC // 2 * (half + 1))
                A.activation(BK[:, :, ns, 0:CH], by_chunk(A0)[:, :, ns], ACT.Copy).then_inc(ops_act, 1)
                A.activation(AR[:, :, ns, 0:CH], by_chunk(KK0)[:, :, ns], ACT.Copy).then_inc(ops_act, 1)

            act.wait_ge(vt_done, 2)
            act.wait_ge(roped, 1)
            A.activation(VA[:, :, :], ps[0][:, :].rearrange("q (i c) -> q i c", c=P), ACT.Copy).then_inc(vt_kept, 1)
            A.activation(VB[0:CH, 0:3, :], ps[1][0:CH, 0:3 * P].rearrange("q (i c) -> q i c", c=P),
                         ACT.Copy).then_inc(vt_kept, 1)
            act.wait_ge(ops_dve, 4)
            act.wait_ge(rk_ready, 4)
            for m, n in enumerate(CHUNKS):
                act.wait_ge(bt_done, m + 1)
                A.activation(BT[:, n, :, :], ps[4 + m % 4][:, :].rearrange("q (p c) -> q p c", p=NP), ACT.Copy).then_inc(bt_kept, 1)
            def v_copy(n):
                act.wait_ge(v_done, n + 1)
                A.activation(UV[CH:P, n, :, :], ps[6 + n % 2][0:CH, :].rearrange("q (p c) -> q p c", p=NP),
                             ACT.Copy).then_inc(v_kept, 1)

            act.wait_ge(mm_done, NC)
            for n in range(NC - 1):
                v_copy(n)

            def y_copy(n):
                act.wait_ge(y_done, n + 1)
                A.activation(Y[:, :, CH * n:CH * n + CH], ps[4][:, 0:NP * CH].rearrange("q (p c) -> q p c", p=NP),
                             ACT.Copy).then_inc(y_kept, 1)

            def gate_copy(c):
                act.wait_ge(g_done, c + 1)
                A.activation(arena[:, G0 + c, :], ps[GATE_BANK[c]][:, :], ACT.Copy).then_inc(g_kept, 1)

            def pt_copy(m):
                i, e = m // 2, m % 2
                act.wait_ge(pt_done, m + 1)
                A.activation(PT1[:, 4 * e:4 * e + 4, :], ps[PT_BANKS[m][0]][:, :].rearrange("q (h c) -> q h c", h=4),
                             ACT.Copy).then_inc(pt_act, 1)

            def o_copy(m):
                i, e = m // 2, m % 2
                act.wait_ge(o_done, m + 1)
                r = CH * e
                A.activation(arena[r:r + CH, QT:QT + 4, P * i:P * i + P],
                             ps[O_BANKS[m]][r:r + CH, :].rearrange("q (p c) -> q p c", p=NP), ACT.Copy).then_inc(o_kept, 1)

            def exponentials(m):
                k0 = CH if m < 2 else 0
                hs = range(NP * (m % 2), NP * (m % 2) + NP)
                act.wait_ge(mx_ready, 2 * m + 2)
                for h in hs:
                    A.activation(SC[:, h, k0:192], SC[:, h, k0:192], ACT.Exp, bias=NMX[:, h:h + 1],
                                 accum_out=DEN[:, h:h + 1])
                A.activation(ESK[:, hs[0]:hs[0] + NP], ESK[:, hs[0]:hs[0] + NP], ACT.Exp).then_inc(e_ready, 1)

            def mix_high_attention(t0, t1):
                A.activation(mix_hi[:, 0:4, t0:t1], arena[:, QT:QT + 4, t0:t1], ACT.Copy).then_inc(mix_hi_done, 1)

            act.wait_ge(tt_kept, 12)
            gate_copy(0)
            gate_copy(1)
            for n in range(NC):
                act.wait_ge(u_done, n + 1)
                A.activation(UV[0:CH, n, :, CH:P], ps[2][0:CH, 0:NP * CH].rearrange("q (p c) -> q p c", p=NP),
                             ACT.Copy).then_inc(u_act, 1)
                if n < 2:
                    gate_copy(2 + n)
                if n == 0:
                    v_copy(NC - 1)
                if n >= 2:
                    pt_copy(n - 2)
                if n:
                    exponentials(n - 1)
                if n == NC - 2:
                    act.wait_ge(y_done, 4)
                    act.wait_ge(o_kept, NC // 2)
                    mix_high_attention(0, T // 2)
                if n == NC - 1:
                    y_copy(n)
                if n >= 2:
                    o_copy(n - 2)
                if n < NC - 1:
                    y_copy(n)
            exponentials(NC - 1)
            pt_copy(NC - 2)
            for c in range(4):
                act.wait_ge(gn_kept, c + 1)
                A.activation(GN_SQ[:, c, :], arena[:, DI0 + c, :], ACT.Square).then_inc(gn_sq, 1)
                if c == 1:
                    pt_copy(NC - 1)
                    o_copy(NC - 2)
            act.wait_ge(pt0_done, NC - 2)
            split("wout", 0, 0)
            o_copy(NC - 1)

            act.wait_ge(o_kept, NC)
            mix_high_attention(T // 2, T)
            split("wout", 0, 1)
            act.wait_ge(ks_ready, 2)
            A.activation(KR, KS, ACT.Sqrt).then_inc(ks_root, 1)
            split("wout", 0, 2)
            krt_copy(1, ps[3], KRT1)
            split("wout", 0, 3)
            for c in range(4):
                act.wait_ge(mix_ready, c + 1)
                A.activation(mix_hi[:, 4 + c, :], arena[:, DI0 + c, :], ACT.Copy).then_inc(mix_hi_done, 1)

            split("wout", 1, 0)
            for j in range(1, NRAW):
                split("wout", 1, j)
                square(2, 2 * j - 2, 0)
                square(2, 2 * j - 1, 1)
            ffn(2, "up2", "down2", KF)
            act.wait_ge(root_done, 3)
            A.activation(small[:, 101:102], MS[:, 0:1], ACT.Sqrt)
            square(3, KD - 1, 1)
            root(3)

        @block.vector
        def _(dve):
            V = nc.vector
            own = [0]

            def link(ins):
                own[0] += 1
                ins.then_inc(dve_own, 1)
                dve.wait_ge(dve_own, own[0])

            def low(name, i, j):
                n = dict((a, c) for a, _, c in PHASES)[name]
                dve.wait_ge(hi_done, FIRST_UNIT[name] + NRAW * i + j + 1)
                V.tensor_tensor(w_lo[:, j % NHL, 0:n], raw[:, j, 0:n], w_hi[:, j % NHL, 0:n].bitcast(F32),
                                ALU.subtract).then_inc(lo_done, 1)

            def hidden(fbase, f, slot):
                dve.wait_ge(w_used, FIRST_UNIT["up1" if fbase == 0 else "up2"] + 2 * f + 2)
                ge(dve, hid_lo_done, fbase + f - 1)
                V.tensor_tensor(tmp[:, slot, :], ps[2 * slot + 1][:, :], rs[:, :], ALU.mult).then_inc(up_done, 1)
                dve.wait_ge(up_done, fbase + f + 1)
                dve.wait_ge(silu_done, fbase + f + 1)
                V.tensor_tensor(tmp[:, slot, :], tmp[:, slot, :], sil[:, slot, :], ALU.mult).then_inc(hid_done, 1)

            def gate(fbase, f, slot):
                dve.wait_ge(w_used, FIRST_UNIT["up1" if fbase == 0 else "up2"] + 2 * f + 1)
                ge(dve, hid_done, fbase + f - 1)
                V.tensor_tensor(sil[:, slot, :], ps[2 * slot][:, :], rs[:, :], ALU.mult).then_inc(gate_done, 1)

            def hid_low(fbase, f, slot):
                dve.wait_ge(hid_hi_done, fbase + f + 1)
                V.tensor_tensor(hid_lo[:, f, :], tmp[:, slot, :], hid_hi[:, f, :].bitcast(F32),
                                ALU.subtract).then_inc(hid_lo_done, 1)

            def residual(name, used, d, bank, scale):
                dve.wait_ge(w_used, FIRST_UNIT[name] + used)
                V.scalar_tensor_tensor(x[:, d, :], ps[bank][:, :], scale, x[:, d, :], ALU.mult, ALU.add).then_inc(resid_done, 1)

            def add_square(n, d, slot):
                dve.wait_ge(sq_done, KD * n + d + 1)
                if isinstance(d, int) and d == 0:
                    V.tensor_copy(small[:, 100:101], acc[:, 0:1]).then_inc(acc_done, 1)
                else:
                    dve.wait_ge(acc_done, KD * n + d)
                    V.tensor_tensor(acc[:, :], acc[:, :], sil[:, slot, :], ALU.add).then_inc(acc_done, 1)

            def inverse_root(y, xx, t, done):
                link(V.reciprocal(y, y))
                link(V.tensor_tensor(t, xx, y, ALU.mult))
                link(V.scalar_tensor_tensor(t, t, -0.5, y, ALU.mult, ALU.mult))
                V.scalar_tensor_tensor(y, t, 1.5, y, ALU.add, ALU.mult).then_inc(done, 1)

            def norm(n):
                dve.wait_ge(sum_done, n + 1)
                V.tensor_scalar(MS, ps[7][:, 0:T // P], 1.0 / D, NORM_EPS, ALU.mult, ALU.add).then_inc(ms_done, 1)
                dve.wait_ge(ms_done, n + 1)
                dve.wait_ge(ms_root, n + 1)
                inverse_root(NR, MS, NX, root_done)

            def factor(n, dst):
                dve.wait_ge(factor_done, n + 1)
                link(V.tensor_copy(dst, ps[7][:, :]))

            def h_low(n, d):
                dve.wait_ge(h_hi_done, KD * n + d + 1)
                V.scalar_tensor_tensor(h_lo[:, d, :], x[:, d, :], par_at(GAIN[n], d), h_hi[:, d, :].bitcast(F32),
                                       ALU.mult, ALU.subtract).then_inc(h_lo_done, 1)

            def wout_residual(u):
                for e in range(2):
                    residual("wout", u + 1, 2 * (u % NRAW) + e, 4 + 2 * (u % 2) + e, 1.0)
                if u >= NRAW:
                    for e in range(2):
                        h_low(2, 2 * (u - NRAW) + e)
                        add_square(2, 2 * (u - NRAW) + e, e)

            def ffn(n, up, down, fbase):
                def up_body(i):
                    first = isinstance(i, int) and i == 0
                    if not (first and n == 0):
                        low(up, i, 0)
                    if first:
                        if n == 2:
                            wout_residual(KD - 1)
                    else:
                        hidden(fbase, 2 * i - 1, 1)
                    if not (first and n == 0):
                        low(up, i, 1)
                    if first:
                        norm(n)
                    else:
                        hid_low(fbase, 2 * i - 1, 1)
                    low(up, i, 2)
                    if first:
                        factor(n, rs[:, :])
                    gate(fbase, 2 * i, 0)
                    hidden(fbase, 2 * i, 0)
                    low(up, i, 3)
                    gate(fbase, 2 * i + 1, 1)
                    hid_low(fbase, 2 * i, 0)

                def down_body(i):
                    first = isinstance(i, int) and i == 0
                    low(down, i, 0)
                    if first:
                        hidden(fbase, KF - 1, 1)
                    else:
                        residual(down, 4 * i, 2 * i - 1, 5, 0.5)
                        if n == 0:
                            h_low(1, 2 * i - 1)
                    low(down, i, 1)
                    if first:
                        hid_low(fbase, KF - 1, 1)
                    else:
                        add_square(n + 1, 2 * i - 1, 1)
                    low(down, i, 2)
                    residual(down, 4 * i + 2, 2 * i, 4, 0.5)
                    low(down, i, 3)
                    if n == 0:
                        h_low(1, 2 * i)
                    add_square(n + 1, 2 * i, 0)

                up_body(0)
                with dve.Fori(1, units(up)[1]) as i:
                    up_body(i)
                down_body(0)
                with dve.Fori(1, units(down)[1]) as i:
                    down_body(i)

            dve.wait_ge(par_ready, 16)
            for d in range(KD):
                h_low(0, d)
                if d in (0, 3):
                    low("up1", 0, d // 3)
                add_square(0, d, d % 2)
            ffn(0, "up1", "down1", 0)

            def shift(t):
                dve.wait_ge(diffed, t + 1)
                p = arena[:, t, :]
                V.scalar_tensor_tensor(p, arena[:, DIFF0 + t % 2, :], par_col("mu", t), p, ALU.mult,
                                       ALU.add).then_inc(shifted, 1)

            def keep_proj(t):
                dve.wait_ge(w_used, FIRST_UNIT["win"] + t + 1)
                V.tensor_tensor(arena[:, t, :], ps[t % 4][:, :], arena[:, RSW, :], ALU.mult).then_inc(proj, 1)

            def substitute(first, last):
                for t in range(first, last):
                    prod = PROD[:, 0:2 * t * t].rearrange("q (e j s) -> q e j s", e=2, j=t)
                    link(V.tensor_tensor(prod, TB[:, :, 0:t, 0:t].rearrange("q e s j -> q e j s"),
                                         AB[:, :, 0:t, t].unsqueeze(2).to_broadcast([P, 2, t, t]), ALU.mult))
                    link(V.tensor_reduce(TB[:, :, t, 0:t], prod, AX_X, ALU.add))

            for t in range(IN_TILES):
                low("win", t // NRAW, t % NRAW)
                if t == 0:
                    residual("down1", 2 * KD, KD - 1, 5, 0.5)
                    h_low(1, KD - 1)
                    add_square(1, KD - 1, 1)
                if t == 1:
                    norm(1)
                    V.tensor_scalar(OMKA, par_all("k_a"), -1.0, 1.0, ALU.mult, ALU.add).then_inc(omka_ready, 1)
                if t == 11:
                    V.tensor_tensor(FAC[:, :, 0:NC - 1], HALF[:, :, 0:NC - 1], HALF[:, :, 1:NC], ALU.add)
                    V.tensor_tensor(tiles(LW0), tiles(D0), tiles(LW0), ALU.subtract).then_inc(cum_ready, 1)
                if t == 13:
                    dve.wait_ge(kk_ready, 4)
                    dve.wait_ge(k_ready, 1)
                    V.tensor_tensor(tiles(A0), tiles(KK0), tiles(A0), ALU.mult).then_inc(ka_ready, 1)
                if t == 2:
                    factor(1, arena[:, RSW, :])
                    keep_proj(0)
                if t > 1:
                    keep_proj(t - 1)
                if 3 <= t < 17:
                    shift(t - 3)
                if t == 8:
                    dve.wait_ge(shifted, 6)
                    for c in range(4):
                        V.tensor_scalar(arena[:, KK0 + c, :], arena[:, KT + c, :], par_col("k_k", c), None,
                                        ALU.mult).then_inc(kk_raw, 1)
                if t == 9:
                    dve.wait_ge(z_kept, 4)
                    for c in range(4):
                        V.tensor_tensor_scan(arena[:, D0 + c, :], C("reset"), arena[:, LW0 + c, :], 0.0,
                                             ALU.mult, ALU.add).then_inc(scanned, 1)
                if t == 10:
                    cum = by_chunk(D0)
                    dve.wait_ge(scanned, 4)
                    link(V.tensor_scalar(HALF, cum[:, :, :, CH - 1], 0.5, None, ALU.mult))
                    link(V.tensor_tensor(cum, cum, HALF.unsqueeze(3).to_broadcast([P, NP, NC, CH]), ALU.subtract))
                    dve.wait_ge(ks_done, 1)
                    V.tensor_scalar(KS, ps[4][:, 0:32], 1e-24, None, ALU.max).then_inc(ks_ready, 1)
                    dve.wait_ge(ks_ready, 1)
                    dve.wait_ge(ks_root, 1)
                    inverse_root(KR, KS, KX, kr_ready)
                if t == 12:
                    for c in range(4):
                        dve.wait_ge(z_done, 8 + c + 1)
                        V.tensor_tensor(arena[:, KK0 + c, :], arena[:, KK0 + c, :], ps[4 + c][:, :],
                                        ALU.mult).then_inc(kk_ready, 1)
                if t == 13:
                    dve.wait_ge(ka_ready, 1)
                    dve.wait_ge(exps, 2)
                    V.scalar_tensor_tensor(tiles(KK0), tiles(KK0), -1.0, tiles(LW0), ALU.mult, ALU.mult).then_inc(early_a, 1)
                if t == 16:
                    dve.wait_ge(shifted, 10)
                    for c in range(4):
                        V.scalar_tensor_tensor(arena[:, BON0 + c, :], arena[:, RT + c, :], par_col("r_k", c),
                                               arena[:, KT + c, :], ALU.mult, ALU.mult).then_inc(rk_ready, 1)
                if t in (14, 15):
                    for g in (2 * (t - 14), 2 * (t - 14) + 1):
                        dve.wait_ge(at_done, g + 1)
                        V.tensor_tensor(AT[:, 8 * g:8 * g + 8, :], ps[4 + g][:, :].rearrange("q (m c) -> q m c", c=CH),
                                        C("atmask").unsqueeze(1).to_broadcast([P, 8, CH]), ALU.mult).then_inc(at_kept, 1)
                if t == 17:
                    dve.wait_ge(blk_in, 16)
                    link(V.memset(TB, 0.0))
                    for e in range(2):
                        ins = V.memset(arena[:, X0 + 1, BLK * BLK * e:BLK * BLK * (e + 1):BLK + 1], 1.0)
                    link(ins)
                    substitute(1, 8)
                if t == 18:
                    substitute(8, 12)
                if t == 19:
                    substitute(12, BLK)
                    V.tensor_copy(TBT, TB.rearrange("q e t j -> q e j t")).then_inc(inv_ready, 1)
            keep_proj(IN_TILES - 1)

            dve.wait_ge(w_used, FIRST_UNIT["wout"])
            dve.wait_ge(exps, 3)
            dve.wait_ge(shifted, 14)
            for half in range(2):
                ns = slice(NC // 2 * half, NC // 2 * (half + 1))
                V.tensor_tensor(BK[:, :, ns, CH:P], by_chunk(KT)[:, :, ns], by_chunk(E0)[:, :, ns], ALU.mult).then_inc(ops_dve, 1)
                V.tensor_tensor(AR[:, :, ns, CH:P], by_chunk(RT)[:, :, ns], by_chunk(D0)[:, :, ns], ALU.mult).then_inc(ops_dve, 1)
                for c in (2 * half, 2 * half + 1):
                    dve.wait_ge(z_done, 12 + c + 1)
                    V.tensor_tensor(arena[:, BON0 + c, :], ps[4 + c][:, :], arena[:, VT + c, :], ALU.mult).then_inc(z_kept, 1)
            dve.wait_ge(ops_act, 4)
            dve.wait_ge(ops_dve, 4)
            for m, n in enumerate(CHUNKS):
                if m == 4:
                    dve.wait_ge(at_kept, 4)
                    V.tensor_tensor(OFF, AT, C("offblock").unsqueeze(1).to_broadcast([P, 32, CH]), ALU.mult).then_inc(off_ready, 1)
                    dve.wait_ge(off_ready, 1)
                dve.wait_ge(mm_done, m + 1)
                for e in range(2):
                    V.tensor_tensor(MM[:, n, e, :, :], ps[2 * (m % 2) + e][:, :].rearrange("q (p c) -> q p c", p=NP),
                                    C("mmask").unsqueeze(1).to_broadcast([P, NP, P]), ALU.mult).then_inc(mm_kept, 1)

            for g in range(4):
                dve.wait_ge(q_done, g + 1)
                V.tensor_copy(QQ[:, 8 * g:8 * g + 8, :], ps[g][:, :].rearrange("q (m c) -> q m c", c=CH)).then_inc(q_kept, 1)
            for k in range(4, 4 * NB):
                g = k % 4
                dve.wait_ge(tt_done, k - 3)
                V.tensor_tensor(TT[:, 8 * g:8 * g + 8, :], ps[k % 6][:, :].rearrange("q (m c) -> q m c", c=CH),
                                DIT[:, 8 * g:8 * g + 8, :], ALU.add).then_inc(tt_kept, 1)

            def normalize(m):
                hs = slice(NP * (m % 2), NP * (m % 2) + NP)
                k0 = CH if m < 2 else 0
                dve.wait_ge(e_ready, m + 1)
                link(V.tensor_tensor(DEN[:, hs], DEN[:, hs], ESK[:, hs], ALU.add))
                link(V.reciprocal(DEN[:, hs], DEN[:, hs]))
                V.tensor_tensor(SC[:, hs, k0:192], SC[:, hs, k0:192],
                                DEN[:, hs].unsqueeze(2).to_broadcast([P, NP, 192 - k0]), ALU.mult).then_inc(p_ready, 1)

            def mix_low_attention(part, t0, t1):
                dve.wait_ge(mix_hi_done, part)
                V.tensor_tensor(mix_lo[:, 0:4, t0:t1], arena[:, QT:QT + 4, t0:t1], mix_hi[:, 0:4, t0:t1].bitcast(F32),
                                ALU.subtract).then_inc(mix_lo_done, 1)

            def pt0_copy(m):
                if m >= 2:
                    dve.wait_ge(pt0_done, m - 1)
                    V.tensor_copy(PT0[0:CH, NP * (m % 2):NP * (m % 2) + NP, :],
                                  ps[PT_BANKS[m][1]][0:CH, :].rearrange("q (h c) -> q h c", h=NP)).then_inc(pt_dve, 1)

            for n in range(NC):
                e = n % 2
                dve.wait_ge(r_done, n + 1)
                V.tensor_copy(RS, ps[0][:, 0:NP * CH].rearrange("q (p c) -> q p c", p=NP)).then_inc(r_kept, 1)
                dve.wait_ge(u_done, n + 1)
                V.tensor_copy(UV[0:CH, n, :, 0:CH], ps[1][0:CH, 0:NP * CH].rearrange("q (p c) -> q p c", p=NP)).then_inc(u_dve, 1)
                if n >= 2:
                    pt0_copy(n - 2)
                if n == NC - 1:
                    mix_low_attention(1, 0, T // 2)
                else:
                    dve.wait_ge(st_done, n + 1)
                    delta = ps[3][:, 0:NP * CH].rearrange("q (p c) -> q p c", p=NP)
                    new = ST[:, (n + 1) % 2]
                    if n:
                        link(V.tensor_tensor(new, delta, ST[:, n % 2], ALU.add))
                        delta = new
                    else:
                        dve.wait_ge(exps, 4)
                    V.tensor_tensor(new, delta, FAC[:, :, n:n + 1].to_broadcast([P, NP, CH]), ALU.mult).then_inc(st_kept, 1)
                hs = slice(NP * e, NP * e + NP)
                k0 = CH if n < 2 else 0
                for b in range(2):
                    dve.wait_ge(s_done, 2 * n + b + 1)
                    V.scalar_tensor_tensor(SC[:, NP * e + 2 * b:NP * e + 2 * b + 2, k0:192],
                                           ps[5 + b][:, 0:384].rearrange("q (h k) -> q h k", h=2)[:, :, k0:192], SCALE,
                                           C("winmask")[:, k0:192].unsqueeze(1).to_broadcast([P, 2, 192 - k0]),
                                           ALU.mult, ALU.add).then_inc(s_kept, 1)
                dve.wait_ge(s_kept, 2 * n + 2)
                link(V.tensor_reduce(MX[:, hs], SC[:, hs, k0:192], AX_X, ALU.max))
                link(V.tensor_tensor(MX[:, hs], MX[:, hs], SINK[:, hs], ALU.max))
                V.tensor_scalar(NMX[:, hs], MX[:, hs], -1.0, None, ALU.mult).then_inc(mx_ready, 1)
                V.tensor_tensor(ESK[:, hs], SINK[:, hs], MX[:, hs], ALU.subtract).then_inc(mx_ready, 1)
                if n:
                    normalize(n - 1)
            def center(c):
                dve.wait_ge(gn_done, c + 1)
                V.scalar_tensor_tensor(arena[:, DI0 + c, :], ps[c][:, :], -1.0 / HD, arena[:, DI0 + c, :],
                                       ALU.mult, ALU.add).then_inc(gn_kept, 1)

            center(0)
            normalize(NC - 1)
            center(1)
            pt0_copy(NC - 2)
            center(2)
            pt0_copy(NC - 1)
            center(3)
            dve.wait_ge(o_done, NC)
            low("wout", 0, 0)
            mix_low_attention(2, T // 2, T)
            dve.wait_ge(ks_done, 2)
            V.tensor_scalar(KS, ps[1][:, 0:32], 1.0 / HD, GN_EPS, ALU.mult, ALU.add).then_inc(ks_ready, 1)
            low("wout", 0, 1)
            dve.wait_ge(ks_ready, 2)
            dve.wait_ge(ks_root, 2)
            inverse_root(KR, KS, KX, kr_ready)
            low("wout", 0, 2)
            wout_residual(0)
            low("wout", 0, 3)
            wout_residual(1)
            for c in range(4):
                y = arena[:, DI0 + c, :]
                dve.wait_ge(gn_done, 4 + c + 1)
                dve.wait_ge(gated, 1)
                link(V.tensor_tensor(y, y, ps[c][:, :], ALU.mult))
                V.tensor_tensor(y, y, arena[:, BON0 + c, :], ALU.add).then_inc(mix_ready, 1)
            for c in range(4):
                dve.wait_ge(mix_hi_done, 3 + c)
                V.tensor_tensor(mix_lo[:, 4 + c, :], arena[:, DI0 + c, :], mix_hi[:, 4 + c, :].bitcast(F32),
                                ALU.subtract).then_inc(mix_lo_done, 1)
            low("wout", 1, 0)
            wout_residual(2)
            wout_residual(3)
            for j in range(1, NRAW):
                low("wout", 1, j)
                wout_residual(NRAW + j - 1)
            ffn(2, "up2", "down2", KF)
            residual("down2", 2 * KD, KD - 1, 5, 0.5)
            add_square(3, KD - 1, 1)
            norm(3)
            dve.wait_ge(factor_done, 4)
            for k in range(KD):
                V.scalar_tensor_tensor(x[:, k, :], x[:, k, :], par_col("gf", k), ps[7][:, :], ALU.mult, ALU.mult).then_inc(y_ready, 1)

        @block.tensor
        def _(pe):
            M = nc.tensor

            def product(bank, j, cols, hi, lo, start, stop):
                whi, wlo = w_hi[:, j % NHL, cols:cols + P], w_lo[:, j % NHL, cols:cols + P]
                M.matmul(ps[bank][:, :], whi, hi, start=start, stop=False)
                M.matmul(ps[bank][:, :], whi, lo, start=False, stop=False)
                return M.matmul(ps[bank][:, :], wlo, hi, start=False, stop=stop)

            def unit(name, i, j, bank, hi, lo, k0, nk, last_k, h_base=None):
                pe.wait_ge(lo_done, FIRST_UNIT[name] + NRAW * i + j + 1)
                for k in range(nk):
                    if h_base is not None:
                        pe.wait_ge(h_lo_done, h_base + k + 1)
                    ins = product(bank, j, k * P, hi[:, k0 + k, :], lo[:, k0 + k, :], k0 + k == 0, k0 + k == last_k)
                ins.then_inc(w_used, 1)

            def norm_sum(n):
                pe.wait_ge(acc_done, KD * (n + 1))
                if n == 0:
                    pe.wait_ge(const_ready, 32)
                for i in range(T // P):
                    ins = M.matmul(ps[7][:, i:i + 1], acc[:, P * i:P * i + P], C("ones")[:, 0:1], start=True, stop=True)
                ins.then_inc(sum_done, 1)

            def norm_factor(n):
                pe.wait_ge(root_done, n + 1)
                for i in range(T // P):
                    ins = M.matmul(ps[7][:, P * i:P * i + P], NR[:, i:i + 1].to_broadcast([P, P]), C("ident"),
                                   start=True, stop=True)
                ins.then_inc(factor_done, 1)

            def ffn(n, up, down, fbase):
                def up_body(i):
                    for j in range(NRAW):
                        if j % 2 == 0:
                            ge(pe, up_done, fbase + 2 * i + j // 2 - 1)
                        first = isinstance(i, int) and i == 0 and j == 0
                        unit(up, i, j, j, h_hi, h_lo, 0, KD, KD - 1, KD * n if first else None)
                        if first:
                            norm_sum(n)
                        if isinstance(i, int) and j == 1:
                            norm_factor(n)

                def down_body(i):
                    for j in range(NRAW):
                        if isinstance(i, int) and j < 2:
                            pe.wait_ge(hid_lo_done, fbase + KF // 2 * (j + 1))
                        if j % 2 == 0:
                            ge(pe, resid_done, RESID[n + 1] + 2 * i + j // 2 - 1)
                        unit(down, i, j, 4 + j // 2, hid_hi, hid_lo, KF // 2 * (j % 2), KF // 2, KF - 1)

                up_body(0)
                with pe.Fori(1, units(up)[1]) as i:
                    up_body(i)
                down_body(0)
                with pe.Fori(1, units(down)[1]) as i:
                    down_body(i)

            ffn(0, "up1", "down1", 0)

            def win_unit(i, j):
                ge(pe, proj, NRAW * i + j - 3)
                first = isinstance(i, int) and i == 0 and j == 0
                unit("win", i, j, j, h_hi, h_lo, 0, KD, KD - 1, KD if first else None)
                if first:
                    norm_sum(1)
                if isinstance(i, int) and (i, j) == (0, 1):
                    norm_factor(1)

            def win_body(i):
                for j in range(NRAW):
                    win_unit(i, j)

            def head_sums(src, bank):
                for i in range(T // P):
                    for p in range(NP):
                        c = NH * i + 2 * p
                        ins = M.matmul(ps[bank][:, c:c + 2], src[:, p, P * i:P * i + P], C("headones")[:, 0:P:CH],
                                       start=True, stop=True)
                ins.then_inc(ks_done, 1)

            def heads_first(bank):
                for i in range(T // P):
                    ins = M.transpose(ps[bank][0:NH, P * i:P * i + P], KR[:, NH * i:NH * i + NH], C("ident"))
                ins.then_inc(krt_done, 1)

            def spread_heads(bank, select, values, done):
                for p in range(NP):
                    M.matmul(ps[bank + p][:, :], arena[0:NH, select, P * p:P * p + P], arena[0:NH, values, :],
                             start=True, stop=True).then_inc(done, 1)

            win_body(0)
            win_body(1)
            pe.wait_ge(lora_w, 32)
            pe.wait_ge(lora_act, 1)
            for c in range(4):
                M.matmul(ps[4 + c][:, :], w2_t[:, c * P:c * P + P], WD, start=True, stop=True).then_inc(z_done, 1)
            win_unit(2, 0)
            for c in range(4):
                pe.wait_ge(z_kept, c + 1)
                M.matmul(ps[4 + c][:, :], a2_t[:, c * P:c * P + P], AD, start=True, stop=True).then_inc(z_done, 1)
            win_unit(2, 1)
            pe.wait_ge(kk_sq, 1)
            pe.wait_ge(z_kept, 5)
            head_sums(tiles(E0), 4)
            win_unit(2, 2)
            pe.wait_ge(kr_ready, 1)
            pe.wait_ge(z_kept, 8)
            heads_first(7)
            win_unit(2, 3)
            pe.wait_ge(krt_kept, 1)
            pe.wait_ge(select_in, 16)
            spread_heads(4, SELECT0, KRT0, z_done)
            win_unit(3, 0)
            win_unit(3, 1)
            def triangles(g):
                for n in (2 * g, 2 * g + 1):
                    for p in range(NP):
                        for e in range(2):
                            r, m = CH * e, (n % 2 * NP + p) * CH
                            ins = M.matmul(ps[4 + g][r:r + CH, m:m + CH], arena[r:r + CH, A0 + p, CH * n:CH * n + CH],
                                           arena[r:r + CH, KK0 + p, CH * n:CH * n + CH], start=True, stop=True)
                ins.then_inc(at_done, 1)

            pe.wait_ge(early_b, 1)
            pe.wait_ge(early_a, 1)
            triangles(0)
            triangles(1)
            win_unit(3, 2)
            triangles(2)
            triangles(3)
            win_unit(3, 3)
            win_body(4)
            pe.wait_ge(proj, QT + 2)
            for i in range(T // P):
                ins = M.transpose(ps[0][:, P * i:P * i + P], arena[:, AV, P * i:P * i + P], C("ident"))
            ins.then_inc(vt_done, 1)
            for i in range(1, T // P):
                ins = M.transpose(ps[1][0:CH, P * (i - 1):P * i], arena[:, AV, P * i - CH:P * i], C("ident"))
            ins.then_inc(vt_done, 1)

            pe.wait_ge(at_kept, 4)
            for c in range(4):
                pe.wait_ge(rk_ready, c + 1)
                M.matmul(ps[4 + c][:, :], C("headones"), arena[:, BON0 + c, :], start=True, stop=True).then_inc(z_done, 1)

            pe.wait_ge(proj, IN_TILES)
            pe.wait_ge(vt_kept, 2)
            for m, n in enumerate(CHUNKS):
                if m in (0, 2):
                    pe.wait_ge(ops_act, 2 if m == 0 else 4)
                    pe.wait_ge(ops_dve, 2 if m == 0 else 4)
                ge(pe, mm_kept, 2 * (m - 1))
                for p in range(NP):
                    for e in range(2):
                        r = CH * e
                        ins = M.matmul(ps[2 * (m % 2) + e][:, p * P:p * P + P], BK[r:r + CH, p, n, :],
                                       AR[r:r + CH, p, n, :], start=True, stop=True)
                ins.then_inc(mm_done, 1)
                if m < 4:
                    pe.wait_ge(z_kept, 9 + m)
                ge(pe, bt_kept, m - 3)
                for p in range(NP):
                    ins = M.transpose(ps[4 + m % 4][:, p * P:p * P + P], BK[:, p, n, :], C("ident"))
                ins.then_inc(bt_done, 1)

            pe.wait_ge(off_ready, 1)
            pe.wait_ge(inv_in, 16 * 4 * NB)

            def by_matrix(bank, g, lhs, rhs, done):
                for m in range(8 * g, 8 * g + 8):
                    for e in range(2):
                        r = CH * e
                        ins = M.matmul(ps[bank][r:r + CH, m % 8 * CH:m % 8 * CH + CH], lhs[r:r + CH, m, :], rhs[r:r + CH, m, :],
                                       start=True, stop=True)
                ins.then_inc(done, 1)

            def turn_v(n):
                ge(pe, v_kept, n - 1)
                for p in range(NP):
                    ins = M.transpose(ps[6 + n % 2][0:CH, p * P:p * P + P], arena[:, VT + p, CH * n:CH * n + CH], C("ident"))
                ins.then_inc(v_done, 1)

            for k in range(4 * NB):
                g = k % 4
                if k < 4:
                    pe.wait_ge(mm_kept, 2 * NC - 2 + k // 2 * 2)
                if k == 1:
                    pe.wait_ge(bt_kept, NC)
                if 6 <= k < 10:
                    pe.wait_ge(q_kept, k - 5)
                if k >= 10:
                    pe.wait_ge(tt_kept, k - 9)
                if k < 4:
                    by_matrix(k, g, OFF, DI, q_done)
                else:
                    pe.wait_ge(q_kept, g + 1)
                    if k >= 8:
                        pe.wait_ge(tt_kept, k - 7)
                    by_matrix(k % 6, g, QQ, DIT if k < 8 else TT, tt_done)
                if k % 2 and k < 4 * NB - 1:
                    turn_v(k // 2)

            def scores(m):
                i, r = m // 2, CH * (m % 2)
                k0 = CH if i == 0 else 0
                ge(pe, pt_act, m - 1)
                ge(pe, pt_dve, m - 3)
                ge(pe, s_kept, 2 * m)
                for b in range(2):
                    for p in (2 * b, 2 * b + 1):
                        c = p % 2 * 192
                        ins = M.matmul(ps[5 + b][:, c + k0:c + 192], arena[r:r + CH, QT + p, P * i:P * i + P],
                                       arena[r:r + CH, AK, P * i - CH + k0:P * i + P], start=True, stop=True)
                    ins.then_inc(s_done, 1)

            def transpose_own(m):
                pe.wait_ge(p_ready, m + 1)
                if m < NC - 1:
                    pe.wait_ge(s_kept, 2 * (m + 2))
                else:
                    pe.wait_ge(y_kept, NC)
                for p in range(NP):
                    ins = M.transpose(ps[PT_BANKS[m][0]][:, p * P:p * P + P], SC[:, NP * (m % 2) + p, CH:192], C("ident"))
                ins.then_inc(pt_done, 1)

            def transpose_before(m):
                if m >= 2:
                    for p in range(NP):
                        ins = M.transpose(ps[PT_BANKS[m][1]][0:CH, p * P:p * P + P], SC[:, NP * (m % 2) + p, 0:CH], C("ident"))
                    ins.then_inc(pt0_done, 1)

            def attend(m):
                i, e = m // 2, m % 2
                pe.wait_ge(pt_act, m + 1)
                ge(pe, pt_dve, m - 1)
                if m < NC - 1:
                    ge(pe, o_kept, m)
                for p in range(NP):
                    o = ps[O_BANKS[m]][CH * e:CH * e + CH, p * P:p * P + P]
                    ins = M.matmul(o, VA[:, i, CH * e:CH * e + CH], PT1[:, NP * e + p, :], start=True, stop=i == 0)
                    if i:
                        ins = M.matmul(o, VB[0:CH, i - 1, CH * e:CH * e + CH], PT0[0:CH, NP * e + p, :],
                                       start=False, stop=True)
                ins.then_inc(o_done, 1)

            def quadrants():
                return [(p, e, CH * e) for p in range(NP) for e in range(2)]

            def outputs(n):
                ge(pe, y_kept, n)
                for p, e, r in quadrants():
                    o = ps[4][r:r + CH, p * CH:p * CH + CH]
                    ins = M.matmul(o, UV[:, n, p, r:r + CH], MM[:, n, e, p, CH:P], start=True, stop=n == 0)
                    if n:
                        ins = M.matmul(o, ST[r:r + CH, n % 2, p, :], AR[r:r + CH, p, n, CH:P], start=False, stop=True)
                ins.then_inc(y_done, 1)

            def gate(c):
                M.matmul(ps[GATE_BANK[c]][:, :], g2_t[:, c * P:c * P + P], GD, start=True, stop=True).then_inc(g_done, 1)

            pe.wait_ge(g2_in, 16)
            pe.wait_ge(tt_kept, 8)
            gate(0)
            gate(1)
            pe.wait_ge(v_kept, NC - 1)
            pe.wait_ge(zeroed, 3)
            pe.wait_ge(roped, 5)
            pe.wait_ge(tt_kept, 12)
            for n in range(NC):
                ge(pe, r_kept, n)
                for p, e, r in quadrants():
                    ins = M.matmul(ps[0][r:r + CH, p * CH:p * CH + CH], MM[:, n, e, p, 0:CH], UV[:, n, p, r:r + CH],
                                   start=p == 0, stop=n == 0 and p == NP - 1)
                if n:
                    pe.wait_ge(st_kept, n)
                    for p, e, r in quadrants():
                        ins = M.matmul(ps[0][r:r + CH, p * CH:p * CH + CH], AR[r:r + CH, p, n, 0:CH], ST[r:r + CH, n % 2, p, :],
                                       start=False, stop=p == NP - 1)
                ins.then_inc(r_done, 1)
                if n >= 2:
                    transpose_own(n - 2)
                else:
                    if n:
                        pe.wait_ge(v_kept, NC)
                    gate(2 + n)
                pe.wait_ge(r_kept, n + 1)
                for p, e, r in quadrants():
                    ins = M.matmul(ps[1 + e][0:CH, p * CH:p * CH + CH], TT[r:r + CH, n * NP + p, :], RS[r:r + CH, p, :],
                                   start=True, stop=True)
                ins.then_inc(u_done, 1)
                if n >= 2:
                    transpose_before(n - 2)
                if n == 0:
                    turn_v(NC - 1)
                pe.wait_ge(u_dve, n + 1)
                pe.wait_ge(u_act, n + 1)
                if n < NC - 1:
                    for p, e, r in quadrants():
                        ins = M.matmul(ps[3][r:r + CH, p * CH:p * CH + CH], BT[:, n, p, r:r + CH], UV[:, n, p, r:r + CH],
                                       start=True, stop=True)
                    ins.then_inc(st_done, 1)
                else:
                    outputs(n)
                if n < 2:
                    pe.wait_ge(g_kept, 3 + n)
                scores(n)
                if n >= 2:
                    attend(n - 2)
                if n < NC - 1:
                    outputs(n)

            pe.wait_ge(y_kept, NC)
            for c in range(4):
                M.matmul(ps[c][:, :], C("headones"), arena[:, DI0 + c, :], start=True, stop=True).then_inc(gn_done, 1)
            transpose_own(NC - 2)
            transpose_before(NC - 2)
            transpose_own(NC - 1)
            pe.wait_ge(gn_kept, 1)
            transpose_before(NC - 1)
            attend(NC - 2)
            attend(NC - 1)

            def wout_unit(u):
                half = u // NRAW
                pe.wait_ge(lo_done, FIRST_UNIT["wout"] + u + 1)
                if u >= 2:
                    pe.wait_ge(resid_done, KD + 2 * (u - 1))
                for e in range(2):
                    for k in range(4):
                        ins = product(4 + 2 * (u % 2) + e, u, (4 * e + k) * P, mix_hi[:, 4 * half + k, :],
                                      mix_lo[:, 4 * half + k, :], k == 0, k == 3)
                ins.then_inc(w_used, 1)

            pe.wait_ge(gn_sq, 4)
            head_sums(GN_SQ, 1)
            pe.wait_ge(mix_lo_done, 2)
            wout_unit(0)
            pe.wait_ge(kr_ready, 2)
            heads_first(3)
            wout_unit(1)
            pe.wait_ge(krt_kept, 2)
            pe.wait_ge(select_in, 32)
            spread_heads(0, SELECT1, KRT1, gn_done)
            for u in range(2, NRAW):
                wout_unit(u)
            pe.wait_ge(mix_lo_done, 2 + 4)
            for u in range(NRAW, 2 * NRAW):
                wout_unit(u)
            ffn(2, "up2", "down2", KF)
            norm_sum(3)
            norm_factor(3)


def unit_layout(wt, nk):
    k, n = wt.shape
    return np.ascontiguousarray(
        wt.reshape(k // (nk * P), nk, P, n // P, P).transpose(3, 0, 2, 1, 4).reshape(-1, P, nk * P))


def columns(v):
    return v.reshape(-1, P).T


def kernel(**inputs):
    import concourse.bacc as _bacc
    from concourse.bass_utils import run_bass_kernel_spmd as _run

    g = {k: np.asarray(v) for k, v in inputs.items()}
    nq, nkv = NH * HD, 2 * HD
    r0 = nq + 2 * nkv
    w_in, w_out = g["w_in"], g["w_out"]
    heads = np.arange(NH).reshape(2, NP).T.ravel()
    q_cols = (heads[:, None] * HD + np.arange(HD)[None, :]).ravel()
    lo = r0 + 3 * nq
    rw = np.concatenate([np.arange(lo + 64, lo + 160), np.arange(lo, lo + 32), np.arange(lo + 32, lo + 64),
                         np.arange(lo + 64, lo + 160), np.arange(r0 + nq, r0 + 2 * nq), np.arange(r0, r0 + nq),
                         np.arange(r0 + 2 * nq, r0 + 3 * nq)])
    cols = np.concatenate([rw, np.arange(nq, nq + nkv), np.arange(nq + nkv, r0), q_cols])
    rows = np.concatenate([q_cols, np.arange(nq, 2 * nq)])

    def up_units(a, b):
        return np.ascontiguousarray(np.stack([unit_layout(a, KD), unit_layout(b, KD)], 1).reshape(2 * KF, P, UP_UNIT))

    parts = {"g1": g["ffn1_norm"], "gm": g["mix_norm"], "g2": g["ffn2_norm"], "gf": g["final_norm"],
             "mu": g["rwkv_shift_mu"][rw - r0], "w0": g["rwkv_w0"], "a0": g["rwkv_a0"], "k_k": g["rwkv_k_k"],
             "k_a": g["rwkv_k_a"], "r_k": g["rwkv_r_k"].reshape(-1), "ln_w": g["rwkv_ln_w"], "ln_b": g["rwkv_ln_b"]}
    arrays = {
        "xT": np.ascontiguousarray(g["x"].reshape(T, KD, P).transpose(2, 1, 0)),
        "up1": up_units(g["ffn1_w_gate"], g["ffn1_w_up"]), "down1": unit_layout(g["ffn1_w_down"], KF // 2),
        "win": unit_layout(w_in[:, cols], KD), "wout": np.concatenate([unit_layout(w_out[rows[h:h + nq]], KD // 2).reshape(KD // 2, 2, P, UP_UNIT // 2)
                                .transpose(0, 2, 1, 3).reshape(KD // 2, P, UP_UNIT) for h in (0, nq)]),
        "up2": up_units(g["ffn2_w_gate"], g["ffn2_w_up"]), "down2": unit_layout(g["ffn2_w_down"], KF // 2),
        "params": np.ascontiguousarray(np.concatenate([columns(parts[n]) for n in PARAMS], 1)),
        "sinks": g["attn_sinks"], "w2": g["rwkv_w2"], "a2": g["rwkv_a2"], "g2": g["rwkv_g2"], "const": constants(),
        "selection": head_selection(),
    }
    nc = _bacc.Bacc("TRN2", target_bir_lowering=False, num_devices=1)
    d = {n: nc.dram_tensor(n, a.shape, F32, kind="ExternalInput").ap() for n, a in arrays.items()}
    out = nc.dram_tensor("out", (P, KD, T), F32, kind="ExternalOutput").ap()
    scratch = [nc.dram_tensor(n, (P, 2, BLK, BLK), F32, kind="Internal").ap() for n in ("blocks", "inverses", "inverses_t")]
    build(nc, d["xT"], {n: d[n] for n, _, _ in PHASES}, d["params"], d["sinks"], d["w2"], d["a2"], d["g2"], d["const"],
          d["selection"], *scratch, out)
    r = _run(nc, [arrays], core_ids=[0])
    return r.results[0]["out"].transpose(2, 1, 0).reshape(1, T, D)
```
